# Optimizing a Trainium2 kernel written in Bass

```python
import jax
import jax.numpy as jnp
from jax import lax
import numpy as np

D_MODEL = 1024
BATCH = 1
SEQ = 512
DEPTH = 2
DEC_BATCH = 8
DEC_SEQ = 8
PAST_LEN = 2048
PAGE_SIZE = 128

MIX = D_MODEL
N_MIXERS = 4
GROUP_W = MIX // N_MIXERS
HEAD_DIM = 64
HEADS = GROUP_W // HEAD_DIM
CHUNK = 128
ROPE_BASE = 10000.0
FORGET_BIAS = 3.0
MOE_GROUPS = 4
EXPERTS_PER_GROUP = 4
N_EXPERTS = MOE_GROUPS * EXPERTS_PER_GROUP
TOP_K_IN_GROUP = 2
D_EXPERT = D_MODEL // 4
ALPHA = (2 * DEPTH) ** 0.25
BETA = (8 * DEPTH) ** -0.25
LN_EPS = 1e-5
RMS_EPS = 1e-6
COL_NAMES = ('a_u', 'a_v', 'b_q', 'b_k', 'b_v', 'b_g', 'c_q', 'c_k', 'c_v', 'c_o', 'c_i', 'c_f', 'd_q', 'd_k', 'd_v', 'd_f')
COL_WIDTHS = (GROUP_W,) * 10 + (HEADS, HEADS) + (GROUP_W,) * 3 + (HEADS,)
D_IN = sum(COL_WIDTHS)
VALUE_COLS = ('b_v', 'c_v', 'd_v')

kernel_name = 'hymba_style_hybrid_decoder_step'

def col_offset(name):
    off = 0
    for n, w in zip(COL_NAMES, COL_WIDTHS):
        if n == name:
            return off
        off += w
    raise KeyError(name)

def split_cols(z):
    out, off = {}, 0
    for n, w in zip(COL_NAMES, COL_WIDTHS):
        out[n] = z[..., off:off + w]
        off += w
    return out

def layer_norm(x, g, b):
    xf = x.astype(jnp.float32)
    mu = jnp.mean(xf, -1, keepdims=True)
    var = jnp.mean(jnp.square(xf - mu), -1, keepdims=True)
    y = (xf - mu) * lax.rsqrt(var + LN_EPS) * g.astype(jnp.float32) + b.astype(jnp.float32)
    return y.astype(x.dtype)

def head_norm(y):
    mu = jnp.mean(y, -1, keepdims=True)
    var = jnp.mean(jnp.square(y - mu), -1, keepdims=True)
    return (y - mu) * lax.rsqrt(var + LN_EPS)

def head_rms(y):
    return y * lax.rsqrt(jnp.mean(jnp.square(y), -1, keepdims=True) + RMS_EPS)

def rope(x, pos):
    half = HEAD_DIM // 2
    inv = ROPE_BASE ** (-jnp.arange(half, dtype=jnp.float32) / half)
    ang = pos.astype(jnp.float32)[:, None] * inv[None, :]
    cos = jnp.cos(ang)[None, :, None, :]
    sin = jnp.sin(ang)[None, :, None, :]
    x1, x2 = x[..., :half], x[..., half:]
    return jnp.concatenate([x1 * cos - x2 * sin, x1 * sin + x2 * cos], -1)

def to_chunks(a, L):
    bn, t = a.shape[:2]
    a = a.reshape((bn, t // L, L) + a.shape[2:])
    return jnp.swapaxes(jnp.moveaxis(a, 1, 0), 2, 3)

def from_chunks(a):
    nc, bn, h, L, d = a.shape
    return a.transpose(1, 0, 3, 2, 4).reshape(bn, nc * L, h, d)

def chunk_mlp(u, v, w_s, b_s):
    bn, t = v.shape[:2]
    L = min(CHUNK, t)
    w = jnp.where(jnp.tril(jnp.ones((L, L), dtype=bool)), w_s[:, :L, :L], 0.0)
    vc = v.reshape(bn, t // L, L, HEADS, HEAD_DIM)
    s = jnp.einsum('hts,bcshd->bcthd', w, vc) + b_s[:, :L].T[None, None, :, :, None]
    return u * s.reshape(bn, t, HEADS, HEAD_DIM)

def retention(q, k, v, r0):
    bn, t = q.shape[:2]
    L = min(CHUNK, t)
    log_g = jnp.log1p(-jnp.exp2(-5.0 - jnp.arange(HEADS, dtype=jnp.float32)))
    idx = jnp.arange(L, dtype=jnp.float32)
    diff = idx[:, None] - idx[None, :]
    decay = jnp.where(diff >= 0, jnp.exp(log_g[:, None, None] * jnp.maximum(diff, 0.0)), 0.0)
    q_dec = jnp.exp(log_g[:, None] * (idx + 1.0))[None, :, :, None]
    k_dec = jnp.exp(log_g[:, None] * (L - 1.0 - idx))[None, :, :, None]
    c_dec = jnp.exp(log_g * L)[None, :, None, None]

    def step(r, inp):
        qc, kc, vc = inp
        s = jnp.einsum('bhld,bhmd->bhlm', qc, kc) * decay
        o = jnp.einsum('bhlm,bhmd->bhld', s, vc) + jnp.einsum('bhld,bhde->bhle', qc, r) * q_dec
        r = c_dec * r + jnp.einsum('bhld,bhle->bhde', kc * k_dec, vc)
        return r, o

    r, o = lax.scan(step, r0, (to_chunks(q, L), to_chunks(k, L), to_chunks(v, L)))
    return from_chunks(o), r

def mlstm(q, k, v, i_pre, f_pre, c0, n0, m0):
    bn, t = q.shape[:2]
    L = min(CHUNK, t)
    causal = jnp.tril(jnp.ones((L, L), dtype=bool))

    def step(carry, inp):
        c, n, m = carry
        qc, kc, vc, ic, lfc = inp
        b = jnp.cumsum(lfc, -1)
        a = b + m[..., None]
        dmat = jnp.where(causal, b[..., :, None] - b[..., None, :] + ic[..., None, :], -jnp.inf)
        m_t = jnp.maximum(a, jnp.max(dmat, -1))
        w_in = jnp.exp(dmat - m_t[..., None])
        w_st = jnp.exp(a - m_t)
        s = jnp.einsum('bhld,bhmd->bhlm', qc, kc) * w_in
        num = jnp.einsum('bhlm,bhmd->bhld', s, vc) + w_st[..., None] * jnp.einsum('bhld,bhde->bhle', qc, c)
        den = jnp.sum(s, -1) + w_st * jnp.einsum('bhld,bhd->bhl', qc, n)
        h = num / jnp.maximum(jnp.abs(den), jnp.exp(-m_t))[..., None]
        m_new = m_t[..., -1]
        g_st = jnp.exp(b[..., -1] + m - m_new)
        g_in = jnp.exp(b[..., -1:] - b + ic - m_new[..., None])
        c = g_st[..., None, None] * c + jnp.einsum('bhld,bhle->bhde', kc * g_in[..., None], vc)
        n = g_st[..., None] * n + jnp.einsum('bhl,bhld->bhd', g_in, kc)
        return (c, n, m_new), h

    xs = (to_chunks(q, L), to_chunks(k, L), to_chunks(v, L), to_chunks(i_pre, L),
          to_chunks(jax.nn.log_sigmoid(f_pre), L))
    (c, n, m), h = lax.scan(step, (c0, n0, m0), xs)
    return from_chunks(h), c, n, m

def fox_prompt(q, k, v, logf):
    bn, t = q.shape[:2]
    L = min(CHUNK, t)
    nb = t // L
    scale = HEAD_DIM ** -0.5
    cum = jnp.cumsum(logf, axis=1).transpose(0, 2, 1)
    kpos = jnp.arange(t)

    def block(args):
        qb, cq, start = args
        logits = jnp.einsum('bqhd,bkhd->bhqk', qb, k) * scale + cq[..., :, None] - cum[:, :, None, :]
        qpos = start + jnp.arange(L)
        logits = jnp.where(kpos[None, :] <= qpos[:, None], logits, -jnp.inf)
        return jnp.einsum('bhqk,bkhd->bqhd', jax.nn.softmax(logits, -1), v)

    qbs = jnp.moveaxis(q.reshape(bn, nb, L, HEADS, HEAD_DIM), 1, 0)
    cqs = jnp.moveaxis(cum.reshape(bn, HEADS, nb, L), 2, 0)
    out = lax.map(block, (qbs, cqs, jnp.arange(nb) * L))
    return jnp.moveaxis(out, 0, 1).reshape(bn, t, HEADS, HEAD_DIM)

def fox_sample(q, k, v, logf, k_past, v_past, lf_past):
    f32 = jnp.float32
    t = q.shape[1]
    scale = HEAD_DIM ** -0.5
    k_past, v_past, lf_past = k_past.astype(f32), v_past.astype(f32), lf_past.astype(f32)
    suffix = (lax.cumsum(lf_past, axis=1, reverse=True) - lf_past).transpose(0, 2, 1)
    cn = jnp.cumsum(logf, axis=1).transpose(0, 2, 1)
    lp = jnp.einsum('bqhd,bkhd->bhqk', q, k_past) * scale + cn[..., :, None] + suffix[..., None, :]
    ln = jnp.einsum('bqhd,bkhd->bhqk', q, k) * scale + cn[..., :, None] - cn[..., None, :]
    ln = jnp.where(jnp.tril(jnp.ones((t, t), dtype=bool)), ln, -jnp.inf)
    p = jax.nn.softmax(jnp.concatenate([lp, ln], -1), -1)
    n_past = k_past.shape[1]
    return (jnp.einsum('bhqk,bkhd->bqhd', p[..., :n_past], v_past)
            + jnp.einsum('bhqk,bkhd->bqhd', p[..., n_past:], v))

def gather_pages(pool, page_table):
    g = pool[page_table]
    return g.reshape((page_table.shape[0], page_table.shape[1] * PAGE_SIZE) + pool.shape[2:])

def hier_moe(x, w_rg, b_rg, w_re, b_re, w1, w3, w2):
    f32 = jnp.float32
    xf = x.astype(f32)
    g_logits = xf @ w_rg.astype(f32) + b_rg.astype(f32)
    g_idx = jnp.argmax(g_logits, -1)
    g_w = jnp.max(jax.nn.softmax(g_logits, -1), -1, keepdims=True)
    e_all = jnp.einsum('btd,gde->btge', xf, w_re.astype(f32)) + b_re.astype(f32)
    e_logits = jnp.einsum('btge,btg->bte', e_all, jax.nn.one_hot(g_idx, MOE_GROUPS, dtype=f32))
    top_v, top_i = lax.top_k(e_logits, TOP_K_IN_GROUP)
    w_pair = g_w * jax.nn.softmax(top_v, -1)
    eid = g_idx[..., None] * EXPERTS_PER_GROUP + top_i
    gates = jnp.sum(jax.nn.one_hot(eid, N_EXPERTS, dtype=f32) * w_pair[..., None], -2)
    h = jax.nn.silu(jnp.einsum('btd,edf->btef', x, w1)) * jnp.einsum('btd,edf->btef', x, w3)
    return jnp.einsum('btef,efd->btd', h * gates[..., None].astype(x.dtype), w2)

def mixing_block(x, pos, w_in, b_in, w_s, b_s, g_mix, w_out, r0, c0, n0, m0, past):
    f32 = jnp.float32
    bn, t = x.shape[:2]
    z = split_cols((x @ w_in + b_in).astype(f32))
    hd = lambda a: a.reshape(bn, t, HEADS, HEAD_DIM)
    scale = HEAD_DIM ** -0.5
    u_a = jax.nn.gelu(hd(z['a_u']))
    v_a = head_norm(jax.nn.gelu(hd(z['a_v'])))
    y_a = chunk_mlp(u_a, v_a, w_s.astype(f32), b_s.astype(f32))
    y_b, r_new = retention(rope(hd(z['b_q']), pos), rope(hd(z['b_k']), pos) * scale, hd(z['b_v']), r0.astype(f32))
    y_c, c_new, n_new, m_new = mlstm(hd(z['c_q']), hd(z['c_k']) * scale, hd(z['c_v']), z['c_i'], z['c_f'],
                                     c0.astype(f32), n0.astype(f32), m0.astype(f32))
    y_c = jax.nn.sigmoid(hd(z['c_o'])) * y_c
    q_d, k_d, v_d = hd(z['d_q']), hd(z['d_k']), hd(z['d_v'])
    logf = jax.nn.log_sigmoid(z['d_f'])
    if past is None:
        y_d = fox_prompt(q_d, k_d, v_d, logf)
    else:
        y_d = fox_sample(q_d, k_d, v_d, logf, past[0], past[1], past[2])
    merged = jnp.concatenate([head_rms(y_a), head_rms(y_b) * jax.nn.silu(hd(z['b_g'])),
                              head_rms(y_c), head_rms(y_d)], axis=2)
    merged = merged.reshape(bn, t, MIX) * g_mix.astype(f32)
    out = merged.astype(x.dtype) @ w_out
    return out, (v_a, r_new, c_new, n_new, m_new, k_d, v_d, logf)

def stack_layers(states, i, dtype):
    return jnp.stack([s[i] for s in states]).astype(dtype)

def setup_inputs(seed: int = 0) -> dict:
    key = jax.random.key(seed)
    ks = jax.random.split(key, 32)
    f32 = jnp.float32
    nrm = lambda k, shape, s: s * jax.random.normal(k, shape, f32)
    n_pages = PAST_LEN // PAGE_SIZE
    n_used = DEC_BATCH * n_pages
    n_pool = (5 * n_used) // 4
    col_scale = jnp.concatenate([jnp.full((w,), BETA if n in VALUE_COLS else 1.0, f32)
                                 for n, w in zip(COL_NAMES, COL_WIDTHS)])
    b_in = nrm(ks[11], (DEPTH, D_IN), 0.02)
    for n in ('c_f', 'd_f'):
        o = col_offset(n)
        b_in = b_in.at[:, o:o + HEADS].add(FORGET_BIAS)
    cache_logf = -jax.random.uniform(ks[4], (DEPTH, n_pool, PAGE_SIZE, HEADS), f32, 0.0, 2.0 / PAST_LEN)
    return {
        'x_prompt': nrm(ks[0], (BATCH, SEQ, D_MODEL), 1.0),
        'x_sample': nrm(ks[1], (DEC_BATCH, DEC_SEQ, D_MODEL), 1.0),
        'cache_k': nrm(ks[2], (DEPTH, n_pool, PAGE_SIZE, HEADS, HEAD_DIM), 1.0),
        'cache_v': nrm(ks[3], (DEPTH, n_pool, PAGE_SIZE, HEADS, HEAD_DIM), 1.0),
        'cache_logf': cache_logf,
        'page_table': jax.random.permutation(ks[5], n_pool)[:n_used].reshape(DEC_BATCH, n_pages).astype(jnp.int32),
        'state_ret': nrm(ks[6], (DEPTH, DEC_BATCH, HEADS, HEAD_DIM, HEAD_DIM), 1.0),
        'state_mlstm_c': nrm(ks[7], (DEPTH, DEC_BATCH, HEADS, HEAD_DIM, HEAD_DIM), 1.0),
        'state_mlstm_n': nrm(ks[8], (DEPTH, DEC_BATCH, HEADS, HEAD_DIM), 1.0),
        'state_mlstm_m': nrm(ks[9], (DEPTH, DEC_BATCH, HEADS), 1.0),
        'w_in': nrm(ks[10], (DEPTH, D_MODEL, D_IN), D_MODEL ** -0.5) * col_scale,
        'b_in': b_in,
        'w_s': nrm(ks[12], (DEPTH, HEADS, CHUNK, CHUNK), CHUNK ** -0.5),
        'b_s': 1.0 + nrm(ks[13], (DEPTH, HEADS, CHUNK), 0.02),
        'g_mix': 1.0 + nrm(ks[14], (DEPTH, MIX), 0.02),
        'w_out': nrm(ks[15], (DEPTH, MIX, D_MODEL), BETA * MIX ** -0.5),
        'ln1_g': 1.0 + nrm(ks[16], (DEPTH, D_MODEL), 0.02),
        'ln1_b': nrm(ks[17], (DEPTH, D_MODEL), 0.02),
        'w_rg': nrm(ks[18], (DEPTH, D_MODEL, MOE_GROUPS), D_MODEL ** -0.5),
        'b_rg': nrm(ks[19], (DEPTH, MOE_GROUPS), 0.01),
        'w_re': nrm(ks[20], (DEPTH, MOE_GROUPS, D_MODEL, EXPERTS_PER_GROUP), D_MODEL ** -0.5),
        'b_re': nrm(ks[21], (DEPTH, MOE_GROUPS, EXPERTS_PER_GROUP), 0.01),
        'w1': nrm(ks[22], (DEPTH, N_EXPERTS, D_MODEL, D_EXPERT), D_MODEL ** -0.5),
        'w3': nrm(ks[23], (DEPTH, N_EXPERTS, D_MODEL, D_EXPERT), D_MODEL ** -0.5),
        'w2': nrm(ks[24], (DEPTH, N_EXPERTS, D_EXPERT, D_MODEL), BETA * D_EXPERT ** -0.5),
        'ln2_g': 1.0 + nrm(ks[25], (DEPTH, D_MODEL), 0.02),
        'ln2_b': nrm(ks[26], (DEPTH, D_MODEL), 0.02),
    }

def reference(x_prompt, x_sample, cache_k, cache_v, cache_logf, page_table,
              state_ret, state_mlstm_c, state_mlstm_n, state_mlstm_m,
              w_in, b_in, w_s, b_s, g_mix, w_out, ln1_g, ln1_b,
              w_rg, b_rg, w_re, b_re, w1, w3, w2, ln2_g, ln2_b):
    f32 = jnp.float32
    dt = x_prompt.dtype
    bp, tp = x_prompt.shape[:2]
    ts = x_sample.shape[1]
    past_len = page_table.shape[1] * PAGE_SIZE
    pos_p = jnp.arange(tp, dtype=jnp.int32)
    pos_s = past_len + jnp.arange(ts, dtype=jnp.int32)
    hp, hs = x_prompt, x_sample
    st_p, st_s = [], []
    for l in range(DEPTH):
        mix_w = (w_in[l], b_in[l], w_s[l], b_s[l], g_mix[l], w_out[l])
        moe_w = (w_rg[l], b_rg[l], w_re[l], b_re[l], w1[l], w3[l], w2[l])
        zc = jnp.zeros((bp, HEADS, HEAD_DIM, HEAD_DIM), f32)
        mix, st = mixing_block(hp, pos_p, *mix_w, zc, zc, jnp.zeros((bp, HEADS, HEAD_DIM), f32),
                               jnp.zeros((bp, HEADS), f32), None)
        hp = layer_norm(ALPHA * hp + mix, ln1_g[l], ln1_b[l])
        hp = layer_norm(ALPHA * hp + hier_moe(hp, *moe_w), ln2_g[l], ln2_b[l])
        st_p.append(st)
        past = (gather_pages(cache_k[l], page_table), gather_pages(cache_v[l], page_table),
                gather_pages(cache_logf[l], page_table))
        mix, st = mixing_block(hs, pos_s, *mix_w, state_ret[l], state_mlstm_c[l], state_mlstm_n[l],
                               state_mlstm_m[l], past)
        hs = layer_norm(ALPHA * hs + mix, ln1_g[l], ln1_b[l])
        hs = layer_norm(ALPHA * hs + hier_moe(hs, *moe_w), ln2_g[l], ln2_b[l])
        st_s.append(st)
    return (hp, hs,
            stack_layers(st_p, 5, dt), stack_layers(st_p, 6, dt), stack_layers(st_p, 7, dt),
            stack_layers(st_p, 1, dt), stack_layers(st_p, 2, dt), stack_layers(st_p, 3, dt), stack_layers(st_p, 4, dt),
            stack_layers(st_s, 5, dt), stack_layers(st_s, 6, dt), stack_layers(st_s, 7, dt),
            stack_layers(st_s, 1, dt), stack_layers(st_s, 2, dt), stack_layers(st_s, 3, dt), stack_layers(st_s, 4, dt),
            stack_layers(st_s, 0, dt))


_drawn_inputs = setup_inputs


def setup_inputs(seed=0):
    import zlib

    import numpy as np

    out = dict(_drawn_inputs(seed))
    spreads = {}
    factors = {'cache_logf': 31.529, 'b_s': 64.0, 'g_mix': 3.18, 'b_rg': 6.231, 'b_re': 23.968}
    for name, (base, spread) in spreads.items():
        noise = np.random.default_rng([zlib.crc32(name.encode()), seed]).standard_normal(out[name].shape)
        drawn = base * np.exp(spread * noise) if base else spread * noise
        out[name] = jnp.asarray(drawn.astype(out[name].dtype))
    for name, factor in factors.items():
        out[name] = (out[name] * factor).astype(out[name].dtype)
    return out
```

```python
import numpy as np
from contextlib import ExitStack

import concourse.bass as bass
from concourse import mybir
from concourse.alu_op_type import AluOpType as ALU

F32 = mybir.dt.float32
U32 = mybir.dt.uint32
I32 = mybir.dt.int32
ACT = mybir.ActivationFunctionType
AX = mybir.AxisListType

P = 128
D_MODEL = 1024
SEQ = 512
DEPTH = 2
DEC_BATCH = 8
DEC_SEQ = 8
PAST_LEN = 2048
PAGE_SIZE = 128
N_PAGES = PAST_LEN // PAGE_SIZE
N_POOL = (5 * DEC_BATCH * N_PAGES) // 4
HEADS = 4
HD = 64
GW = HEADS * HD
PAIRS = HEADS // 2
EXPERTS = 16
GROUPS = 4
D_EXPERT = D_MODEL // 4
ALPHA = (2 * DEPTH) ** 0.25
LN_EPS = 1e-5
RMS_EPS = 1e-6
SCALE = HD ** -0.5
KD = D_MODEL // P
NT = SEQ // P + 1
NP = NT - 1
NS = DEC_BATCH * DEC_SEQ
TOK = SEQ + NS
TOP_K = 2
BLOCK = P
MORE = TOP_K * TOK // (BLOCK + 1)
MORE_PER_EXPERT = -(-TOK // BLOCK) - 1
N_BLOCKS = EXPERTS + MORE
assert MORE % 2 == 0
KPP = PAST_LEN // P
RPP = PAGE_SIZE // KPP
BP = DEC_BATCH // 2
NEG = -1e30
RESET = -3e38

COLS, _at = {}, 0
for _name, _w in (("a_u", GW), ("a_v", GW), ("b_q", GW), ("b_k", GW), ("b_v", GW), ("b_g", GW),
                  ("c_q", GW), ("c_k", GW), ("c_v", GW), ("c_o", GW), ("c_i", HEADS), ("c_f", HEADS),
                  ("d_q", GW), ("d_k", GW), ("d_v", GW), ("d_f", HEADS)):
    COLS[_name] = _at
    _at += _w
D_IN = _at
SLAB = 512
N_SLABS = -(-D_IN // SLAB)
MERGED = ("a_u", "b_q", "c_q", "d_q")

def make_tables():
    f = np.float32
    parts = []
    i = np.arange(P)
    s, t = i[:, None], i[None, :]
    log_g = np.log1p(-np.exp2(-5.0 - np.arange(HEADS)))
    j = np.arange(NS)
    block, step = j // DEC_SEQ, j % DEC_SEQ
    same = block[:, None] == block[None, :]
    up_s = same & (j[:, None] <= j[None, :])

    def put(name, a):
        a = np.asarray(a, np.float64)
        a = a.reshape(a.shape[0], -1)
        full = np.zeros((P, a.shape[1]), f)
        full[:a.shape[0]] = a.astype(f)
        parts.append((name, full))

    put("ident", np.eye(P))
    put("ones", np.ones((P, P)))
    put("upper", s <= t)
    put("after", s > t)
    put("neg_t", np.where(s <= t, 0.0, NEG))
    put("neg_q", np.where(t <= s, 0.0, NEG))
    put("last", np.repeat((i == P - 1)[:, None], P, 1))
    dec = np.where(s <= t, np.exp(log_g[:, None, None] * np.maximum(t - s, 0)), 0.0)
    by_parity = [2 * pair + par for par in range(2) for pair in range(PAIRS)]
    put("dec", dec[by_parity].transpose(1, 0, 2))
    reset = np.zeros((P, HEADS, P))
    reset[:, :, 0] = RESET
    put("reset", reset)
    put("upper_s", up_s)
    put("lower_s", up_s.T)
    put("neg_ts", np.where(up_s, 0.0, NEG))
    put("last_s", (j[:, None] == 8 * block[None, :] + DEC_SEQ - 1))
    dec_s = np.where(up_s, np.exp(log_g[:, None, None] * np.maximum(j[None, :] - j[:, None], 0)), 0.0)
    put("dec_s", dec_s[by_parity].transpose(1, 0, 2))
    reset = np.zeros((NS, HEADS, NS))
    reset[:, :, ::DEC_SEQ] = RESET
    put("reset_s", reset)
    half = np.repeat(np.arange(2), HD)
    put("last_of", (j[:, None, None] == DEC_SEQ * (2 * np.arange(BP)[:, None] + half) + DEC_SEQ - 1))
    put("seq_of", (2 * np.arange(BP)[:, None] + half[:, None, None] == block))
    put("in_seq", block[:, None] == np.arange(DEC_BATCH))
    n_half = HD // 2
    inv = f(10000.0) ** (-np.arange(n_half, dtype=f) / f(n_half))
    pos = np.zeros((P, NT), f)
    pos[:, :NP] = i[:, None] + P * np.arange(NP)
    pos[:NS, NP] = PAST_LEN + step
    ang = (pos[:, :, None] * inv.astype(f)).astype(f).astype(np.float64)
    put("cos", np.cos(ang))
    put("sin", np.sin(ang))
    put("q_dec", np.exp(log_g[by_parity] * (i[:, None] + 1.0)))
    put("q_dec_s", np.exp(log_g * (step[:, None] + 1.0)))
    put("k_dec", np.exp(log_g * (P - 1.0 - i[:, None])) * SCALE)
    put("k_dec_s", np.exp(log_g * (DEC_SEQ - 1.0 - step[:, None])) * SCALE)
    put("c_dec", np.exp(log_g.reshape(PAIRS, 2).T * P)[half])
    put("c_dec_s", np.tile(np.exp(log_g * DEC_SEQ), (P, 1)))
    put("start", np.where(i[:, None] == 0, 0.0, NEG))
    put("start_s", np.where(step[:, None] == 0, 0.0, NEG))
    put("sub_row", (i % RPP)[:, None])
    put("ln_eps", np.full((P, 1), LN_EPS))
    put("rms_eps", np.full((P, 1), RMS_EPS))
    put("rank", np.tile(np.arange(GROUPS, 0, -1), (P, 1)))
    put("before", s < t)
    e = np.arange(EXPERTS)
    put("first_row", np.tile(e * BLOCK, (P, 1)))
    put("more_row", np.tile(EXPERTS * BLOCK - BLOCK - e * BLOCK, (P, 1)))
    put("count", np.tile(np.arange(MORE), (P, 1)))
    put("experts", np.tile(e, (P, 1)))
    at, cols = 0, {}
    for name, a in parts:
        cols[name] = (at, a.shape[1])
        at += a.shape[1]
    return cols, np.concatenate([a for _, a in parts], 1)

TABLE_COLS, TABLES = make_tables()

class Due:

    def __init__(self):
        self.n = {}

    def __call__(self, sem, k=1):
        self.n[sem.name] = self.n.get(sem.name, 0) + k
        return self.n[sem.name]

def b3(ap, n):
    return ap.unsqueeze(2).to_broadcast([ap.shape[0], ap.shape[1], n])

def rep(ap, n):
    return ap.unsqueeze(1).to_broadcast([ap.shape[0], n, ap.shape[1]])

def decoder(nc, d):
    ctx = ExitStack()
    with ctx:
        def sb(name, shape, dt=F32):
            return ctx.enter_context(nc.sbuf_tensor(name, shape, dt))

        signals = []

        def sig(name):
            s = ctx.enter_context(nc.semaphore(name))
            signals.append(s)
            return s

        tab = sb("tab", [P, TABLES.shape[1]])

        def T(name, n=P):
            at, w = TABLE_COLS[name]
            return tab[0:n, at:at + w]

        x = sb("x", [P, NT, D_MODEL])
        xT = sb("xT", [P, KD * TOK])
        z = sb("z", [P, NT * D_IN])
        ring = sb("ring", [P, 3, KD * SLAB])
        kbuf = sb("kbuf", [P, KPP * GW])
        vbuf = sb("vbuf", [P, KPP * GW])
        wsT = sb("wsT", [P, HEADS, P])
        wsTs = sb("wsTs", [NS, HEADS, NS])
        ws8 = sb("ws8", [NS, HEADS, DEC_SEQ])
        bs = sb("bs", [P, HEADS])
        bss = sb("bss", [NS, HEADS])
        gmix = sb("gmix", [P, KD])
        ret = sb("ret", [P, PAIRS, HD])
        mem = sb("mem", [P, PAIRS, HD + 1])
        small = sb("small", [P, 600])
        idx_f = sb("idx_f", [P, DEC_BATCH])
        idx_u = sb("idx_u", [P, DEC_BATCH], U32)
        pages = sb("pages", [P, DEC_BATCH], I32)

        rows_u = sb("rows_u", [P, NT, TOP_K], U32)
        plan = sb("plan", [1, N_BLOCKS + 1], I32)
        zero = sb("zero", [P, P])
        xd = nc.dram_tensor("expert_in", (N_BLOCKS * BLOCK, D_MODEL), F32, kind="Internal").ap()
        yd = nc.dram_tensor("expert_out", (N_BLOCKS * BLOCK, D_MODEL), F32, kind="Internal").ap()

        ps = ctx.enter_context(nc.psum_tensor("ps", [P, 8, SLAB], F32))

        zt = z[:, :].rearrange("p (t c) -> p t c", t=NT)
        xTv = xT[:, :].rearrange("p (k n) -> p k n", k=KD)

        def Z(t, name, n=P, w=GW):
            c = COLS[name]
            return zt[0:n, t, c:c + w]

        def Zall(name, w=GW):
            c = COLS[name]
            return zt[:, :, c:c + w]

        cut = [0]

        def stat(w):
            cut[0] += w
            assert cut[0] <= 600, cut[0]
            return small[:, cut[0] - w:cut[0]]

        def carve(tensor, start, *dims):
            n = int(np.prod(dims))
            v = tensor[:, start:start + n]
            if len(dims) == 2:
                v = v.rearrange("p (a b) -> p a b", b=dims[1])
            if len(dims) == 3:
                v = v.rearrange("p (a b c) -> p a b c", b=dims[1], c=dims[2])
            return v

        r2 = ring[:, 2, :]
        ws_nat = carve(r2, 0, HEADS, P)
        qkT = carve(r2, 512, 4, P)
        sw = carve(r2, 1024, HEADS, P)
        wexp = carve(r2, 1536, HEADS, P)
        mrow = carve(r2, 2048, HEADS, P)
        diag = carve(r2, 2560, HEADS, P)
        kd = carve(r2, 3072, GW)
        vx = carve(r2, 3328, HEADS, HD + 1)
        mix = carve(r2, 3588, HEADS, HD + 1)
        mrow_flat = mrow.rearrange("p a b -> p (a b)")
        ws_exp = carve(r2, 1024, HEADS, NS)
        tmp_a = carve(xT, 0, NT, GW)
        tmp_b = carve(xT, 1280, NT, GW)
        tmp_c = carve(xT, 2560, NT, GW)
        rs = carve(xT, 0, BP, HEADS, HD)
        cs = carve(xT, 1024, BP, HEADS, HD + 1)
        qm = carve(xT, 2064, BP, HEADS, NS)
        km = carve(xT, 3088, DEC_BATCH, HD)
        qd2 = carve(xT, 3600, HEADS, 2 * HD)
        qTa = carve(xT, 0, PAIRS, SEQ)
        kTa = carve(xT, 1024, PAIRS, SEQ)
        ncr = carve(xT, 2048, HEADS, SEQ)
        pT = [carve(xT, 4096, 4, P), carve(r2, 0, 4, P)]
        lg = [carve(r2, 512, SEQ), carve(r2, 1024, SEQ)]
        dg = [carve(r2, 1536, 4, P), carve(r2, 2048, 4, P)]
        NK = KPP + 1
        xs = [carve(r2, 0, NK, 32), carve(r2, 544, NK, 32)]
        pp = [carve(r2, 1088, NK, 32), carve(r2, 1632, NK, 32)]
        kTs = [carve(r2, 2176, 4, P), carve(r2, 2688, 4, P)]
        qbd = carve(r2, 3200, PAIRS, DEC_BATCH, 16)
        newb = carve(r2, 3456, DEC_BATCH, HEADS, DEC_SEQ)
        yT = carve(r2, 3712, PAIRS, NS)
        kTn = carve(r2, 3840, PAIRS, NS)
        sfx = carve(xT, 0, DEC_BATCH, KPP, HEADS)
        lfg = carve(xT, 512, DEC_BATCH, KPP, HEADS)
        xg = [carve(z, i * 1024, D_MODEL) for i in range(2)]
        xgT = [carve(z, 2048 + i * 1024, KD, BLOCK) for i in range(2)]
        hT = [carve(z, 4096 + i * 256, 2, BLOCK) for i in range(2)]
        sil = [carve(z, 4608 + i * 256, 2 * BLOCK) for i in range(2)]
        yo = [carve(z, 5120 + i * 1024, D_MODEL) for i in range(2)]
        wr = carve(z, 7168, KD, GROUPS + EXPERTS)
        br = carve(z, 7328, GROUPS + EXPERTS)
        rt = carve(z, 7348, NT, GROUPS + EXPERTS)
        yg = carve(z, 0, NT, TOP_K, D_MODEL)
        moe_small = carve(z, 10240, 2000)

        r_at = [0]

        def rview(*dims):
            n = int(np.prod(dims))
            r_at[0] += n
            assert r_at[0] <= 2000
            return carve(moe_small, r_at[0] - n, *dims)

        r_gm, r_gw, r_v1, r_v2, r_vd, r_ex, r_w1, r_w2, r_m = [rview(NT) for _ in range(9)]
        r_goh, r_gd, r_ge, r_el, r_oh1, r_oh2, r_e2l = [rview(NT, 4) for _ in range(7)]
        r_t16 = rview(NT, GROUPS, 4)
        r_hot = [rview(NT, EXPERTS) for _ in range(TOP_K)]
        r_pick = rview(NT, EXPERTS)
        r_pos, r_row = rview(NT, EXPERTS), rview(NT, EXPERTS)
        r_tot, r_nb, r_cum, r_more = [rview(EXPERTS) for _ in range(4)]
        r_owner3 = rview(MORE, EXPERTS)
        r_plan = rview(N_BLOCKS + 1)
        r_even = rview(MORE // 2)
        r_rowf = rview(NT, TOP_K)

        w13 = [ring[:, s, :].rearrange("p (w k f) -> p w k f", w=2, k=KD) for s in range(2)]
        w2 = [ring[:, 2, s * 2048:(s + 1) * 2048].rearrange("p (f n) -> p f n", f=2) for s in range(2)]
        slab = [ring[:, s, :].rearrange("p (k n) -> p k n", k=KD) for s in range(3)]

        rows = [P] * NP + [NS]
        tiles = range(NT)

        s_tab = ctx.enter_context(nc.semaphore("tables_loaded"))
        s_x0 = ctx.enter_context(nc.semaphore("tokens_loaded"))
        s_zero = ctx.enter_context(nc.semaphore("tails_zeroed"))
        s_idx = ctx.enter_context(nc.semaphore("rows_numbered"))
        s_fill = ctx.enter_context(nc.semaphore("expert_in_filled"))
        with nc.Block() as block:
            @block.sync
            def _(sp):
                sp.dma_start(tab[:, :], d["tables"]).then_inc(s_tab, 16)
                for i in range(N_PAGES):
                    sp.dma_start(pages[i * RPP:(i + 1) * RPP, :],
                                 d["page_table"][:, i:i + 1].rearrange("b o -> o b").to_broadcast([RPP, DEC_BATCH]),
                                 allow_slow_non_contiguous=True).then_inc(s_tab, 16)
                sp.dma_start(x[:, 0:NP, :], d["x_prompt"].rearrange("o (t p) n -> p (o t) n", p=P)).then_inc(s_x0, 16)
                sp.dma_start(x[0:NS, NP, :], d["x_sample"].rearrange("b s n -> (b s) n")).then_inc(s_x0, 16)
                sp.wait_ge(s_zero, 1)
                sp.wait_ge(s_x0, 32)

            @block.vector
            def _(dve):
                dve.memset(zero[:, :], 0.0).then_inc(s_zero, 1)
                dve.memset(x[NS:P, NP, :], 0.0)
                dve.memset(zt[NS:P, NP, :], 0.0)
                dve.wait_ge(s_tab, 16 * (1 + N_PAGES))
                dve.tensor_scalar(idx_f[:, :], pages[:, :], float(RPP), T("sub_row"), ALU.mult, ALU.add).then_inc(s_idx, 1)

        xT_ps = sig("xT_ps")
        xT_sb = sig("xT_sb")
        w_slab0 = sig("w_slab0")
        w_slab1 = sig("w_slab1")
        w_slab2 = sig("w_slab2")
        z_ps = sig("z_ps")
        z_sb = sig("z_sb")
        bias_in = sig("bias_in")
        gate_in = sig("gate_in")
        gelu_done = sig("gelu_done")
        silu_done = sig("silu_done")
        sigm_done = sig("sigm_done")
        norm_sum = sig("norm_sum")
        norm_rs = sig("norm_rs")
        va_ready = sig("va_ready")
        ws_ps = sig("ws_ps")
        ws_n = sig("ws_n")
        ws_s8 = sig("ws_s8")
        ws_sb = sig("ws_sb")
        a_ps = sig("a_ps")
        rope_done = sig("rope_done")
        chain_v = sig("chain_v")
        chain_a = sig("chain_a")
        b_T = sig("b_T")
        b_Tsb = sig("b_Tsb")
        b_sc = sig("b_sc")
        b_sw = sig("b_sw")
        b_out = sig("b_out")
        b_kd = sig("b_kd")
        b_up = sig("b_up")
        b_state = sig("b_state")
        s_in = sig("s_in")
        qm_q = sig("qm_q")
        qm_ps = sig("qm_ps")
        qm_sb = sig("qm_sb")
        km_sb = sig("km_sb")
        km_used = sig("km_used")
        idx_set = sig("idx_set")
        f_in = sig("f_in")
        f_exp = sig("f_exp")
        f_gates = sig("f_gates")
        gate_ps = sig("gate_ps")
        gate_sb = sig("gate_sb")
        c_T = sig("c_T")
        c_Tsb = sig("c_Tsb")
        c_dg = sig("c_dg")
        c_row = sig("c_row")
        c_t = sig("c_t")
        c_w = sig("c_w")
        c_exps = sig("c_exps")
        c_mt = sig("c_mt")
        c_last = sig("c_last")
        c_gin = sig("c_gin")
        c_gs = sig("c_gs")
        c_sc = sig("c_sc")
        c_sw = sig("c_sw")
        c_vx = sig("c_vx")
        c_out = sig("c_out")
        c_kd = sig("c_kd")
        c_up = sig("c_up")
        c_cd = sig("c_cd")
        c_free = sig("c_free")
        d_T = sig("d_T")
        d_Tsb = sig("d_Tsb")
        d_cum = sig("d_cum")
        d_dg = sig("d_dg")
        d_row = sig("d_row")
        d_ncr = sig("d_ncr")
        d_lg = sig("d_lg")
        d_lgx = sig("d_lgx")
        d_exp = sig("d_exp")
        d_pT = sig("d_pT")
        d_pTsb = sig("d_pTsb")
        d_o = sig("d_o")
        d_y = sig("d_y")
        e_T = sig("e_T")
        e_Tsb = sig("e_Tsb")
        e_kps = sig("e_kps")
        e_ksb = sig("e_ksb")
        e_s = sig("e_s")
        e_pm = sig("e_pm")
        e_mt = sig("e_mt")
        e_dg = sig("e_dg")
        e_bc = sig("e_bc")
        e_xs = sig("e_xs")
        e_p = sig("e_p")
        e_psum = sig("e_psum")
        e_pv = sig("e_pv")
        e_fin = sig("e_fin")
        e_lf = sig("e_lf")
        e_cumps = sig("e_cumps")
        e_yT = sig("e_yT")
        e_tot = sig("e_tot")
        rms_s = sig("rms_s")
        rms_r = sig("rms_r")
        merged = sig("merged")
        m_ps = sig("m_ps")
        m_sb = sig("m_sb")
        wout_in = sig("wout_in")
        o_ps = sig("o_ps")
        o_var = sig("o_var")
        o_rstd = sig("o_rstd")
        ln_n = sig("ln_n")
        ln_par = sig("ln_par")
        h_ps = sig("h_ps")
        sil_sb = sig("sil_sb")
        y_ps = sig("y_ps")
        w13_in0 = sig("w13_in0")
        w13_in1 = sig("w13_in1")
        w2_in0 = sig("w2_in0")
        w2_in1 = sig("w2_in1")
        r_ps = sig("r_ps")
        r_w = sig("r_w")
        r_exp = sig("r_exp")
        r_lg = sig("r_lg")
        r_e2 = sig("r_e2")
        r_e2x = sig("r_e2x")
        stored = sig("stored")
        stored_in = sig("stored_in")
        y_init = sig("y_init")
        y_free = sig("y_free")
        r_picked = sig("r_picked")
        r_pos_ps = sig("r_pos_ps")
        planned = sig("planned")
        xg_in0 = sig("xg_in0")
        xg_in1 = sig("xg_in1")
        xgT_ps = sig("xgT_ps")
        xgT_sb = sig("xgT_sb")
        hT_sb = sig("hT_sb")
        y_out0 = sig("y_out0")
        y_out1 = sig("y_out1")
        y_sb = sig("y_sb")
        y_stored = sig("y_stored")
        k_in = ctx.enter_context(nc.semaphore("k_gathered"))
        v_in = ctx.enter_context(nc.semaphore("v_gathered"))
        l_in = ctx.enter_context(nc.semaphore("logf_gathered"))
        x_sent = ctx.enter_context(nc.semaphore("tokens_sent"))
        y_back = [ctx.enter_context(nc.semaphore(f"outputs_back{t}")) for t in range(NT)]

        s_sum = stat(NT * HEADS)
        s_rstd = stat(NT * HEADS)
        ff = stat(NT * 2 * HEADS)
        fa = stat(NT * 2 * HEADS)
        fe = stat(NT * 2 * HEADS)
        lf = stat(NT * 2 * HEADS)
        cum = stat(NT * HEADS)
        gi = stat(NT * HEADS)
        ncum = stat(NT * HEADS)
        mp_p = stat(HEADS)
        mp_s = stat(HEADS)
        gp = stat(HEADS)
        mcol = stat(HEADS)
        mtb = stat(2 * HEADS)
        wx = stat(2 * HEADS)
        we = stat(2 * HEADS)
        gx = stat(2 * HEADS)
        ge = stat(2 * HEADS)
        gcol = stat(PAIRS)
        den = stat(HEADS)
        rden = stat(HEADS)
        nmax = stat(NP * HEADS)
        rsum = stat(NP * HEADS)
        drec = stat(NP * HEADS)
        pmax = stat(32)
        pcol = stat(2)
        pdiag = stat(32)
        ptot = stat(32)
        prec = stat(32)
        sufp = stat(DEC_BATCH * HEADS)
        lastv = stat(2 * HEADS)
        lnst = stat(12)
        lnmv = stat(2)
        lnr = stat(2)
        par_pair = "p (a b) -> p b a"

        def v4(ap):
            return ap.rearrange("p t (h e) -> p t h e", h=HEADS)

        def th(ap, a=NT):
            return ap.rearrange("p (t h) -> p t h", t=a)

        def over_e(ap4, n=HD):
            return ap4.unsqueeze(3).to_broadcast([*ap4.shape, n])

        def heads(ap, w=HD):
            return ap.rearrange("p (h e) -> p h e", e=w)

        def by_par(ap):
            return ap.rearrange("p (b a) e -> p a b e", a=2)

        with nc.Fori(0, DEPTH) as layer:
            L = bass.ds(layer, 1)
            with nc.Block() as block:
                @block.sync
                def _(sp):
                    sp.dma_start(vbuf[:, 0:D_IN], d["b_in"][L, :].to_broadcast([P, D_IN])).then_inc(bias_in, 16)
                    w_in_l = d["w_in"][L].rearrange("o (k p) c -> p (o k) c", p=P)
                    w_slab = (w_slab0, w_slab1, w_slab2)

                    def load_slab(g):
                        w = min(SLAB, D_IN - g * SLAB)
                        sp.dma_start(slab[g % 3][:, :, 0:w], w_in_l[:, :, g * SLAB:g * SLAB + w]).then_inc(w_slab[g % 3], 16)

                    for g in range(3):
                        load_slab(g)
                    with sp.If(layer < 1):
                        for rows_d in (xd, yd):
                            sp.dma_start(rows_d.rearrange("(p a) (c n) -> p (a c) n", p=P, n=P),
                                         zero[:, :].unsqueeze(1).to_broadcast([P, N_BLOCKS * D_MODEL // P, P])).then_inc(s_fill, 16)
                    ws_l = d["w_s"][L].rearrange("o h t s -> t (o h) s")
                    bs_l = d["b_s"][L].rearrange("o h t -> t (o h)")
                    for b in range(DEC_BATCH):
                        at = slice(b * DEC_SEQ, (b + 1) * DEC_SEQ)
                        sp.dma_start(ws8[at], ws_l[0:DEC_SEQ, :, 0:DEC_SEQ]).then_inc(gate_in, 16)
                        sp.dma_start(bss[at, :], bs_l[0:DEC_SEQ, :], allow_slow_non_contiguous=True).then_inc(gate_in, 16)
                        sp.dma_start(mp_s[at, :], d["state_mlstm_m"][L, b, :].to_broadcast([DEC_SEQ, HEADS])).then_inc(gate_in, 16)
                    sp.dma_start(bs[:, :], bs_l, allow_slow_non_contiguous=True).then_inc(gate_in, 16)
                    sp.dma_start(gmix[:, :], d["g_mix"][L].rearrange("o (k p) -> p (o k)", p=P),
                                 allow_slow_non_contiguous=True).then_inc(gate_in, 16)
                    for g in range(3, N_SLABS):
                        sp.wait_ge(z_ps, NT * (g - 2))
                        load_slab(g)
                    sp.wait_ge(z_ps, NT * 6)
                    sp.dma_start(ws_nat, ws_l).then_inc(ws_n, 16)
                    sp.wait_ge(z_ps, NT * N_SLABS)
                    w_out_l = d["w_out"][L].rearrange("o (k p) c -> p (o k) c", p=P)
                    for s in range(2):
                        sp.dma_start(slab[s][:, :, :], w_out_l[:, :, s * SLAB:(s + 1) * SLAB]).then_inc(wout_in, 16)
                    sp.wait_ge(rope_done, 1)
                    for b in range(DEC_BATCH):
                        at = slice(b % 2 * HD, (b % 2 + 1) * HD)
                        for st, to in (("state_ret", rs[at, b // 2, :, :]), ("state_mlstm_c", cs[at, b // 2, :, 0:HD])):
                            sp.dma_start(to, d[st][L, b].rearrange("o h d e -> d (o h) e")).then_inc(s_in, 16)
                        sp.dma_start(cs[at, b // 2, :, HD:HD + 1].rearrange("p h o -> p (h o)"), d["state_mlstm_n"][L, b].rearrange("o h d -> d (o h)"),
                                     allow_slow_non_contiguous=True).then_inc(s_in, 16)
                    sp.wait_ge(e_pv, DEC_BATCH)
                    for i, name in enumerate(("ln1_g", "ln1_b", "ln2_g", "ln2_b")):
                        sp.dma_start(vbuf[:, i * D_MODEL:(i + 1) * D_MODEL],
                                     d[name][L, :].to_broadcast([P, D_MODEL])).then_inc(ln_par, 16)
                    sp.wait_ge(m_ps, 2 * NT)
                    sp.dma_start(wr[:, :, 0:GROUPS], d["w_rg"][L].rearrange("o (k p) g -> p (o k) g", p=P)).then_inc(r_w, 16)
                    for g in range(GROUPS):
                        c = GROUPS * (g + 1)
                        sp.dma_start(wr[:, :, c:c + 4], d["w_re"][L, g].rearrange("o (k p) e -> p (o k) e", p=P)).then_inc(r_w, 16)
                    sp.dma_start(br[:, 0:GROUPS], d["b_rg"][L, :].to_broadcast([P, GROUPS])).then_inc(r_w, 16)
                    sp.dma_start(br[:, GROUPS:], d["b_re"][L].rearrange("o g e -> o (g e)").to_broadcast([P, EXPERTS])).then_inc(r_w, 16)
                    sp.wait_ge(o_ps, NT)
                    w13_in, w2_in = (w13_in0, w13_in1), (w2_in0, w2_in1)

                    def load_w13(e, s):
                        sp.dma_start(w13[s][:, 0], d["w1"][e].rearrange("o (p k) f -> p (o k) f", p=P)).then_inc(w13_in[s], 16)
                        sp.dma_start(w13[s][:, 1], d["w3"][e].rearrange("o (p k) f -> p (o k) f", p=P)).then_inc(w13_in[s], 16)

                    def load_w2(e, s):
                        sp.dma_start(w2[s], d["w2"][e].rearrange("o (p f) n -> p (o f) n", p=P)).then_inc(w2_in[s], 16)

                    def expert_of(k):
                        return bass.ds(layer * EXPERTS + sp.value_load(plan[0:1, bass.ds(k, 1)], min_val=0, max_val=EXPERTS - 1), 1)

                    for s in range(2):
                        load_w13(bass.ds(layer * EXPERTS + s, 1), s)
                    for s in range(2):
                        load_w2(bass.ds(layer * EXPERTS + s, 1), s)
                    sp.wait_ge(planned, 1)
                    last_pair = sp.value_load(plan[0:1, N_BLOCKS:N_BLOCKS + 1], min_val=EXPERTS // 2 - 1, max_val=N_BLOCKS // 2 - 1)
                    with sp.Fori(1, last_pair + 1) as i:
                        es = [expert_of(i * 2 + s) for s in range(2)]
                        for s in range(2):
                            sp.wait_ge(h_ps, i * 2 + (s - 1))
                            load_w13(es[s], s)
                        for s in range(2):
                            sp.wait_ge(y_ps, i * 2 + (s - 1))
                            load_w2(es[s], s)

                @block.gpsimd
                def _(pool):
                    ck = d["cache_k"].rearrange("l n (a b) h e -> (l n a) (b h e)", b=KPP)
                    cv = d["cache_v"].rearrange("l n (a b) h e -> (l n a) (b h e)", b=KPP)
                    cl = d["cache_logf"].rearrange("l n (a b) h -> (l n a) (b h)", b=KPP)

                    def gather(to, table, b, sem):
                        pool.indirect_dma_start(to, None, table, bass.IndirectOffsetOnAxis(idx_u[:, b:b + 1], 0)).then_inc(sem, 16)

                    pool.wait_ge(idx_set, 1)
                    gather(kbuf[:, :], ck, 0, k_in)
                    pool.wait_ge(z_sb, NT * N_SLABS)
                    gather(vbuf[:, :], cv, 0, v_in)
                    pool.wait_ge(d_y, NP)
                    for b in range(DEC_BATCH):
                        gather(lfg[:, b, :, :].rearrange("p a b -> p (a b)"), cl, b, l_in)
                    for b in range(1, DEC_BATCH):
                        pool.wait_ge(e_kps, 8 * b)
                        gather(kbuf[:, :], ck, b, k_in)
                        pool.wait_ge(e_pv, b)
                        gather(vbuf[:, :], cv, b, v_in)

                    pool.wait_ge(s_fill, 32)
                    pool.wait_ge(planned, 1)
                    for t in tiles:
                        n = rows[t]
                        for c in range(TOP_K):
                            pool.indirect_dma_start(xd, bass.IndirectOffsetOnAxis(rows_u[0:n, t, c:c + 1], 0), x[0:n, t, :], None).then_inc(x_sent, 16)
                    pool.wait_ge(y_stored, 1)
                    for t in tiles:
                        n = rows[t]
                        for c in range(TOP_K):
                            pool.indirect_dma_start(yg[0:n, t, c, :], None, yd, bass.IndirectOffsetOnAxis(rows_u[0:n, t, c:c + 1], 0)).then_inc(y_back[t], 16)

                @block.scalar
                def _(act):
                    due = Due()
                    own = Due()

                    def link(ins):
                        ins.then_inc(chain_a, 1)
                        act.wait_ge(chain_a, own(chain_a))

                    def f(out, in_, fn, **kw):
                        return nc.scalar.activation(out, in_, fn, **kw)

                    def rsqrt(out, in_, eps, scale, sem):
                        link(f(out, in_, ACT.Ln, scale=scale, bias=eps))
                        f(out, out, ACT.Exp, scale=-0.5).then_inc(sem, 1)

                    def store(out, in_, **kw):
                        act.dma_start(out, in_, **kw).then_inc(stored, 16)
                        own(stored, 16)

                    for i in range(2 * NT):
                        t, hf = i // 2, i % 2
                        act.wait_ge(xT_ps, i + 1)
                        f(xTv[:, 4 * hf:4 * hf + 4, t * P:t * P + rows[t]], ps[:, 4 + i % 4, 0:4 * rows[t]].rearrange("p (k n) -> p k n", k=4),
                          ACT.Copy).then_inc(xT_sb, 1)
                    act.wait_ge(z_sb, NT * 1)
                    f(zt[:, :, 0:2 * GW], zt[:, :, 0:2 * GW], ACT.Gelu_apprx_tanh).then_inc(gelu_done, 1)
                    act.wait_ge(z_sb, NT * 3)
                    f(Zall("b_g"), Zall("b_g"), ACT.Silu).then_inc(silu_done, 1)
                    act.wait_ge(z_sb, NT * 5)
                    f(Zall("c_o"), Zall("c_o"), ACT.Sigmoid).then_inc(sigm_done, 1)
                    act.wait_ge(z_sb, NT * N_SLABS)
                    kp, vp = d["k_prompt"], d["v_prompt"]
                    for name, out in (("d_k", kp), ("d_v", vp)):
                        c = COLS[name]
                        store(out[L].rearrange("o a (t p) h e -> p (o a t) (h e)", p=P), zt[:, 0:NP, c:c + GW])
                    for name, out in (("d_k", d["k_sample"]), ("d_v", d["v_sample"])):
                        store(out[L].rearrange("o b t h e -> (o b t) (h e)"), Z(NP, name, NS))
                    act.wait_ge(norm_sum, 1)
                    rsqrt(s_rstd, s_sum, T("ln_eps"), 1.0 / HD, norm_rs)
                    act.wait_ge(va_ready, 1)
                    store(d["chunk_v_sample"][L].rearrange("o b t h e -> (o b t) (h e)"), Z(NP, "a_v", NS))
                    act.wait_ge(f_in, 1)
                    link(f(fe, fa, ACT.Exp))
                    f(fe, fe, ACT.Ln, bias=1.0).then_inc(f_exp, 1)
                    act.wait_ge(f_gates, 1)
                    store(d["logf_prompt"][L].rearrange("o a (t p) h -> p (o a t) h", p=P), th(lf)[:, 0:NP, HEADS:])
                    store(d["logf_sample"][L].rearrange("o b t h -> (o b t) h"), th(lf)[0:NS, NP, HEADS:])

                    for t in tiles:
                        n = rows[t]
                        act.wait_ge(b_T, t + 1)
                        src = ps[:, 5, 0:4 * n].rearrange("p (a n) -> p a n", a=4)
                        f(qkT[:, 0:2, 0:n], src[:, 0:2], ACT.Copy).then_inc(b_Tsb, 1)
                        f(qkT[:, 2:4, 0:n], src[:, 2:4], ACT.Copy, scale=SCALE).then_inc(b_Tsb, 1)
                        if t == NP - 1:
                            act.wait_ge(b_state, NP)
                            for par in range(2):
                                store(d["ret_prompt"][L].rearrange("o a (pr r) d e -> r d (o a pr) e", r=2)[par],
                                      ret[par * HD:(par + 1) * HD])
                    act.wait_ge(b_state, NT)
                    for b in range(DEC_BATCH):
                        at = slice(b % 2 * HD, (b % 2 + 1) * HD)
                        store(d["ret_sample"][L, b].rearrange("o h d e -> d (o h) e"), rs[at, b // 2, :, :])

                    for t in tiles:
                        n = rows[t]
                        act.wait_ge(c_T, t + 1)
                        src = ps[:, 5, 0:4 * n].rearrange("p (a n) -> p a n", a=4)
                        f(qkT[:, 0:2, 0:n], src[:, 0:2], ACT.Copy).then_inc(c_Tsb, 1)
                        f(qkT[:, 2:4, 0:n], src[:, 2:4], ACT.Copy, scale=SCALE).then_inc(c_Tsb, 1)
                        if t > 0:
                            act.wait_ge(c_up, t)
                        else:
                            act.wait_ge(c_free, 1)
                        f(vx[0:n, :, 0:HD], heads(Z(t, "c_v", n)), ACT.Copy).then_inc(c_vx, 1)
                        act.wait_ge(c_t, t + 1)
                        for h in range(HEADS):
                            c = t * HEADS + h
                            f(wexp[0:n, h, 0:n], wexp[0:n, h, 0:n], ACT.Exp, bias=gi[0:n, c:c + 1]).then_inc(c_w, 1)
                        act.wait_ge(c_mt, t + 1)
                        f(we[0:n], wx[0:n], ACT.Exp).then_inc(c_exps, 1)
                        act.wait_ge(c_gin, t + 1)
                        f(ge[0:n], gx[0:n], ACT.Exp).then_inc(c_gs, 1)
                        if t == NP - 1:
                            act.wait_ge(c_cd, NP)
                            for par in range(2):
                                at = slice(par * HD, (par + 1) * HD)
                                store(d["mlstm_c_prompt"][L].rearrange("o a (pr r) d e -> r d (o a pr) e", r=2)[par],
                                      mem[at, :, 0:HD])
                                store(d["mlstm_n_prompt"][L].rearrange("o a (pr r) d -> r d (o a pr)", r=2)[par],
                                      mem[at, :, HD:HD + 1].rearrange("p a b -> p (a b)"), allow_slow_non_contiguous=True)
                            store(d["mlstm_m_prompt"][L].rearrange("o a h -> (o a) h"), mp_p[0:1, :])
                    act.wait_ge(c_cd, NT)
                    for b in range(DEC_BATCH):
                        at = slice(b % 2 * HD, (b % 2 + 1) * HD)
                        store(d["mlstm_c_sample"][L, b].rearrange("o h d e -> d (o h) e"), cs[at, b // 2, :, 0:HD])
                        store(d["mlstm_n_sample"][L, b].rearrange("o h d -> d (o h)"),
                              cs[at, b // 2, :, HD:HD + 1].rearrange("p h o -> p (h o)"), allow_slow_non_contiguous=True)
                    store(d["mlstm_m_sample"][L].rearrange("o b h -> (o b) h"), mp_s[0:NS:DEC_SEQ, :])
                    act.wait_ge(stored, own(stored, 0))
                    act.sem_inc(stored_in, 1)

                    for t in range(NP):
                        act.wait_ge(d_T, t + 1)
                        src = ps[:, t % 2, :].rearrange("p (a n) -> p a n", a=4)
                        f(qTa[:, :, t * P:(t + 1) * P], src[:, 0:2], ACT.Copy, scale=SCALE).then_inc(d_Tsb, 1)
                        f(kTa[:, :, t * P:(t + 1) * P], src[:, 2:4], ACT.Copy).then_inc(d_Tsb, 1)
                    for m in range(NP * HEADS + 1):
                        if m < NP * HEADS:
                            w = (m // HEADS + 1) * P
                            act.wait_ge(d_lgx, m + 1)
                            f(lg[m % 2][:, 0:w], lg[m % 2][:, 0:w], ACT.Exp, bias=nmax[:, m:m + 1],
                              accum_out=rsum[:, m:m + 1]).then_inc(d_exp, 1)
                        if m > 0:
                            w = (m - 1) // HEADS + 1
                            act.wait_ge(d_pT, m)
                            f(pT[(m - 1) % 2][:, 0:w, :], ps[:, 4 + (m - 1) % 2, 0:w * P].rearrange("p (a n) -> p a n", n=P),
                              ACT.Copy).then_inc(d_pTsb, 1)

                    act.wait_ge(e_T, 1)
                    f(kTn, ps[:, 0, 2 * NS:4 * NS].rearrange("p (a n) -> p a n", a=2), ACT.Copy).then_inc(e_Tsb, 1)
                    for i in range(DEC_BATCH + 1):
                        for g in range(8):
                            if i < DEC_BATCH:
                                m = 8 * i + g
                                act.wait_ge(e_kps, m + 1)
                                if m >= 2:
                                    act.wait_ge(e_s, m - 1)
                                f(kTs[m % 2], ps[:, m % 2, :].rearrange("p (a n) -> p a n", a=4), ACT.Copy).then_inc(e_ksb, 1)
                            if g == 5 and i > 0:
                                act.wait_ge(e_xs, i)
                                if i > 2:
                                    act.wait_ge(e_pv, i - 2)
                                f(pp[(i - 1) % 2], xs[(i - 1) % 2], ACT.Exp).then_inc(e_p, 1)

                    for _ in MERGED:
                        act.wait_ge(rms_s, due(rms_s))
                        rsqrt(s_rstd, s_sum, T("rms_eps"), 1.0 / HD, rms_r)

                    def layer_norm():
                        for t in tiles:
                            n = rows[t]
                            act.wait_ge(o_var, due(o_var))
                            rsqrt(lnr[0:n, 0:1], lnmv[0:n, 1:2], T("ln_eps", n), 1.0, o_rstd)
                    layer_norm()
                    for i in range(2 * NT):
                        t, hf = i // 2, i % 2
                        act.wait_ge(xT_ps, 2 * NT + i + 1)
                        f(xTv[:, 4 * hf:4 * hf + 4, t * P:t * P + rows[t]], ps[:, 4 + i % 4, 0:4 * rows[t]].rearrange("p (k n) -> p k n", k=4),
                          ACT.Copy).then_inc(xT_sb, 1)
                    act.wait_ge(r_lg, 1)
                    f(r_ge, r_gd, ACT.Exp).then_inc(r_exp, 1)
                    act.wait_ge(r_e2, 1)
                    f(r_ex, r_vd, ACT.Exp).then_inc(r_e2x, 1)
                    act.wait_ge(planned, 1)
                    last_pair = act.value_load(plan[0:1, N_BLOCKS:N_BLOCKS + 1], min_val=EXPERTS // 2 - 1, max_val=N_BLOCKS // 2 - 1)
                    act.wait_ge(x_sent, layer * (16 * NT * TOP_K) + 16 * NT * TOP_K)
                    xg_in, y_out = (xg_in0, xg_in1), (y_out0, y_out1)

                    def load_block(k, s):
                        act.dma_start(xg[s], xd[bass.ds(k * BLOCK, BLOCK), :]).then_inc(xg_in[s], 16)

                    def turn_block(k2, s):
                        for hf in range(2):
                            act.wait_ge(xgT_ps, k2 + (hf + 1))
                            f(xgT[s][:, 4 * hf:4 * hf + 4, :], ps[:, hf, :].rearrange("p (k n) -> p k n", k=4), ACT.Copy).then_inc(xgT_sb, 1)

                    def act_block(i, k, s, more, turn):
                        if more:
                            load_block(k + 2, s)
                        act.wait_ge(h_ps, k + 1)
                        f(sil[s], ps[:, 2 + s, 0:2 * BLOCK], ACT.Silu).then_inc(sil_sb, 1)
                        if turn:
                            turn_block(k * 2 + 2, 1 - s)
                        act.wait_ge(y_ps, k + 1)
                        act.wait_ge(y_out[s], i * 16 + 16)
                        f(yo[s][:, SLAB:], ps[:, 5 + 2 * s, :], ACT.Copy).then_inc(y_sb, 1)
                        act.wait_ge(y_sb, k * 2 + 5)
                        act.dma_start(yd[bass.ds(k * BLOCK, BLOCK), :], yo[s]).then_inc(y_out[s], 16)

                    act.sem_inc(y_out0, 16)
                    act.sem_inc(y_out1, 16)
                    for s in range(2):
                        act.dma_start(xg[s], xd[s * BLOCK:(s + 1) * BLOCK, :]).then_inc(xg_in[s], 16)
                    turn_block(0, 0)
                    with act.Fori(0, last_pair) as i:
                        act_block(i, i * 2, 0, True, True)
                        act_block(i, i * 2 + 1, 1, True, True)
                    lp = last_pair
                    act_block(lp, lp * 2, 0, False, True)
                    act_block(lp, lp * 2 + 1, 1, False, False)
                    for s in range(2):
                        act.wait_ge(y_out[s], last_pair * 16 + 32)
                    act.sem_inc(y_stored, 1)
                    for t in tiles:
                        f(x[0:rows[t], t, :], x[0:rows[t], t, :], ACT.Copy, scale=ALPHA).then_inc(y_init, 1)
                    layer_norm()
                    act.wait_ge(stored, own(stored, 0))

                @block.vector
                def _(dve):
                    due = Due()
                    own = Due()
                    V = nc.vector

                    def link(ins, sem=None):
                        sem = sem or chain_v
                        ins.then_inc(sem, 1)
                        dve.wait_ge(sem, own(sem))

                    def tt(out, a, b, op):
                        return V.tensor_tensor(out, a, b, op)

                    V.tensor_copy(idx_u[:, :], idx_f[:, :]).then_inc(idx_set, 1)
                    link(V.tensor_scalar(idx_f[:, :], idx_f[:, :], float(N_POOL * RPP), None, ALU.add))
                    dve.wait_ge(bias_in, 16)
                    for g in range(N_SLABS):
                        w = min(SLAB, D_IN - g * SLAB)
                        for t in tiles:
                            i, n = g * NT + t, rows[t]
                            dve.wait_ge(z_ps, i + 1)
                            tt(zt[0:n, t, g * SLAB:g * SLAB + w], ps[0:n, i % 4, 0:w], vbuf[0:n, g * SLAB:g * SLAB + w],
                               ALU.add).then_inc(z_sb, 1)
                    dve.wait_ge(z_sb, NT * N_SLABS)
                    dve.wait_ge(gelu_done, 1)
                    va, sq = v4(Zall("a_v")), v4(tmp_a)
                    link(V.tensor_reduce(th(s_sum), va, AX.X, ALU.add))
                    link(V.tensor_scalar(s_sum, s_sum, 1.0 / HD, None, ALU.mult))
                    link(tt(va, va, over_e(th(s_sum)), ALU.subtract))
                    link(tt(sq, va, va, ALU.mult))
                    V.tensor_reduce(th(s_sum), sq, AX.X, ALU.add).then_inc(norm_sum, 1)
                    V.tensor_copy(th(ff)[:, :, 0:HEADS], Zall("c_f", HEADS))
                    link(V.tensor_copy(th(ff)[:, :, HEADS:], Zall("d_f", HEADS)))
                    link(V.tensor_scalar(fa, ff, -1.0, None, ALU.mult))
                    tt(fa, ff, fa, ALU.min).then_inc(f_in, 1)
                    c0 = COLS["b_q"]
                    qk = zt[:, :, c0:c0 + 2 * GW].rearrange("p t (h r e) -> p t h r e", h=2 * HEADS, r=2)
                    x1, x2 = qk[:, :, :, 0, :], qk[:, :, :, 1, :]
                    co, si = [T(name).rearrange("p (t e) -> p t e", t=NT).unsqueeze(2).to_broadcast([P, NT, 2 * HEADS, HD // 2])
                              for name in ("cos", "sin")]
                    rb, rc = [tmp.rearrange("p t (h e) -> p t h e", h=2 * HEADS) for tmp in (tmp_b, tmp_c)]
                    tt(rb, x1, si, ALU.mult)
                    link(tt(rc, x2, si, ALU.mult))
                    tt(x1, x1, co, ALU.mult)
                    link(tt(x2, x2, co, ALU.mult))
                    tt(x1, x1, rc, ALU.subtract)
                    link(tt(x2, x2, rb, ALU.add))
                    dve.wait_ge(norm_rs, 1)
                    tt(va, va, over_e(th(s_rstd)), ALU.mult).then_inc(va_ready, 1)
                    dve.wait_ge(va_ready, 1)
                    V.memset(ret[:, :, :], 0.0)
                    V.memset(mem[:, :, :], 0.0)
                    V.memset(mp_p, 0.0).then_inc(rope_done, 1)
                    dve.wait_ge(rope_done, 1)
                    dve.wait_ge(f_exp, 1)
                    link(V.tensor_scalar(ff, ff, 0.0, None, ALU.min))
                    tt(lf, ff, fe, ALU.subtract).then_inc(f_gates, 1)
                    dve.wait_ge(f_gates, 1)
                    dve.wait_ge(gate_in, 16 * (3 * DEC_BATCH + 2))
                    up_b = T("lower_s", NS).rearrange("p (b s) -> p b s", s=DEC_SEQ).unsqueeze(1)
                    link(tt(ws_exp[0:NS].rearrange("p h (b s) -> p h b s", s=DEC_SEQ),
                            ws8[:, :, :].unsqueeze(2).to_broadcast([NS, HEADS, DEC_BATCH, DEC_SEQ]),
                            up_b.to_broadcast([NS, HEADS, DEC_BATCH, DEC_SEQ]), ALU.mult), ws_s8)
                    dve.wait_ge(ws_ps, 1)
                    tt(wsT[:, :, :], ps[:, 4, :].rearrange("p (h t) -> p h t", h=HEADS), rep(T("upper"), HEADS), ALU.mult).then_inc(ws_sb, 1)
                    dve.wait_ge(ws_ps, 2)
                    V.tensor_copy(wsTs[:, :, :], ps[0:NS, 5, 0:GW].rearrange("p (h t) -> p h t", h=HEADS)).then_inc(ws_sb, 1)
                    dve.wait_ge(a_ps, 1)
                    ya = v4(Zall("a_u"))
                    for t in tiles:
                        n = rows[t]
                        link(tt(mix[0:n, :, 0:HD], heads(ps[0:n, t if t < NP else 6, 0:GW]), b3((bs if t < NP else bss)[0:n, :], HD), ALU.add))
                        link(tt(ya[0:n, t], ya[0:n, t], mix[0:n, :, 0:HD], ALU.mult))
                    dve.wait_ge(gate_ps, 1)
                    V.tensor_copy(cum[:, 0:NP * HEADS], ps[:, 7, 0:NP * HEADS])
                    link(V.tensor_copy(cum[0:NS, NP * HEADS:], ps[0:NS, 7, NP * HEADS:NT * HEADS]), gate_sb)
                    ci = Zall("c_i", HEADS)
                    tt(th(gi)[:, 0:NP], ci[:, 0:NP], th(cum)[:, 0:NP], ALU.subtract)
                    link(tt(gi[0:NS, NP * HEADS:], ci[0:NS, NP], cum[0:NS, NP * HEADS:], ALU.subtract))

                    def sample_queries(name):
                        link(V.tensor_copy(qd2[0:NS].rearrange("p h (r e) -> p h r e", r=2),
                                           heads(Z(NP, name, NS)).unsqueeze(2).to_broadcast([NS, HEADS, 2, HD])), qm_q)
                        dve.wait_ge(qm_ps, due(qm_ps))
                        for bp in range(BP):
                            m = tt(qm[:, bp], ps[:, 4, 0:GW].rearrange("p (h n) -> p h n", h=HEADS),
                                   rep(T("seq_of")[:, bp * NS:(bp + 1) * NS], HEADS), ALU.mult)
                        m.then_inc(qm_sb, 1)

                    def sample_keys(w):
                        for h in range(HEADS):
                            if h > 0:
                                dve.wait_ge(km_used, due(km_used))
                            tt(km[0:NS], rep(kd[0:NS, h * HD:(h + 1) * HD], DEC_BATCH), b3(T("in_seq", NS), HD), ALU.mult).then_inc(km_sb, 1)
                        due(km_used)
                        dve.wait_ge(km_used, own(km_used, HEADS))

                    for t in tiles:
                        n, samp = rows[t], t == NP
                        sfx_ = "_s" if samp else ""
                        kdec = b3(T("k_dec" + sfx_, n), HD)
                        link(tt(heads(kd[0:n]), heads(Z(t, "b_k", n)), kdec, ALU.mult), b_kd)
                        if samp:
                            sample_queries("b_q")
                        dve.wait_ge(b_sc, t + 1)
                        tt(sw[0:n, :, 0:n].rearrange("p (a b) n -> p a b n", a=2), ps[0:n, 6:8, 0:2 * n].rearrange("p a (b n) -> p a b n", b=2),
                           T("dec" + sfx_, n).rearrange("p (a b n) -> p a b n", a=2, b=2), ALU.mult).then_inc(b_sw, 1)
                        dve.wait_ge(b_out, t + 1)
                        yb = heads(Z(t, "b_q", n))
                        if not samp:
                            link(tt(by_par(mix[0:n, :, 0:HD]), ps[0:n, 1:3, 0:2 * HD].rearrange("p a (b e) -> p a b e", b=2),
                                    T("q_dec", n).rearrange("p (a b) -> p a b", a=2).unsqueeze(3).to_broadcast([n, 2, 2, HD]), ALU.mult))
                        else:
                            link(tt(mix[0:n, :, 0:HD], heads(ps[0:n, 1, 0:GW]), b3(T("q_dec_s", n), HD), ALU.mult))
                        link(tt(yb, heads(ps[0:n, 0, 0:GW]), mix[0:n, :, 0:HD], ALU.add))
                        if not samp:
                            link(tt(ret[:, :, :], ret[:, :, :], b3(T("c_dec"), HD), ALU.mult))
                            dve.wait_ge(b_up, t + 1)
                            for par in range(2):
                                at = slice(par * HD, (par + 1) * HD)
                                m = tt(ret[at], ret[at], ps[at, 3, 0:4 * HD].rearrange("p (a b) -> p a b", a=2)[:, :, par * HD:(par + 1) * HD], ALU.add)
                            link(m, b_state)
                        else:
                            sample_keys("b")
                            link(tt(rs, rs, T("c_dec_s").unsqueeze(1).unsqueeze(3).to_broadcast([P, BP, HEADS, HD]), ALU.mult))
                            link(tt(rs.rearrange("p (x a) h e -> p x (a h e)", x=2), rs.rearrange("p (x a) h e -> p x (a h e)", x=2), ps[:, 2:4, :], ALU.add), b_state)

                    V.memset(vx[:, :, HD:HD + 1], 1.0).then_inc(c_free, 1)
                    dve.wait_ge(c_free, 1)
                    for t in tiles:
                        n, samp = rows[t], t == NP
                        sfx_ = "_s" if samp else ""
                        mp = mp_s if samp else mp_p
                        g_t, b_t = [a[0:n, t * HEADS:(t + 1) * HEADS] for a in (gi, cum)]
                        link(V.scalar_tensor_tensor(gp[0:n], mp[0:n], T("start" + sfx_, n), g_t, ALU.add, ALU.max))
                        tt(diag[0:n, :, 0:n], rep(T("ident", n)[:, 0:n], HEADS), b3(gp[0:n], n), ALU.mult).then_inc(c_dg, 1)
                        if samp:
                            sample_queries("c_q")
                        dve.wait_ge(c_row, t + 1)
                        mr = mrow_flat[0:n, 0:HEADS * n]
                        link(V.tensor_tensor_scan(mr, T("reset" + sfx_, n), ps[0:n, 3, 0:HEADS * n], 0.0, ALU.add, ALU.max))
                        mr = mr.rearrange("p (h n) -> p h n", h=HEADS)
                        tt(wexp[0:n, :, 0:n], rep(T("neg_ts" if samp else "neg_t", n), HEADS), mr, ALU.subtract).then_inc(c_t, 1)
                        link(tt(diag[0:n, :, 0:n], rep(T("ident", n)[:, 0:n], HEADS), mr, ALU.mult))
                        link(V.tensor_reduce(mcol[0:n], diag[0:n, :, 0:n], AX.X, ALU.add))
                        tt(wx[0:n, 0:HEADS], mp[0:n], mcol[0:n], ALU.subtract)
                        V.tensor_copy(mtb[0:n, HEADS:], b_t)
                        link(tt(mtb[0:n, 0:HEADS], b_t, mcol[0:n], ALU.add))
                        link(V.tensor_scalar(wx[0:n, HEADS:], mtb[0:n, 0:HEADS], -1.0, None, ALU.mult), c_mt)
                        dve.wait_ge(c_last, t + 1)
                        link(V.tensor_copy(lastv[0:n], ps[0:n, 3, 0:2 * HEADS]))
                        link(tt(lastv[0:n, HEADS:], lastv[0:n, HEADS:], lastv[0:n, 0:HEADS], ALU.subtract))
                        tt(gx[0:n, 0:HEADS], g_t, lastv[0:n, HEADS:], ALU.add)
                        link(tt(gx[0:n, HEADS:], mp[0:n], lastv[0:n, HEADS:], ALU.add), c_gin)
                        V.tensor_copy(mp[0:n], lastv[0:n, 0:HEADS])
                        dve.wait_ge(c_gs, t + 1)
                        link(V.scalar_tensor_tensor(heads(kd[0:n]), heads(Z(t, "c_k", n)), SCALE, b3(ge[0:n, 0:HEADS], HD), ALU.mult, ALU.mult), c_kd)
                        dve.wait_ge(c_sc, t + 1)
                        dve.wait_ge(c_w, HEADS * (t + 1))
                        tt(sw[0:n, :, 0:n].rearrange("p (a b) n -> p a b n", a=2), ps[0:n, 6:8, 0:2 * n].rearrange("p a (b n) -> p a b n", b=2),
                           by_par(wexp[0:n, :, 0:n]), ALU.mult).then_inc(c_sw, 1)
                        dve.wait_ge(c_out, t + 1)
                        dve.wait_ge(c_exps, t + 1)
                        wst = b3(we[0:n, 0:HEADS], HD + 1)
                        if not samp:
                            link(tt(by_par(mix[0:n]), ps[0:n, 1:3, 0:2 * (HD + 1)].rearrange("p a (b e) -> p a b e", b=2), by_par(wst), ALU.mult))
                        else:
                            link(tt(mix[0:n], heads(ps[0:n, 1, 0:HEADS * (HD + 1)], HD + 1), wst, ALU.mult))
                        link(tt(mix[0:n], heads(ps[0:n, 0, 0:HEADS * (HD + 1)], HD + 1), mix[0:n], ALU.add))
                        dcol = mix[0:n, :, HD:HD + 1].rearrange("p h o -> p (h o)")
                        link(V.scalar_tensor_tensor(den[0:n], dcol, -1.0, we[0:n, HEADS:], ALU.mult, ALU.max))
                        link(tt(den[0:n], den[0:n], dcol, ALU.max))
                        link(V.reciprocal(rden[0:n], den[0:n]))
                        link(tt(heads(Z(t, "c_q", n)), mix[0:n, :, 0:HD], b3(rden[0:n], HD), ALU.mult))
                        if not samp:
                            for par in range(2):
                                at = slice(par * HD, (par + 1) * HD)
                                m = V.tensor_copy(gcol[at], ge[at, HEADS:].rearrange("p (a b) -> p b a", b=2)[:, par, :])
                            link(m)
                            link(tt(mem[:, :, :], mem[:, :, :], b3(gcol, HD + 1), ALU.mult))
                            dve.wait_ge(c_up, t + 1)
                            for par in range(2):
                                at = slice(par * HD, (par + 1) * HD)
                                m = tt(mem[at], mem[at], ps[at, 3, 0:4 * (HD + 1)].rearrange("p (a b) -> p a b", a=2)[:, :, par * (HD + 1):(par + 1) * (HD + 1)], ALU.add)
                            link(m, c_cd)
                        else:
                            sample_keys("c")
                            csf = cs.rearrange("p a h e -> p (a h) e")
                            dve.wait_ge(c_up, t + 1)
                            link(tt(csf, csf, b3(ps[:, 7, 0:BP * HEADS], HD + 1), ALU.mult))
                            for bp, bank in enumerate((2, 3, 5, 6)):
                                m = tt(cs[:, bp].rearrange("p h e -> p (h e)"), cs[:, bp].rearrange("p h e -> p (h e)"),
                                       ps[:, bank, 0:HEADS * (HD + 1)], ALU.add)
                            link(m, c_cd)

                    dve.wait_ge(stored_in, 1)
                    dve.wait_ge(d_cum, 1)
                    V.tensor_scalar(ncum[:, 0:NP * HEADS], ps[:, 2, 0:NP * HEADS], -1.0, None, ALU.mult)
                    link(V.tensor_scalar(ncum[0:NS, NP * HEADS:], ps[0:NS, 2, NP * HEADS:NT * HEADS], -1.0, None, ALU.mult))
                    for h in range(HEADS):
                        if h >= 2:
                            dve.wait_ge(d_row, h - 1)
                        tt(dg[h % 2], rep(T("ident"), NP), b3(th(ncum)[:, 0:NP, h:h + 1].rearrange("p t o -> p (t o)"), P), ALU.mult).then_inc(d_dg, 1)
                        if h >= 1:
                            dve.wait_ge(d_row, h)
                            V.tensor_copy(ncr[:, h - 1, :], ps[:, 3 + (h - 1) % 2, :]).then_inc(d_ncr, 1)
                    dve.wait_ge(d_row, HEADS)
                    V.tensor_copy(ncr[:, HEADS - 1, :], ps[:, 3 + (HEADS - 1) % 2, :]).then_inc(d_ncr, 1)
                    dve.wait_ge(d_ncr, HEADS)

                    def d_finish(c):
                        dve.wait_ge(d_o, HEADS * (c + 1))
                        dve.wait_ge(d_exp, HEADS * (c + 1))
                        at = slice(c * HEADS, (c + 1) * HEADS)
                        link(V.reciprocal(drec[:, at], rsum[:, at]))
                        tt(heads(Z(c, "d_q")), heads(ps[:, 6 + c % 2, 0:GW]), b3(drec[:, at], HD), ALU.mult).then_inc(d_y, 1)

                    for m in range(NP * HEADS):
                        c, h = m // HEADS, m % HEADS
                        w = (c + 1) * P
                        if m >= 2:
                            dve.wait_ge(d_pT, m - 1)
                        dve.wait_ge(d_lg, m + 1)
                        link(tt(lg[m % 2][:, 0:w], ps[:, 2 + m % 2, 0:w], ncr[:, h, 0:w], ALU.add))
                        V.tensor_reduce(nmax[:, m:m + 1], lg[m % 2][:, 0:w], AX.X, ALU.max, negate=True).then_inc(d_lgx, 1)
                        if h == 2 and c > 0:
                            d_finish(c - 1)
                    d_finish(NP - 1)
                    dve.wait_ge(d_y, NP)

                    V.memset(qbd, 0.0)
                    V.memset(xs[0], NEG)
                    link(V.memset(xs[1], NEG))
                    dve.wait_ge(e_Tsb, 1)
                    for par in range(2):
                        at = slice(par * HD, (par + 1) * HD)
                        V.tensor_scalar(qbd[at, :, :, par * 8:par * 8 + 8], ps[at, 0, 0:2 * NS].rearrange("p (a b t) -> p a b t", a=2, t=DEC_SEQ),
                                        SCALE, None, ALU.mult).then_inc(e_Tsb, 1)
                    msk = T("neg_ts", NS).rearrange("p (b t) -> p b t", t=DEC_SEQ)
                    for h in range(HEADS):
                        m = tt(newb[0:NS, :, h, :], msk, ncum[0:NS, NP * HEADS + h:NP * HEADS + h + 1].unsqueeze(2).to_broadcast([NS, DEC_BATCH, DEC_SEQ]), ALU.add)
                    link(m)
                    dve.wait_ge(l_in, layer * (16 * DEC_BATCH) + 16 * DEC_BATCH)
                    link(V.tensor_reduce(sufp.rearrange("p (b h) -> p b h", h=HEADS), lfg.rearrange("p b k h -> p b h k"), AX.X, ALU.add), e_tot)
                    dve.wait_ge(e_cumps, 1)
                    link(V.tensor_copy(sfx[:, :, KPP - 1, :], ps[:, 7, 0:DEC_BATCH * HEADS].rearrange("p (b h) -> p b h", h=HEADS)))
                    for k in range(KPP - 2, -1, -1):
                        link(tt(sfx[:, :, k, :], sfx[:, :, k + 1, :], lfg[:, :, k + 1, :], ALU.add))

                    def e_finish(i):
                        dve.wait_ge(e_pv, i + 1)
                        bank = 4 if i % 2 else 7
                        link(V.reciprocal(prec, ps[:, bank, 64:96]))
                        for par in range(2):
                            at = slice(par * HD, (par + 1) * HD)
                            m = tt(yT[at, :, i * 8:i * 8 + 8], ps[at, bank, 0:32].rearrange("p (a r t) -> p a r t", a=2, r=2)[:, :, par, :],
                                   prec[at].rearrange("p (a r t) -> p a r t", a=2, r=2)[:, :, par, :], ALU.mult)
                        m.then_inc(e_fin, 1)

                    for i in range(DEC_BATCH):
                        X = xs[i % 2]
                        dve.wait_ge(e_s, 8 * i + 8)
                        dve.wait_ge(e_psum, 2 * i + 2)
                        if i >= 2:
                            dve.wait_ge(e_p, i - 1)
                        S = ps[:, 2 + i % 2, :].rearrange("p (k h t) -> p (k h) t", h=HEADS, t=DEC_SEQ)
                        tt(X[:, 0:KPP, :].rearrange("p k (h t) -> p (k h) t", t=DEC_SEQ), S, b3(sfx[:, i].rearrange("p k h -> p (k h)"), DEC_SEQ), ALU.add)
                        link(tt(X[0:NS, KPP, :], ps[0:NS, 5, (i % 2) * 32:(i % 2) * 32 + 32], newb[0:NS, i].rearrange("p h t -> p (h t)"), ALU.add))
                        V.tensor_reduce(pmax, X.rearrange("p k c -> p c k"), AX.X, ALU.max).then_inc(e_pm, 1)
                        if i > 0:
                            e_finish(i - 1)
                        dve.wait_ge(e_mt, i + 1)
                        link(V.tensor_reduce(pcol[0:32, 0:1], ps[0:32, 6, 0:P], AX.X, ALU.max))
                        V.tensor_scalar(pdiag[0:32], T("ident", 32)[:, 0:32], pcol[0:32, 0:1], None, ALU.mult).then_inc(e_dg, 1)
                        dve.wait_ge(e_bc, i + 1)
                        link(V.tensor_copy(pmax, ps[:, 6, P:P + 32]))
                        tt(X, X, rep(pmax, NK), ALU.subtract).then_inc(e_xs, 1)
                        dve.wait_ge(e_p, i + 1)
                        V.tensor_reduce(ptot, pp[i % 2].rearrange("p k c -> p c k"), AX.X, ALU.add).then_inc(e_lf, 1)
                    e_finish(DEC_BATCH - 1)
                    dve.wait_ge(e_yT, 1)
                    link(V.tensor_copy(Z(NP, "d_q", NS), ps[0:NS, 0, 0:GW]))

                    dve.wait_ge(sigm_done, 1)
                    link(tt(Zall("c_q"), Zall("c_q"), Zall("c_o"), ALU.mult))
                    for name in MERGED:
                        y = v4(Zall(name))
                        link(tt(v4(tmp_a), y, y, ALU.mult))
                        V.tensor_reduce(th(s_sum), v4(tmp_a), AX.X, ALU.add).then_inc(rms_s, 1)
                        dve.wait_ge(rms_r, due(rms_r))
                        link(tt(y, y, over_e(th(s_rstd)), ALU.mult))
                        if name == "b_q":
                            dve.wait_ge(silu_done, 1)
                            link(tt(Zall("b_q"), Zall("b_q"), Zall("b_g"), ALU.mult))
                    V.memset(pcol, 0.0).then_inc(merged, 1)
                    for i in range(2 * NT):
                        t, hf = i // 2, i % 2
                        n = rows[t]
                        dve.wait_ge(m_ps, i + 1)
                        tt(xTv[:, 4 * hf:4 * hf + 4, t * P:t * P + n], ps[:, 4 + i % 4, 0:4 * n].rearrange("p (k n) -> p k n", k=4),
                           b3(gmix[:, 4 * hf:4 * hf + 4], n), ALU.mult).then_inc(m_sb, 1)

                    def layer_norm(t, gcol_, src):
                        n = rows[t]
                        X = src[0:n, t, :]
                        for hf in range(2):
                            m = V.bn_stats(lnst[0:n, 6 * hf:6 * hf + 6], X[:, hf * 512:hf * 512 + 512])
                        link(m)
                        link(V.bn_aggr(lnmv[0:n, :], lnst[0:n, :]), o_var)
                        dve.wait_ge(o_rstd, due(o_rstd))
                        link(V.tensor_scalar(X, X, lnmv[0:n, 0:1], lnr[0:n, 0:1], ALU.subtract, ALU.mult))
                        g = gcol_ * D_MODEL
                        link(tt(X, X, vbuf[0:n, g:g + D_MODEL], ALU.mult))
                        link(tt(x[0:n, t, :], X, vbuf[0:n, g + D_MODEL:g + 2 * D_MODEL], ALU.add), ln_n)

                    dve.wait_ge(ln_par, 64)
                    for t in tiles:
                        n = rows[t]
                        dve.wait_ge(o_ps, t + 1)
                        bank = 2 * (t % 2)
                        link(V.scalar_tensor_tensor(x[0:n, t, :].rearrange("p (a b) -> p a b", a=2), x[0:n, t, :].rearrange("p (a b) -> p a b", a=2), ALPHA,
                                                    ps[0:n, bank:bank + 2, :], ALU.mult, ALU.add), y_free)
                        layer_norm(t, 0, x)

                    dve.wait_ge(r_w, 16 * 7)
                    V.memset(rt[:, :, :], 0.0)
                    dve.wait_ge(r_ps, 1)
                    link(V.memset(moe_small, 0.0))
                    NR = GROUPS + EXPERTS
                    tt(rt[:, 0:NP, :], ps[:, 0, 0:NP * NR].rearrange("p (t c) -> p t c", t=NP), rep(br, NP), ALU.add)
                    link(tt(rt[0:NS, NP, :], ps[0:NS, 0, NP * NR:NT * NR], br[0:NS], ALU.add))

                    def first_max(v, vmax, hot):
                        link(V.tensor_reduce(vmax, v, AX.X, ALU.max))
                        link(tt(hot, v, over(vmax), ALU.is_equal))
                        link(tt(hot, hot, rank, ALU.mult))
                        link(V.tensor_reduce(r_m, hot, AX.X, ALU.max))
                        link(tt(hot, hot, over(r_m), ALU.is_equal))

                    def over(v):
                        return b3(v, 4)

                    rank = rep(T("rank"), NT)
                    g_l = rt[:, :, 0:GROUPS]
                    first_max(g_l, r_gm, r_goh)
                    link(tt(r_gd, g_l, over(r_gm), ALU.subtract), r_lg)
                    e_l = rt[:, :, GROUPS:].rearrange("p t (g e) -> p t g e", g=GROUPS)
                    link(tt(r_t16, e_l, r_goh.unsqueeze(3).to_broadcast([P, NT, GROUPS, 4]), ALU.mult))
                    link(V.tensor_reduce(r_el, r_t16.rearrange("p t g e -> p t e g"), AX.X, ALU.add))
                    first_max(r_el, r_v1, r_oh1)
                    link(V.scalar_tensor_tensor(r_e2l, r_oh1, NEG, r_el, ALU.mult, ALU.add))
                    first_max(r_e2l, r_v2, r_oh2)
                    link(tt(r_vd, r_v2, r_v1, ALU.subtract), r_e2)
                    dve.wait_ge(r_exp, 1)
                    link(V.tensor_reduce(r_gw, r_ge, AX.X, ALU.add))
                    link(V.reciprocal(r_gw, r_gw))
                    dve.wait_ge(r_e2x, 1)
                    link(V.tensor_scalar(r_w1, r_ex, 1.0, None, ALU.add))
                    link(V.reciprocal(r_w1, r_w1))
                    link(tt(r_w1, r_w1, r_gw, ALU.mult))
                    link(tt(r_w2, r_w1, r_ex, ALU.mult))
                    for hot, oh in zip(r_hot, (r_oh1, r_oh2)):
                        m = tt(hot.rearrange("p t (g e) -> p t g e", g=GROUPS), r_goh.unsqueeze(3).to_broadcast([P, NT, GROUPS, 4]),
                               oh.unsqueeze(2).to_broadcast([P, NT, GROUPS, 4]), ALU.mult)
                    link(m)
                    link(tt(r_pick, r_hot[0], r_hot[1], ALU.add), r_picked)
                    dve.wait_ge(r_pos_ps, 1)
                    V.memset(r_pos[:, NP:NT, :], 0.0)
                    V.tensor_copy(r_pos[:, 0:NP, :], ps[:, 1, 0:NP * EXPERTS].rearrange("p (t e) -> p t e", t=NP))
                    link(V.tensor_copy(r_tot, ps[:, 1, NT * EXPERTS:(NT + 1) * EXPERTS]))
                    V.tensor_copy(r_pos[0:NS, NP, :], ps[0:NS, 1, NP * EXPERTS:NT * EXPERTS])
                    link(V.tensor_scalar(r_nb, r_tot, float(BLOCK), None, ALU.is_gt))
                    for c in range(2, MORE_PER_EXPERT + 1):
                        link(V.scalar_tensor_tensor(r_nb, r_tot, float(c * BLOCK), r_nb, ALU.is_gt, ALU.add))
                    link(V.tensor_tensor_scan(r_cum, T("ones")[:, 0:EXPERTS], r_nb, 0.0, ALU.mult, ALU.add))
                    V.tensor_copy(r_plan[:, 0:EXPERTS], T("experts"))
                    link(tt(r_owner3, rep(r_cum, MORE), b3(T("count"), EXPERTS), ALU.is_le))
                    link(V.tensor_reduce(r_plan[:, EXPERTS:N_BLOCKS], r_owner3, AX.X, ALU.add))
                    V.tensor_scalar(r_plan[:, EXPERTS:N_BLOCKS], r_plan[:, EXPERTS:N_BLOCKS], float(EXPERTS - 1), None, ALU.min)
                    link(tt(r_even, r_cum[:, EXPERTS - 1:EXPERTS].to_broadcast([P, MORE // 2]), T("count")[:, 0:MORE:2], ALU.is_gt))
                    link(V.tensor_reduce(r_plan[:, N_BLOCKS:], r_even, AX.X, ALU.add))
                    link(V.tensor_scalar(r_plan[:, N_BLOCKS:], r_plan[:, N_BLOCKS:], float(EXPERTS // 2 - 1), None, ALU.add))
                    V.tensor_copy(plan[:, :], r_plan[0:1, :])
                    link(tt(r_more, r_cum, r_nb, ALU.subtract))
                    link(V.scalar_tensor_tensor(r_more, r_more, float(BLOCK), T("more_row"), ALU.mult, ALU.add))
                    link(V.scalar_tensor_tensor(r_row, r_pos, float(BLOCK), rep(r_more, NT), ALU.is_ge, ALU.mult))
                    link(tt(r_row, r_row, r_pos, ALU.add))
                    link(tt(r_row, r_row, rep(T("first_row"), NT), ALU.add))
                    for c in range(TOP_K):
                        link(tt(r_hot[c], r_hot[c], r_row, ALU.mult))
                        link(V.tensor_reduce(r_rowf[:, :, c:c + 1], r_hot[c], AX.X, ALU.add))
                    V.tensor_copy(rows_u[:, :, :], r_rowf).then_inc(planned, 1)
                    dve.wait_ge(planned, 1)
                    last_pair = dve.value_load(plan[0:1, N_BLOCKS:N_BLOCKS + 1], min_val=EXPERTS // 2 - 1, max_val=N_BLOCKS // 2 - 1)

                    def dve_block(k, i, s):
                        dve.wait_ge(sil_sb, k + 1)
                        tt(hT[s].rearrange("p a n -> p (a n)"), sil[s], ps[:, 2 + s, 2 * BLOCK:], ALU.mult).then_inc(hT_sb, 1)
                        dve.wait_ge(y_ps, k + 1)
                        dve.wait_ge((y_out0, y_out1)[s], i * 16 + 16)
                        V.tensor_copy(yo[s][:, 0:SLAB], ps[:, 4 + 2 * s, :]).then_inc(y_sb, 1)

                    dve.sem_inc(y_sb, 3)
                    with dve.Fori(0, last_pair + 1) as i:
                        dve_block(i * 2, i, 0)
                        dve_block(i * 2 + 1, i, 1)
                    for t in tiles:
                        n = rows[t]
                        dve.wait_ge(y_init, t + 1)
                        dve.wait_ge(y_back[t], layer * (16 * TOP_K) + 16 * TOP_K)
                        for c, w in enumerate((r_w1, r_w2)):
                            link(V.scalar_tensor_tensor(x[0:n, t, :], yg[0:n, t, c, :], w[0:n, t:t + 1], x[0:n, t, :], ALU.mult, ALU.add))
                        layer_norm(t, 2, x)

                @block.tensor
                def _(pe):
                    due = Due()
                    mm = nc.tensor.matmul
                    tr = nc.tensor.transpose
                    idn = T("ident")

                    def turn_x(base):
                        for i in range(2 * NT):
                            t, hf = i // 2, i % 2
                            n = rows[t]
                            if base + i >= 4:
                                pe.wait_ge(xT_sb, max(base + i - 3, base))
                            for k in range(4):
                                c = (4 * hf + k) * P
                                m = tr(ps[:, 4 + i % 4, k * n:(k + 1) * n], x[0:n, t, c:c + P], idn[0:n, 0:n])
                            m.then_inc(xT_ps, 1)

                    turn_x(0)
                    pe.wait_ge(xT_sb, 2 * NT)
                    w_slab = (w_slab0, w_slab1, w_slab2)
                    for g in range(N_SLABS):
                        w = min(SLAB, D_IN - g * SLAB)
                        pe.wait_ge(w_slab[g % 3], 16 * (g // 3 + 1))
                        for t in tiles:
                            i, n = g * NT + t, rows[t]
                            if i >= 4:
                                pe.wait_ge(z_sb, i - 3)
                            for k in range(KD):
                                m = mm(ps[0:n, i % 4, 0:w], xTv[:, k, t * P:t * P + n], slab[g % 3][:, k, 0:w], start=(k == 0), stop=(k == KD - 1))
                            m.then_inc(z_ps, 1)
                    pe.wait_ge(ws_n, 16)
                    for h in range(HEADS):
                        m = tr(ps[:, 4, h * P:(h + 1) * P], ws_nat[:, h, :], idn)
                    m.then_inc(ws_ps, 1)
                    pe.wait_ge(ws_s8, 1)
                    for h in range(HEADS):
                        m = tr(ps[0:NS, 5, h * NS:(h + 1) * NS], ws_exp[0:NS, h, :], idn[0:NS, 0:NS])
                    m.then_inc(ws_ps, 1)
                    pe.wait_ge(f_gates, 1)
                    for t in tiles:
                        n = rows[t]
                        m = mm(ps[0:n, 7, t * HEADS:(t + 1) * HEADS], T("upper" if t < NP else "upper_s", n), th(lf)[0:n, t, 0:HEADS], start=True, stop=True)
                    m.then_inc(gate_ps, 1)
                    pe.wait_ge(va_ready, 1)
                    pe.wait_ge(ws_sb, 2)
                    pe.wait_ge(z_sb, NT * N_SLABS)
                    for t in tiles:
                        n = rows[t]
                        for h in range(HEADS):
                            v = COLS["a_v"] + h * HD
                            m = mm(ps[0:n, t if t < NP else 6, h * HD:(h + 1) * HD], (wsT if t < NP else wsTs)[0:n, h, 0:n], zt[0:n, t, v:v + HD], start=True, stop=True)
                    m.then_inc(a_ps, 1)

                    def turn_qk(t, q, k, bank, sem):
                        n = rows[t]
                        for a, name in enumerate((q, q, k, k)):
                            c = COLS[name] + a % 2 * P
                            m = tr(ps[:, bank, a * n:(a + 1) * n], zt[0:n, t, c:c + P], idn[0:n, 0:n])
                        m.then_inc(sem, 1)

                    def scores(t, sem):
                        n = rows[t]
                        for pair in range(PAIRS):
                            for par in range(2):
                                at = slice(par * HD, (par + 1) * HD)
                                m = mm(ps[0:n, 6 + par, pair * n:(pair + 1) * n], qkT[at, 2 + pair, 0:n], qkT[at, pair, 0:n], start=True, stop=True)
                        m.then_inc(sem, 1)

                    def sample_queries():
                        pe.wait_ge(qm_q, due(qm_q))
                        for h in range(HEADS):
                            m = tr(ps[:, 4, h * NS:(h + 1) * NS], qd2[0:NS, h, :], idn[0:NS, 0:NS])
                        m.then_inc(qm_ps, 1)

                    def mixed(t, state, sstate, w, val, sem):
                        n = rows[t]
                        for h in range(HEADS):
                            m = mm(ps[0:n, 0, h * w:(h + 1) * w], sw[0:n, h % 2 * 2 + h // 2, 0:n], val(h), start=True, stop=True)
                        if t < NP:
                            for pair in range(PAIRS):
                                for par in range(2):
                                    at = slice(par * HD, (par + 1) * HD)
                                    m = mm(ps[0:n, 1 + par, pair * w:(pair + 1) * w], qkT[at, pair, 0:n], state[at, pair, :], start=True, stop=True)
                        else:
                            pe.wait_ge(qm_sb, due(qm_sb))
                            pe.wait_ge(s_in, 16 * 3 * DEC_BATCH)
                            for h in range(HEADS):
                                for bp in range(BP):
                                    m = mm(ps[0:n, 1, h * w:(h + 1) * w], qm[:, bp, h, :], sstate[:, bp, h, :], start=(bp == 0), stop=(bp == BP - 1))
                        m.then_inc(sem, 1)

                    def sample_update(w, val, place):
                        for h in range(HEADS):
                            pe.wait_ge(km_sb, due(km_sb))
                            for bp in range(BP):
                                m = mm(place(bp, h), km[0:NS, 2 * bp:2 * bp + 2, :].rearrange("p a b -> p (a b)"), val(h), start=True, stop=True)
                            m.then_inc(km_used, 1)

                    pe.wait_ge(rope_done, 1)
                    pe.wait_ge(gate_sb, 1)
                    for t in tiles:
                        n = rows[t]
                        turn_qk(t, "b_q", "b_k", 5, b_T)
                        pe.wait_ge(b_Tsb, 2 * t + 2)
                        scores(t, b_sc)
                        if t == NP:
                            sample_queries()
                        val = lambda h: zt[0:n, t, COLS["b_v"] + h * HD:COLS["b_v"] + (h + 1) * HD]
                        pe.wait_ge(b_sw, t + 1)
                        if t > 0:
                            pe.wait_ge(b_state, t)
                        mixed(t, ret, rs, HD, val, b_out)
                        pe.wait_ge(b_kd, t + 1)
                        if t < NP:
                            for pair in range(PAIRS):
                                c = COLS["b_v"] + pair * P
                                m = mm(ps[:, 3, pair * P:(pair + 1) * P], kd[:, pair * P:(pair + 1) * P], zt[:, t, c:c + P], start=True, stop=True)
                            m.then_inc(b_up, 1)
                        else:
                            sample_update(HD, val, lambda bp, h: ps[:, 2 + bp // 2, (bp % 2 * HEADS + h) * HD:(bp % 2 * HEADS + h + 1) * HD])
                    pe.wait_ge(b_state, NT)
                    for t in tiles:
                        n = rows[t]
                        W = HD + 1
                        turn_qk(t, "c_q", "c_k", 5, c_T)
                        pe.wait_ge(c_dg, t + 1)
                        m = mm(ps[0:n, 3, 0:HEADS * n], T("ones", n)[:, 0:n], diag[0:n, :, 0:n], start=True, stop=True)
                        m.then_inc(c_row, 1)
                        pe.wait_ge(c_Tsb, 2 * t + 2)
                        scores(t, c_sc)
                        if t == NP:
                            sample_queries()
                        pe.wait_ge(c_mt, t + 1)
                        mm(ps[0:n, 3, 0:2 * HEADS], T("last" if t < NP else "last_s", n), mtb[0:n, :], start=True, stop=True).then_inc(c_last, 1)
                        val = lambda h: vx[0:n, h, :]
                        pe.wait_ge(c_sw, t + 1)
                        pe.wait_ge(c_vx, t + 1)
                        if t > 0:
                            pe.wait_ge(c_cd, t)
                        mixed(t, mem, cs, W, val, c_out)
                        pe.wait_ge(c_kd, t + 1)
                        if t < NP:
                            for pair in range(PAIRS):
                                m = mm(ps[:, 3, pair * 2 * W:(pair + 1) * 2 * W], kd[:, pair * P:(pair + 1) * P],
                                       vx[:, 2 * pair:2 * pair + 2, :].rearrange("p a b -> p (a b)"), start=True, stop=True)
                            m.then_inc(c_up, 1)
                        else:
                            sample_update(W, val, lambda bp, h: ps[:, (2, 3, 5, 6)[bp], h * W:(h + 1) * W])
                            for bp in range(BP):
                                m = mm(ps[:, 7, bp * HEADS:(bp + 1) * HEADS], T("last_of", NS)[:, bp * P:(bp + 1) * P], ge[0:NS, HEADS:], start=True, stop=True)
                            m.then_inc(c_up, 1)
                    pe.wait_ge(c_cd, NT)
                    for t in tiles:
                        n = rows[t]
                        lfd = lambda c: th(lf)[0:n, c, HEADS:]
                        for c in range(t if t < NP else 0):
                            mm(ps[0:n, 2, t * HEADS:(t + 1) * HEADS], T("ones"), lfd(c), start=(c == 0), stop=False)
                        m = mm(ps[0:n, 2, t * HEADS:(t + 1) * HEADS], T("upper" if t < NP else "upper_s", n), lfd(t), start=(t in (0, NP)), stop=True)
                    m.then_inc(d_cum, 1)
                    for t in range(NP):
                        if t >= 2:
                            pe.wait_ge(d_Tsb, 2 * t - 2)
                        turn_qk(t, "d_q", "d_k", t % 2, d_T)
                    for h in range(HEADS):
                        pe.wait_ge(d_dg, h + 1)
                        if h >= 2:
                            pe.wait_ge(d_ncr, h - 1)
                        mm(ps[:, 3 + h % 2, :], T("ones"), dg[h % 2].rearrange("p a b -> p (a b)"), start=True, stop=True).then_inc(d_row, 1)
                    pe.wait_ge(d_Tsb, 2 * NP)

                    def logits(m_):
                        c, h = m_ // HEADS, m_ % HEADS
                        w = (c + 1) * P
                        at = slice(h % 2 * HD, (h % 2 + 1) * HD)
                        pe.wait_ge(d_lgx, m_ - 1) if m_ >= 2 else None
                        mm(ps[:, 2 + m_ % 2, 0:w], qTa[at, h // 2, c * P:(c + 1) * P], kTa[at, h // 2, 0:w], start=True, stop=False)
                        mm(ps[:, 2 + m_ % 2, c * P:w], idn, T("neg_q"), start=False, stop=True).then_inc(d_lg, 1)

                    def values(m_):
                        c, h = m_ // HEADS, m_ % HEADS
                        pe.wait_ge(d_pTsb, m_ + 1)
                        if c >= 2 and h == 0:
                            pe.wait_ge(d_y, c - 1)
                        v = COLS["d_v"] + h * HD
                        for s in range(c + 1):
                            m = mm(ps[:, 6 + c % 2, h * HD:(h + 1) * HD], pT[m_ % 2][:, s, :], zt[:, s, v:v + HD], start=(s == 0), stop=(s == c))
                        m.then_inc(d_o, 1)

                    pe.wait_ge(d_ncr, HEADS)
                    for m_ in range(NP * HEADS + 2):
                        if m_ < NP * HEADS:
                            logits(m_)
                        if 1 <= m_ <= NP * HEADS:
                            pe.wait_ge(d_exp, m_)
                            for s in range((m_ - 1) // HEADS + 1):
                                m = tr(ps[:, 4 + (m_ - 1) % 2, s * P:(s + 1) * P], lg[(m_ - 1) % 2][:, s * P:(s + 1) * P], idn)
                            m.then_inc(d_pT, 1)
                        if m_ >= 2:
                            values(m_ - 2)
                    pe.wait_ge(d_y, NP)
                    turn_qk(NP, "d_q", "d_k", 0, e_T)
                    pe.wait_ge(e_tot, 1)
                    mm(ps[:, 7, 0:DEC_BATCH * HEADS], T("after"), sufp, start=True, stop=True).then_inc(e_cumps, 1)
                    pe.wait_ge(e_Tsb, 3)
                    kv = kbuf[:, :].rearrange("p (k c) -> p k c", k=KPP)
                    vv = vbuf[:, :].rearrange("p (k c) -> p k c", k=KPP)

                    def cache_scores(i, g):
                        m_ = 8 * i + g
                        pe.wait_ge(e_ksb, m_ + 1)
                        if g == 0 and i >= 2:
                            pe.wait_ge(e_pm, i - 1)
                        for a in range(4):
                            k, pair = 2 * g + a // 2, a % 2
                            c = k * 32 + pair * 16
                            m = mm(ps[:, 2 + i % 2, c:c + 16], kTs[m_ % 2][:, a, :], qbd[:, pair, i, :], start=True, stop=True)
                        m.then_inc(e_s, 1)

                    for i in range(DEC_BATCH + 1):
                        j = i - 1
                        if i < DEC_BATCH:
                            pe.wait_ge(k_in, layer * (16 * DEC_BATCH) + 16 * (i + 1))
                        for g in range(8):
                            if i < DEC_BATCH:
                                m_ = 8 * i + g
                                if m_ >= 2:
                                    pe.wait_ge(e_ksb, m_ - 1)
                                for a in range(4):
                                    m = tr(ps[:, m_ % 2, a * P:(a + 1) * P], kv[:, 2 * g + a // 2, a % 2 * P:(a % 2 + 1) * P], idn)
                                m.then_inc(e_kps, 1)
                                if g > 0:
                                    cache_scores(i, g - 1)
                            if j >= 0 and g == 1:
                                pe.wait_ge(e_pm, j + 1)
                                tr(ps[0:32, 6, 0:P], pmax, idn).then_inc(e_mt, 1)
                            if j >= 0 and g == 4:
                                pe.wait_ge(e_dg, j + 1)
                                mm(ps[:, 6, P:P + 32], T("ones", 32), pdiag[0:32], start=True, stop=True).then_inc(e_bc, 1)
                        if i < DEC_BATCH:
                            cache_scores(i, 7)
                            if i > 0:
                                pe.wait_ge(e_pm, i)
                            for pair in range(PAIRS):
                                c = i % 2 * 32 + pair * 16
                                mm(ps[0:NS, 5, c:c + 16], kTn[:, pair, :], qbd[:, pair, i, :], start=True, stop=True).then_inc(e_psum, 1)
                        if j >= 0:
                            bank = 4 if j % 2 else 7
                            pe.wait_ge(v_in, layer * (16 * DEC_BATCH) + 16 * (j + 1))
                            pe.wait_ge(e_p, j + 1)
                            if j >= 2:
                                pe.wait_ge(e_fin, j - 1)
                            for pair in range(PAIRS):
                                c = COLS["d_v"] + pair * P
                                for k in range(KPP):
                                    mm(ps[:, bank, pair * 16:pair * 16 + 16], vv[:, k, pair * P:(pair + 1) * P], pp[j % 2][:, k, pair * 16:pair * 16 + 16],
                                       start=(k == 0), stop=False)
                                mm(ps[:, bank, pair * 16:pair * 16 + 16], zt[0:NS, NP, c:c + P], pp[j % 2][0:NS, KPP, pair * 16:pair * 16 + 16],
                                   start=False, stop=True)
                            pe.wait_ge(e_lf, j + 1)
                            mm(ps[:, bank, 64:96], T("ones"), ptot, start=True, stop=True).then_inc(e_pv, 1)
                    pe.wait_ge(e_fin, DEC_BATCH)
                    for pair in range(PAIRS):
                        m = tr(ps[0:NS, 0, pair * P:(pair + 1) * P], yT[:, pair, :], idn)
                    m.then_inc(e_yT, 1)
                    pe.wait_ge(merged, 1)
                    for i in range(2 * NT):
                        t, hf = i // 2, i % 2
                        n = rows[t]
                        if i >= 4:
                            pe.wait_ge(m_sb, i - 3)
                        for k in range(4):
                            kk = 4 * hf + k
                            c = COLS[MERGED[kk // 2]] + kk % 2 * P
                            m = tr(ps[:, 4 + i % 4, k * n:(k + 1) * n], zt[0:n, t, c:c + P], idn[0:n, 0:n])
                        m.then_inc(m_ps, 1)
                    pe.wait_ge(m_sb, 2 * NT)
                    pe.wait_ge(wout_in, 32)
                    for t in tiles:
                        n = rows[t]
                        bank = 2 * (t % 2)
                        if t >= 2:
                            pe.wait_ge(y_free, t - 1)
                        for hf in range(2):
                            for k in range(KD):
                                m = mm(ps[0:n, bank + hf, :], xTv[:, k, t * P:t * P + n], slab[hf][:, k, :], start=(k == 0), stop=(k == KD - 1))
                        m.then_inc(o_ps, 1)
                    pe.wait_ge(ln_n, NT)
                    turn_x(2 * NT)
                    pe.wait_ge(xT_sb, 4 * NT)
                    pe.wait_ge(r_w, 16 * 7)
                    NR = GROUPS + EXPERTS
                    for t in tiles:
                        n = rows[t]
                        for k in range(KD):
                            m = mm(ps[0:n, 0, t * NR:(t + 1) * NR], xTv[:, k, t * P:t * P + n], wr[:, k, :], start=(k == 0), stop=(k == KD - 1))
                    m.then_inc(r_ps, 1)

                    pe.wait_ge(r_picked, 1)
                    for t in tiles:
                        n = rows[t]
                        out = ps[0:n, 1, t * EXPERTS:(t + 1) * EXPERTS]
                        for c in range(t):
                            mm(out, T("ones")[:, 0:n], r_pick[:, c, :], start=(c == 0), stop=False)
                        mm(out, T("before", n)[:, 0:n], r_pick[0:n, t, :], start=(t == 0), stop=True)
                    for t in tiles:
                        m = mm(ps[:, 1, NT * EXPERTS:(NT + 1) * EXPERTS], T("ones", rows[t]), r_pick[0:rows[t], t, :], start=(t == 0), stop=(t == NP))
                    m.then_inc(r_pos_ps, 1)
                    pe.wait_ge(planned, 1)
                    last_pair = pe.value_load(plan[0:1, N_BLOCKS:N_BLOCKS + 1], min_val=EXPERTS // 2 - 1, max_val=N_BLOCKS // 2 - 1)

                    def pe_turn(i, s):
                        pe.wait_ge((xg_in0, xg_in1)[s], i * 16 + 16)
                        for hf in range(2):
                            for k in range(4):
                                m = tr(ps[:, hf, k * P:(k + 1) * P], xg[s][:, 4 * hf + k::KD], idn)
                            m.then_inc(xgT_ps, 1)

                    def pe_h(i, k, s):
                        pe.wait_ge((w13_in0, w13_in1)[s], i * 32 + 32)
                        pe.wait_ge(xgT_sb, k * 2 + 2)
                        for w in range(2):
                            for c in range(2):
                                at = (2 * w + c) * BLOCK
                                for q in range(KD):
                                    m = mm(ps[:, 2 + s, at:at + BLOCK], w13[s][:, w, q, c::2], xgT[s][:, q, :], start=(q == 0), stop=(q == KD - 1))
                        m.then_inc(h_ps, 1)

                    def pe_y(i, k, s):
                        pe.wait_ge((w2_in0, w2_in1)[s], i * 16 + 16)
                        pe.wait_ge(hT_sb, k + 1)
                        pe.wait_ge(y_sb, k * 2 + 1)
                        for hf in range(2):
                            for c in range(2):
                                m = mm(ps[:, 4 + 2 * s + hf, :], hT[s][:, c, :], w2[s][:, c, hf * SLAB:(hf + 1) * SLAB], start=(c == 0), stop=(c == 1))
                        m.then_inc(y_ps, 1)

                    pe.wait_ge(y_free, NT)
                    pe_turn(0, 0)
                    with pe.Fori(0, last_pair) as i:
                        pe_h(i, i * 2, 0)
                        pe_turn(i, 1)
                        pe_y(i, i * 2, 0)
                        pe_h(i, i * 2 + 1, 1)
                        pe_turn(i + 1, 0)
                        pe_y(i, i * 2 + 1, 1)
                    lp = last_pair
                    pe_h(lp, lp * 2, 0)
                    pe_turn(lp, 1)
                    pe_y(lp, lp * 2, 0)
                    pe_h(lp, lp * 2 + 1, 1)
                    pe_y(lp, lp * 2 + 1, 1)

            nc.all_engine_barrier()
            nc.sync.sem_clear(range(signals[0].num, signals[-1].num + 1))
            nc.all_engine_barrier()

        with nc.Block() as block:
            @block.sync
            def _(sp):
                sp.dma_start(d["y_prompt"].rearrange("o (t p) n -> p (o t) n", p=P), x[:, 0:NP, :]).then_inc(s_x0, 16)
                sp.dma_start(d["y_sample"].rearrange("b s n -> (b s) n"), x[0:NS, NP, :]).then_inc(s_x0, 16)
                sp.wait_ge(s_x0, 64)

_INS = ["x_prompt", "x_sample", "cache_k", "cache_v", "cache_logf", "page_table", "state_ret", "state_mlstm_c",
        "state_mlstm_n", "state_mlstm_m", "w_in", "b_in", "w_s", "b_s", "g_mix", "w_out", "ln1_g", "ln1_b",
        "w_rg", "b_rg", "w_re", "b_re", "w1", "w3", "w2", "ln2_g", "ln2_b"]
_KV = (HEADS, HD)
_OUTS = [("y_prompt", (1, SEQ, D_MODEL)), ("y_sample", (DEC_BATCH, DEC_SEQ, D_MODEL)),
         ("k_prompt", (DEPTH, 1, SEQ) + _KV), ("v_prompt", (DEPTH, 1, SEQ) + _KV), ("logf_prompt", (DEPTH, 1, SEQ, HEADS)),
         ("ret_prompt", (DEPTH, 1, HEADS, HD, HD)), ("mlstm_c_prompt", (DEPTH, 1, HEADS, HD, HD)),
         ("mlstm_n_prompt", (DEPTH, 1, HEADS, HD)), ("mlstm_m_prompt", (DEPTH, 1, HEADS)),
         ("k_sample", (DEPTH, DEC_BATCH, DEC_SEQ) + _KV), ("v_sample", (DEPTH, DEC_BATCH, DEC_SEQ) + _KV),
         ("logf_sample", (DEPTH, DEC_BATCH, DEC_SEQ, HEADS)),
         ("ret_sample", (DEPTH, DEC_BATCH, HEADS, HD, HD)), ("mlstm_c_sample", (DEPTH, DEC_BATCH, HEADS, HD, HD)),
         ("mlstm_n_sample", (DEPTH, DEC_BATCH, HEADS, HD)), ("mlstm_m_sample", (DEPTH, DEC_BATCH, HEADS)),
         ("chunk_v_sample", (DEPTH, DEC_BATCH, DEC_SEQ) + _KV)]

def kernel(**inputs):
    import concourse.bacc as _bacc
    from concourse.bass_utils import run_bass_kernel_spmd as _run

    nc = _bacc.Bacc("TRN2", target_bir_lowering=False, num_devices=1)
    arrays, d = {}, {}
    for name in _INS + ["tables"]:
        a = np.ascontiguousarray(TABLES if name == "tables" else inputs[name])
        if name in ("w1", "w3", "w2"):
            a = a.reshape((DEPTH * EXPERTS,) + a.shape[2:])
        arrays["in_" + name] = a
        d[name] = nc.dram_tensor("in_" + name, a.shape, mybir.dt.from_np(a.dtype), kind="ExternalInput").ap()
    for name, shape in _OUTS:
        d[name] = nc.dram_tensor("out_" + name, shape, F32, kind="ExternalOutput").ap()
    decoder(nc, d)
    r = _run(nc, [arrays], core_ids=[0])
    return tuple(r.results[0]["out_" + name] for name, _ in _OUTS)
```

```python
import numpy as np
from contextlib import ExitStack

import concourse.bass as bass
from concourse import mybir
from concourse.alu_op_type import AluOpType as ALU

F32 = mybir.dt.float32
U32 = mybir.dt.uint32
I32 = mybir.dt.int32
ACT = mybir.ActivationFunctionType
AX = mybir.AxisListType

P = 128
D_MODEL = 1024
SEQ = 512
DEPTH = 2
DEC_BATCH = 8
DEC_SEQ = 8
PAST_LEN = 2048
PAGE_SIZE = 128
N_PAGES = PAST_LEN // PAGE_SIZE
N_POOL = (5 * DEC_BATCH * N_PAGES) // 4
HEADS = 4
HD = 64
GW = HEADS * HD
PAIRS = HEADS // 2
EXPERTS = 16
GROUPS = 4
D_EXPERT = D_MODEL // 4
ALPHA = (2 * DEPTH) ** 0.25
LN_EPS = 1e-5
RMS_EPS = 1e-6
SCALE = HD ** -0.5
KD = D_MODEL // P
NT = SEQ // P + 1
NP = NT - 1
NS = DEC_BATCH * DEC_SEQ
TOK = SEQ + NS
TOP_K = 2
BLOCK = P
MORE = TOP_K * TOK // (BLOCK + 1)
MORE_PER_EXPERT = -(-TOK // BLOCK) - 1
N_BLOCKS = EXPERTS + MORE
assert MORE % 2 == 0
KPP = PAST_LEN // P
RPP = PAGE_SIZE // KPP
BP = DEC_BATCH // 2
NEG = -1e30
RESET = -3e38

COLS, _at = {}, 0
for _name, _w in (("a_u", GW), ("a_v", GW), ("b_q", GW), ("b_k", GW), ("b_v", GW), ("b_g", GW),
                  ("c_q", GW), ("c_k", GW), ("c_v", GW), ("c_o", GW), ("c_i", HEADS), ("c_f", HEADS),
                  ("d_q", GW), ("d_k", GW), ("d_v", GW), ("d_f", HEADS)):
    COLS[_name] = _at
    _at += _w
D_IN = _at
SLAB = 512
N_SLABS = -(-D_IN // SLAB)
MERGED = ("a_u", "b_q", "c_q", "d_q")

def make_tables():
    f = np.float32
    parts = []
    i = np.arange(P)
    s, t = i[:, None], i[None, :]
    log_g = np.log1p(-np.exp2(-5.0 - np.arange(HEADS)))
    j = np.arange(NS)
    block, step = j // DEC_SEQ, j % DEC_SEQ
    same = block[:, None] == block[None, :]
    up_s = same & (j[:, None] <= j[None, :])

    def put(name, a):
        a = np.asarray(a, np.float64)
        a = a.reshape(a.shape[0], -1)
        full = np.zeros((P, a.shape[1]), f)
        full[:a.shape[0]] = a.astype(f)
        parts.append((name, full))

    put("ident", np.eye(P))
    put("ones", np.ones((P, P)))
    put("upper", s <= t)
    put("after", s > t)
    put("neg_t", np.where(s <= t, 0.0, NEG))
    put("neg_q", np.where(t <= s, 0.0, NEG))
    put("last", np.repeat((i == P - 1)[:, None], P, 1))
    dec = np.where(s <= t, np.exp(log_g[:, None, None] * np.maximum(t - s, 0)), 0.0)
    by_parity = [2 * pair + par for par in range(2) for pair in range(PAIRS)]
    put("dec", dec[by_parity].transpose(1, 0, 2))
    reset = np.zeros((P, HEADS, P))
    reset[:, :, 0] = RESET
    put("reset", reset)
    put("upper_s", up_s)
    put("lower_s", up_s.T)
    put("neg_ts", np.where(up_s, 0.0, NEG))
    put("last_s", (j[:, None] == 8 * block[None, :] + DEC_SEQ - 1))
    dec_s = np.where(up_s, np.exp(log_g[:, None, None] * np.maximum(j[None, :] - j[:, None], 0)), 0.0)
    put("dec_s", dec_s[by_parity].transpose(1, 0, 2))
    reset = np.zeros((NS, HEADS, NS))
    reset[:, :, ::DEC_SEQ] = RESET
    put("reset_s", reset)
    half = np.repeat(np.arange(2), HD)
    put("last_of", (j[:, None, None] == DEC_SEQ * (2 * np.arange(BP)[:, None] + half) + DEC_SEQ - 1))
    put("seq_of", (2 * np.arange(BP)[:, None] + half[:, None, None] == block))
    put("in_seq", block[:, None] == np.arange(DEC_BATCH))
    n_half = HD // 2
    inv = f(10000.0) ** (-np.arange(n_half, dtype=f) / f(n_half))
    pos = np.zeros((P, NT), f)
    pos[:, :NP] = i[:, None] + P * np.arange(NP)
    pos[:NS, NP] = PAST_LEN + step
    ang = (pos[:, :, None] * inv.astype(f)).astype(f).astype(np.float64)
    put("cos", np.cos(ang))
    put("sin", np.sin(ang))
    put("q_dec", np.exp(log_g[by_parity] * (i[:, None] + 1.0)))
    put("q_dec_s", np.exp(log_g * (step[:, None] + 1.0)))
    put("k_dec", np.exp(log_g * (P - 1.0 - i[:, None])) * SCALE)
    put("k_dec_s", np.exp(log_g * (DEC_SEQ - 1.0 - step[:, None])) * SCALE)
    put("c_dec", np.exp(log_g.reshape(PAIRS, 2).T * P)[half])
    put("c_dec_s", np.tile(np.exp(log_g * DEC_SEQ), (P, 1)))
    put("start", np.where(i[:, None] == 0, 0.0, NEG))
    put("start_s", np.where(step[:, None] == 0, 0.0, NEG))
    put("sub_row", (i % RPP)[:, None])
    hq = np.arange(HEADS * DEC_SEQ)
    put("own_head", (hq[:, None] // DEC_SEQ) == (np.arange(GW)[None, :] // HD))
    put("to_row", np.arange(2 * NS - DEC_SEQ)[None, :] == NS - DEC_SEQ + hq[:, None] % DEC_SEQ)
    put("ln_eps", np.full((P, 1), LN_EPS))
    put("rms_eps", np.full((P, 1), RMS_EPS))
    put("rank", np.tile(np.arange(GROUPS, 0, -1), (P, 1)))
    put("before", s < t)
    e = np.arange(EXPERTS)
    put("first_row", np.tile(e * BLOCK, (P, 1)))
    put("more_row", np.tile(EXPERTS * BLOCK - BLOCK - e * BLOCK, (P, 1)))
    put("count", np.tile(np.arange(MORE), (P, 1)))
    put("experts", np.tile(e, (P, 1)))
    at, cols = 0, {}
    for name, a in parts:
        cols[name] = (at, a.shape[1])
        at += a.shape[1]
    return cols, np.concatenate([a for _, a in parts], 1)

TABLE_COLS, TABLES = make_tables()

class Due:

    def __init__(self):
        self.n = {}

    def __call__(self, sem, k=1):
        self.n[sem.name] = self.n.get(sem.name, 0) + k
        return self.n[sem.name]

def b3(ap, n):
    return ap.unsqueeze(2).to_broadcast([ap.shape[0], ap.shape[1], n])

def rep(ap, n):
    return ap.unsqueeze(1).to_broadcast([ap.shape[0], n, ap.shape[1]])

def decoder(nc, d):
    ctx = ExitStack()
    with ctx:
        def sb(name, shape, dt=F32):
            return ctx.enter_context(nc.sbuf_tensor(name, shape, dt))

        signals = []

        def sig(name):
            s = ctx.enter_context(nc.semaphore(name))
            signals.append(s)
            return s

        tab = sb("tab", [P, TABLES.shape[1]])

        def T(name, n=P):
            at, w = TABLE_COLS[name]
            return tab[0:n, at:at + w]

        x = sb("x", [P, NT, D_MODEL])
        xT = sb("xT", [P, KD * TOK])
        z = sb("z", [P, NT * D_IN])
        ring = sb("ring", [P, 3, KD * SLAB])
        kbuf = sb("kbuf", [P, KPP * GW])
        vbuf = sb("vbuf", [P, KPP * GW])
        wsT = sb("wsT", [P, HEADS, P])
        wsTs = sb("wsTs", [NS, HEADS, NS])
        ws8 = sb("ws8", [NS, HEADS, DEC_SEQ])
        bs = sb("bs", [P, HEADS])
        bss = sb("bss", [NS, HEADS])
        gmix = sb("gmix", [P, KD])
        ret = sb("ret", [P, PAIRS, HD])
        mem = sb("mem", [P, PAIRS, HD + 1])
        small = sb("small", [P, 600])
        idx_f = sb("idx_f", [P, DEC_BATCH])
        idx_u = sb("idx_u", [P, DEC_BATCH], U32)
        pages = sb("pages", [P, DEC_BATCH], I32)

        rows_u = sb("rows_u", [P, NT, TOP_K], U32)
        plan = sb("plan", [1, N_BLOCKS + 1], I32)
        zero = sb("zero", [P, P])
        xd = nc.dram_tensor("expert_in", (N_BLOCKS * BLOCK, D_MODEL), F32, kind="Internal").ap()
        yd = nc.dram_tensor("expert_out", (N_BLOCKS * BLOCK, D_MODEL), F32, kind="Internal").ap()

        ps = ctx.enter_context(nc.psum_tensor("ps", [P, 8, SLAB], F32))

        zt = z[:, :].rearrange("p (t c) -> p t c", t=NT)
        xTv = xT[:, :].rearrange("p (k n) -> p k n", k=KD)

        def Z(t, name, n=P, w=GW):
            c = COLS[name]
            return zt[0:n, t, c:c + w]

        def Zall(name, w=GW):
            c = COLS[name]
            return zt[:, :, c:c + w]

        cut = [0]

        def stat(w):
            cut[0] += w
            assert cut[0] <= 600, cut[0]
            return small[:, cut[0] - w:cut[0]]

        def carve(tensor, start, *dims):
            n = int(np.prod(dims))
            v = tensor[:, start:start + n]
            if len(dims) == 2:
                v = v.rearrange("p (a b) -> p a b", b=dims[1])
            if len(dims) == 3:
                v = v.rearrange("p (a b c) -> p a b c", b=dims[1], c=dims[2])
            return v

        r2 = ring[:, 2, :]
        ws_nat = carve(r2, 0, HEADS, P)
        qkT = carve(r2, 512, 4, P)
        sw = carve(r2, 1024, HEADS, P)
        wexp = carve(r2, 1536, HEADS, P)
        mrow = carve(r2, 2048, HEADS, P)
        diag = carve(r2, 2560, HEADS, P)
        kd = carve(r2, 3072, GW)
        vx = carve(r2, 3328, HEADS, HD + 1)
        mix = carve(r2, 3588, HEADS, HD + 1)
        mrow_flat = mrow.rearrange("p a b -> p (a b)")
        ws_exp = carve(r2, 1024, HEADS, NS)
        tmp_a = carve(xT, 0, NT, GW)
        tmp_b = carve(xT, 1280, NT, GW)
        tmp_c = carve(xT, 2560, NT, GW)
        rs = carve(xT, 0, BP, HEADS, HD)
        cs = carve(xT, 1024, BP, HEADS, HD + 1)
        qm = carve(xT, 2064, BP, HEADS, NS)
        km = carve(xT, 3088, DEC_BATCH, HD)
        qd2 = carve(xT, 3600, HEADS, 2 * HD)
        qTa = carve(xT, 0, PAIRS, SEQ)
        kTa = carve(xT, 1024, PAIRS, SEQ)
        ncr = carve(xT, 2048, HEADS, SEQ)
        pT = [carve(xT, 4096, 4, P), carve(r2, 0, 4, P)]
        lg = [carve(r2, 512, SEQ), carve(r2, 1024, SEQ)]
        dg = [carve(r2, 1536, 4, P), carve(r2, 2048, 4, P)]
        NK = KPP + 1
        HQ = HEADS * DEC_SEQ
        r01 = ring[:, 0:2, :].rearrange("p s c -> p (s c)")
        xs = [carve(r01, i * NK * HQ, NK, HQ) for i in range(2)]
        pp = [carve(r01, (2 + i) * NK * HQ, NK, HQ) for i in range(2)]
        kTs = [carve(r01, 2176 + i * SLAB, SLAB) for i in range(2)]
        srow = [carve(r01, 3200 + i * SLAB, SLAB) for i in range(2)]
        qz = carve(r01, 4224, PAIRS, DEC_BATCH, HQ)
        newb = carve(r01, 4736, DEC_BATCH, HEADS, DEC_SEQ)
        kTn = carve(r01, 4992, PAIRS, NS)
        sfx = carve(r01, 5120, DEC_BATCH, KPP, HEADS)
        lfg = carve(r01, 5632, DEC_BATCH, KPP, HEADS)
        ym = carve(r01, 6144, DEC_BATCH, GW)

        xg = [carve(z, i * 1024, D_MODEL) for i in range(2)]
        xgT = [carve(z, 2048 + i * 1024, KD, BLOCK) for i in range(2)]
        hT = [carve(z, 4096 + i * 256, 2, BLOCK) for i in range(2)]
        sil = [carve(z, 4608 + i * 256, 2 * BLOCK) for i in range(2)]
        yo = [carve(z, 5120 + i * 1024, D_MODEL) for i in range(2)]
        wr = carve(z, 7168, KD, GROUPS + EXPERTS)
        br = carve(z, 7328, GROUPS + EXPERTS)
        rt = carve(z, 7348, NT, GROUPS + EXPERTS)
        yg = carve(z, 0, NT, TOP_K, D_MODEL)
        moe_small = carve(z, 10240, 2000)

        r_at = [0]

        def rview(*dims):
            n = int(np.prod(dims))
            r_at[0] += n
            assert r_at[0] <= 2000
            return carve(moe_small, r_at[0] - n, *dims)

        r_gm, r_gw, r_v1, r_v2, r_vd, r_ex, r_w1, r_w2, r_m = [rview(NT) for _ in range(9)]
        r_goh, r_gd, r_ge, r_el, r_oh1, r_oh2, r_e2l = [rview(NT, 4) for _ in range(7)]
        r_t16 = rview(NT, GROUPS, 4)
        r_hot = [rview(NT, EXPERTS) for _ in range(TOP_K)]
        r_pick = rview(NT, EXPERTS)
        r_pos, r_row = rview(NT, EXPERTS), rview(NT, EXPERTS)
        r_tot, r_nb, r_cum, r_more = [rview(EXPERTS) for _ in range(4)]
        r_owner3 = rview(MORE, EXPERTS)
        r_plan = rview(N_BLOCKS + 1)
        r_even = rview(MORE // 2)
        r_rowf = rview(NT, TOP_K)

        w13 = [ring[:, s, :].rearrange("p (w k f) -> p w k f", w=2, k=KD) for s in range(2)]
        w2 = [ring[:, 2, s * 2048:(s + 1) * 2048].rearrange("p (f n) -> p f n", f=2) for s in range(2)]
        slab = [ring[:, s, :].rearrange("p (k n) -> p k n", k=KD) for s in range(3)]

        CACHE_STEPS = 8 * (DEC_BATCH + 1)
        MT, BC, NEW = 260, 388, 420
        CU = HEADS * (HD + 1)
        rows = [P] * NP + [NS]
        tiles = range(NT)

        s_tab = ctx.enter_context(nc.semaphore("tables_loaded"))
        s_x0 = ctx.enter_context(nc.semaphore("tokens_loaded"))
        s_zero = ctx.enter_context(nc.semaphore("tails_zeroed"))
        s_idx = ctx.enter_context(nc.semaphore("rows_numbered"))
        s_fill = ctx.enter_context(nc.semaphore("expert_in_filled"))
        with nc.Block() as block:
            @block.sync
            def _(sp):
                sp.dma_start(tab[:, :], d["tables"]).then_inc(s_tab, 16)
                for i in range(N_PAGES):
                    sp.dma_start(pages[i * RPP:(i + 1) * RPP, :],
                                 d["page_table"][:, i:i + 1].rearrange("b o -> o b").to_broadcast([RPP, DEC_BATCH]),
                                 allow_slow_non_contiguous=True).then_inc(s_tab, 16)
                sp.dma_start(x[:, 0:NP, :], d["x_prompt"].rearrange("o (t p) n -> p (o t) n", p=P)).then_inc(s_x0, 16)
                sp.dma_start(x[0:NS, NP, :], d["x_sample"].rearrange("b s n -> (b s) n")).then_inc(s_x0, 16)
                sp.wait_ge(s_zero, 1)
                sp.wait_ge(s_x0, 32)

            @block.vector
            def _(dve):
                dve.memset(zero[:, :], 0.0).then_inc(s_zero, 1)
                dve.memset(x[NS:P, NP, :], 0.0)
                dve.memset(zt[NS:P, NP, :], 0.0)
                dve.wait_ge(s_tab, 16 * (1 + N_PAGES))
                dve.tensor_scalar(idx_f[:, :], pages[:, :], float(RPP), T("sub_row"), ALU.mult, ALU.add).then_inc(s_idx, 1)

        xT_ps = sig("xT_ps")
        xT_sb = sig("xT_sb")
        w_slab0 = sig("w_slab0")
        w_slab1 = sig("w_slab1")
        w_slab2 = sig("w_slab2")
        z_ps = sig("z_ps")
        z_sb = sig("z_sb")
        bias_in = sig("bias_in")
        gate_in = sig("gate_in")
        gelu_done = sig("gelu_done")
        silu_done = sig("silu_done")
        sigm_done = sig("sigm_done")
        norm_sum = sig("norm_sum")
        norm_rs = sig("norm_rs")
        va_ready = sig("va_ready")
        ws_ps = sig("ws_ps")
        ws_n = sig("ws_n")
        ws_s8 = sig("ws_s8")
        ws_sb = sig("ws_sb")
        a_ps = sig("a_ps")
        rope_done = sig("rope_done")
        chain_v = sig("chain_v")
        chain_a = sig("chain_a")
        b_T = sig("b_T")
        b_Tsb = sig("b_Tsb")
        b_sc = sig("b_sc")
        b_sw = sig("b_sw")
        b_out = sig("b_out")
        b_kd = sig("b_kd")
        b_up = sig("b_up")
        b_state = sig("b_state")
        s_in = sig("s_in")
        qm_q = sig("qm_q")
        qm_ps = sig("qm_ps")
        qm_sb = sig("qm_sb")
        km_sb = sig("km_sb")
        km_used = sig("km_used")
        idx_set = sig("idx_set")
        f_in = sig("f_in")
        f_exp = sig("f_exp")
        f_gates = sig("f_gates")
        gate_ps = sig("gate_ps")
        gate_sb = sig("gate_sb")
        c_T = sig("c_T")
        c_Tsb = sig("c_Tsb")
        c_dg = sig("c_dg")
        c_row = sig("c_row")
        c_t = sig("c_t")
        c_w = sig("c_w")
        c_exps = sig("c_exps")
        c_mt = sig("c_mt")
        c_last = sig("c_last")
        c_gin = sig("c_gin")
        c_gs = sig("c_gs")
        c_sc = sig("c_sc")
        c_sw = sig("c_sw")
        c_vx = sig("c_vx")
        c_out = sig("c_out")
        c_kd = sig("c_kd")
        c_up = sig("c_up")
        c_cd = sig("c_cd")
        c_free = sig("c_free")
        d_T = sig("d_T")
        d_Tsb = sig("d_Tsb")
        d_cum = sig("d_cum")
        d_dg = sig("d_dg")
        d_row = sig("d_row")
        d_ncr = sig("d_ncr")
        d_lg = sig("d_lg")
        d_lgx = sig("d_lgx")
        d_exp = sig("d_exp")
        d_pT = sig("d_pT")
        d_pTsb = sig("d_pTsb")
        d_o = sig("d_o")
        d_y = sig("d_y")
        e_T = sig("e_T")
        e_Tsb = sig("e_Tsb")
        e_kps = sig("e_kps")
        e_row = sig("e_row")
        e_rsb = sig("e_rsb")
        e_ksb = sig("e_ksb")
        e_s = sig("e_s")
        e_pm = sig("e_pm")
        e_mt = sig("e_mt")
        e_dg = sig("e_dg")
        e_bc = sig("e_bc")
        e_xs = sig("e_xs")
        e_p = sig("e_p")
        e_psum = sig("e_psum")
        e_pv = sig("e_pv")
        e_fin = sig("e_fin")
        e_lf = sig("e_lf")
        e_cumps = sig("e_cumps")
        e_ym = sig("e_ym")
        e_tot = sig("e_tot")
        rms_s = sig("rms_s")
        rms_r = sig("rms_r")
        merged = sig("merged")
        m_ps = sig("m_ps")
        m_sb = sig("m_sb")
        wout_in = sig("wout_in")
        o_ps = sig("o_ps")
        o_var = sig("o_var")
        o_rstd = sig("o_rstd")
        ln_n = sig("ln_n")
        ln_par = sig("ln_par")
        h_ps = sig("h_ps")
        sil_sb = sig("sil_sb")
        y_ps = sig("y_ps")
        w13_in0 = sig("w13_in0")
        w13_in1 = sig("w13_in1")
        w2_in0 = sig("w2_in0")
        w2_in1 = sig("w2_in1")
        r_ps = sig("r_ps")
        r_w = sig("r_w")
        r_exp = sig("r_exp")
        r_lg = sig("r_lg")
        r_e2 = sig("r_e2")
        r_e2x = sig("r_e2x")
        stored = sig("stored")
        stored_in = sig("stored_in")
        y_init = sig("y_init")
        y_free = sig("y_free")
        r_picked = sig("r_picked")
        r_pos_ps = sig("r_pos_ps")
        planned = sig("planned")
        xg_in0 = sig("xg_in0")
        xg_in1 = sig("xg_in1")
        xgT_ps = sig("xgT_ps")
        xgT_sb = sig("xgT_sb")
        hT_sb = sig("hT_sb")
        y_out0 = sig("y_out0")
        y_out1 = sig("y_out1")
        y_sb = sig("y_sb")
        y_stored = sig("y_stored")
        k_in = ctx.enter_context(nc.semaphore("k_gathered"))
        v_in = ctx.enter_context(nc.semaphore("v_gathered"))
        l_in = ctx.enter_context(nc.semaphore("logf_gathered"))
        x_sent = ctx.enter_context(nc.semaphore("tokens_sent"))
        y_back = [ctx.enter_context(nc.semaphore(f"outputs_back{t}")) for t in range(NT)]

        s_sum = stat(NT * HEADS)
        s_rstd = stat(NT * HEADS)
        ff = stat(NT * 2 * HEADS)
        fa = stat(NT * 2 * HEADS)
        fe = stat(NT * 2 * HEADS)
        lf = stat(NT * 2 * HEADS)
        cum = stat(NT * HEADS)
        gi = stat(NT * HEADS)
        ncum = stat(NT * HEADS)
        mp_p = stat(HEADS)
        mp_s = stat(HEADS)
        gp = stat(HEADS)
        mcol = stat(HEADS)
        mtb = stat(2 * HEADS)
        wx = stat(2 * HEADS)
        we = stat(2 * HEADS)
        gx = stat(2 * HEADS)
        ge = stat(2 * HEADS)
        gcol = stat(PAIRS)
        den = stat(HEADS)
        rden = stat(HEADS)
        nmax = stat(NP * HEADS)
        rsum = stat(NP * HEADS)
        drec = stat(NP * HEADS)
        pmax = stat(32)
        pcol = stat(2)
        pdiag = stat(32)
        ptot = stat(32)
        prec = stat(32)
        sufp = stat(DEC_BATCH * HEADS)
        lastv = stat(2 * HEADS)
        lnst = stat(12)
        lnmv = stat(2)
        lnr = stat(2)
        par_pair = "p (a b) -> p b a"

        def v4(ap):
            return ap.rearrange("p t (h e) -> p t h e", h=HEADS)

        def th(ap, a=NT):
            return ap.rearrange("p (t h) -> p t h", t=a)

        def over_e(ap4, n=HD):
            return ap4.unsqueeze(3).to_broadcast([*ap4.shape, n])

        def heads(ap, w=HD):
            return ap.rearrange("p (h e) -> p h e", e=w)

        def by_par(ap):
            return ap.rearrange("p (b a) e -> p a b e", a=2)

        with nc.Fori(0, DEPTH) as layer:
            L = bass.ds(layer, 1)
            with nc.Block() as block:
                @block.sync
                def _(sp):
                    sp.dma_start(vbuf[:, 0:D_IN], d["b_in"][L, :].to_broadcast([P, D_IN])).then_inc(bias_in, 16)
                    w_in_l = d["w_in"][L].rearrange("o (k p) c -> p (o k) c", p=P)
                    w_slab = (w_slab0, w_slab1, w_slab2)

                    def load_slab(g):
                        w = min(SLAB, D_IN - g * SLAB)
                        sp.dma_start(slab[g % 3][:, :, 0:w], w_in_l[:, :, g * SLAB:g * SLAB + w]).then_inc(w_slab[g % 3], 16)

                    for g in range(3):
                        load_slab(g)
                    with sp.If(layer < 1):
                        for rows_d in (xd, yd):
                            sp.dma_start(rows_d.rearrange("(p a) (c n) -> p (a c) n", p=P, n=P),
                                         zero[:, :].unsqueeze(1).to_broadcast([P, N_BLOCKS * D_MODEL // P, P])).then_inc(s_fill, 16)
                    ws_l = d["w_s"][L].rearrange("o h t s -> t (o h) s")
                    bs_l = d["b_s"][L].rearrange("o h t -> t (o h)")
                    for b in range(DEC_BATCH):
                        at = slice(b * DEC_SEQ, (b + 1) * DEC_SEQ)
                        sp.dma_start(ws8[at], ws_l[0:DEC_SEQ, :, 0:DEC_SEQ]).then_inc(gate_in, 16)
                        sp.dma_start(bss[at, :], bs_l[0:DEC_SEQ, :], allow_slow_non_contiguous=True).then_inc(gate_in, 16)
                        sp.dma_start(mp_s[at, :], d["state_mlstm_m"][L, b, :].to_broadcast([DEC_SEQ, HEADS])).then_inc(gate_in, 16)
                    sp.dma_start(bs[:, :], bs_l, allow_slow_non_contiguous=True).then_inc(gate_in, 16)
                    sp.dma_start(gmix[:, :], d["g_mix"][L].rearrange("o (k p) -> p (o k)", p=P),
                                 allow_slow_non_contiguous=True).then_inc(gate_in, 16)
                    for g in range(3, N_SLABS):
                        sp.wait_ge(z_ps, NT * (g - 2))
                        load_slab(g)
                    sp.wait_ge(z_ps, NT * 6)
                    sp.dma_start(ws_nat, ws_l).then_inc(ws_n, 16)
                    sp.wait_ge(rope_done, 1)
                    for b in range(DEC_BATCH):
                        at = slice(b % 2 * HD, (b % 2 + 1) * HD)
                        for st, to in (("state_ret", rs[at, b // 2, :, :]), ("state_mlstm_c", cs[at, b // 2, :, 0:HD])):
                            sp.dma_start(to, d[st][L, b].rearrange("o h d e -> d (o h) e")).then_inc(s_in, 16)
                        sp.dma_start(cs[at, b // 2, :, HD:HD + 1].rearrange("p h o -> p (h o)"), d["state_mlstm_n"][L, b].rearrange("o h d -> d (o h)"),
                                     allow_slow_non_contiguous=True).then_inc(s_in, 16)
                    sp.wait_ge(e_fin, 1)
                    w_out_l = d["w_out"][L].rearrange("o (k p) c -> p (o k) c", p=P)
                    for s in range(2):
                        sp.dma_start(slab[s][:, :, :], w_out_l[:, :, s * SLAB:(s + 1) * SLAB]).then_inc(wout_in, 16)
                    for i, name in enumerate(("ln1_g", "ln1_b", "ln2_g", "ln2_b")):
                        sp.dma_start(vbuf[:, i * D_MODEL:(i + 1) * D_MODEL],
                                     d[name][L, :].to_broadcast([P, D_MODEL])).then_inc(ln_par, 16)
                    sp.wait_ge(m_ps, 2 * NT)
                    sp.dma_start(wr[:, :, 0:GROUPS], d["w_rg"][L].rearrange("o (k p) g -> p (o k) g", p=P)).then_inc(r_w, 16)
                    for g in range(GROUPS):
                        c = GROUPS * (g + 1)
                        sp.dma_start(wr[:, :, c:c + 4], d["w_re"][L, g].rearrange("o (k p) e -> p (o k) e", p=P)).then_inc(r_w, 16)
                    sp.dma_start(br[:, 0:GROUPS], d["b_rg"][L, :].to_broadcast([P, GROUPS])).then_inc(r_w, 16)
                    sp.dma_start(br[:, GROUPS:], d["b_re"][L].rearrange("o g e -> o (g e)").to_broadcast([P, EXPERTS])).then_inc(r_w, 16)
                    sp.wait_ge(o_ps, NT)
                    w13_in, w2_in = (w13_in0, w13_in1), (w2_in0, w2_in1)

                    def load_w13(e, s):
                        sp.dma_start(w13[s][:, 0], d["w1"][e].rearrange("o (p k) f -> p (o k) f", p=P)).then_inc(w13_in[s], 16)
                        sp.dma_start(w13[s][:, 1], d["w3"][e].rearrange("o (p k) f -> p (o k) f", p=P)).then_inc(w13_in[s], 16)

                    def load_w2(e, s):
                        sp.dma_start(w2[s], d["w2"][e].rearrange("o (p f) n -> p (o f) n", p=P)).then_inc(w2_in[s], 16)

                    def expert_of(k):
                        return bass.ds(layer * EXPERTS + sp.value_load(plan[0:1, bass.ds(k, 1)], min_val=0, max_val=EXPERTS - 1), 1)

                    for s in range(2):
                        load_w13(bass.ds(layer * EXPERTS + s, 1), s)
                    for s in range(2):
                        load_w2(bass.ds(layer * EXPERTS + s, 1), s)
                    sp.wait_ge(planned, 1)
                    last_pair = sp.value_load(plan[0:1, N_BLOCKS:N_BLOCKS + 1], min_val=EXPERTS // 2 - 1, max_val=N_BLOCKS // 2 - 1)
                    with sp.Fori(1, last_pair + 1) as i:
                        es = [expert_of(i * 2 + s) for s in range(2)]
                        for s in range(2):
                            sp.wait_ge(h_ps, i * 2 + (s - 1))
                            load_w13(es[s], s)
                        for s in range(2):
                            sp.wait_ge(y_ps, i * 2 + (s - 1))
                            load_w2(es[s], s)

                @block.gpsimd
                def _(pool):
                    ck = d["cache_k"].rearrange("l n (a b) h e -> (l n a) (b h e)", b=KPP)
                    cv = d["cache_v"].rearrange("l n (a b) h e -> (l n a) (b h e)", b=KPP)
                    cl = d["cache_logf"].rearrange("l n (a b) h -> (l n a) (b h)", b=KPP)

                    def gather(to, table, b, sem):
                        pool.indirect_dma_start(to, None, table, bass.IndirectOffsetOnAxis(idx_u[:, b:b + 1], 0)).then_inc(sem, 16)

                    pool.wait_ge(idx_set, 1)
                    gather(kbuf[:, :], ck, 0, k_in)
                    pool.wait_ge(z_sb, NT * N_SLABS)
                    gather(vbuf[:, :], cv, 0, v_in)
                    for b in range(DEC_BATCH):
                        gather(lfg[:, b, :, :].rearrange("p a b -> p (a b)"), cl, b, l_in)
                    for b in range(DEC_BATCH):
                        if b < DEC_BATCH - 1:
                            pool.wait_ge(e_kps, 8 * (b + 1))
                            gather(kbuf[:, :], ck, b + 1, k_in)
                        if b > 0:
                            pool.wait_ge(e_pv, b)
                            gather(vbuf[:, :], cv, b, v_in)

                    pool.wait_ge(s_fill, 32)
                    pool.wait_ge(planned, 1)
                    for t in tiles:
                        n = rows[t]
                        for c in range(TOP_K):
                            pool.indirect_dma_start(xd, bass.IndirectOffsetOnAxis(rows_u[0:n, t, c:c + 1], 0), x[0:n, t, :], None).then_inc(x_sent, 16)
                    pool.wait_ge(y_stored, 1)
                    for t in tiles:
                        n = rows[t]
                        for c in range(TOP_K):
                            pool.indirect_dma_start(yg[0:n, t, c, :], None, yd, bass.IndirectOffsetOnAxis(rows_u[0:n, t, c:c + 1], 0)).then_inc(y_back[t], 16)

                @block.scalar
                def _(act):
                    due = Due()
                    own = Due()

                    def link(ins):
                        ins.then_inc(chain_a, 1)
                        act.wait_ge(chain_a, own(chain_a))

                    def f(out, in_, fn, **kw):
                        return nc.scalar.activation(out, in_, fn, **kw)

                    def rsqrt(out, in_, eps, scale, sem):
                        link(f(out, in_, ACT.Ln, scale=scale, bias=eps))
                        f(out, out, ACT.Exp, scale=-0.5).then_inc(sem, 1)

                    def store(out, in_, **kw):
                        act.dma_start(out, in_, **kw).then_inc(stored, 16)
                        own(stored, 16)

                    for i in range(2 * NT):
                        t, hf = i // 2, i % 2
                        act.wait_ge(xT_ps, i + 1)
                        f(xTv[:, 4 * hf:4 * hf + 4, t * P:t * P + rows[t]], ps[:, 4 + i % 4, 0:4 * rows[t]].rearrange("p (k n) -> p k n", k=4),
                          ACT.Copy).then_inc(xT_sb, 1)
                    act.wait_ge(z_sb, NT * 1)
                    f(zt[:, :, 0:2 * GW], zt[:, :, 0:2 * GW], ACT.Gelu_apprx_tanh).then_inc(gelu_done, 1)
                    act.wait_ge(z_sb, NT * 3)
                    f(Zall("b_g"), Zall("b_g"), ACT.Silu).then_inc(silu_done, 1)
                    act.wait_ge(z_sb, NT * 5)
                    f(Zall("c_o"), Zall("c_o"), ACT.Sigmoid).then_inc(sigm_done, 1)
                    act.wait_ge(z_sb, NT * N_SLABS)
                    kp, vp = d["k_prompt"], d["v_prompt"]
                    for name, out in (("d_k", kp), ("d_v", vp)):
                        c = COLS[name]
                        store(out[L].rearrange("o a (t p) h e -> p (o a t) (h e)", p=P), zt[:, 0:NP, c:c + GW])
                    for name, out in (("d_k", d["k_sample"]), ("d_v", d["v_sample"])):
                        store(out[L].rearrange("o b t h e -> (o b t) (h e)"), Z(NP, name, NS))
                    act.wait_ge(norm_sum, 1)
                    rsqrt(s_rstd, s_sum, T("ln_eps"), 1.0 / HD, norm_rs)
                    act.wait_ge(va_ready, 1)
                    store(d["chunk_v_sample"][L].rearrange("o b t h e -> (o b t) (h e)"), Z(NP, "a_v", NS))
                    act.wait_ge(f_in, 1)
                    link(f(fe, fa, ACT.Exp))
                    f(fe, fe, ACT.Ln, bias=1.0).then_inc(f_exp, 1)
                    act.wait_ge(f_gates, 1)
                    store(d["logf_prompt"][L].rearrange("o a (t p) h -> p (o a t) h", p=P), th(lf)[:, 0:NP, HEADS:])
                    store(d["logf_sample"][L].rearrange("o b t h -> (o b t) h"), th(lf)[0:NS, NP, HEADS:])

                    act.wait_ge(e_T, 1)
                    f(kTn, ps[:, 0, 2 * NS:4 * NS].rearrange("p (a n) -> p a n", a=2), ACT.Copy).then_inc(e_Tsb, 1)

                    def copy_scores(r):
                        act.wait_ge(e_row, 2 * r + 2)
                        if r >= 2:
                            act.wait_ge(e_s, r - 1)
                        f(srow[r % 2][0:HQ], ps[0:HQ, 1, :], ACT.Copy).then_inc(e_rsb, 1)

                    def cache_step(u):
                        i, g = u // 8, u % 8
                        if i < DEC_BATCH:
                            act.wait_ge(e_kps, u + 1)
                            if u >= 2:
                                act.wait_ge(e_row, u - 1)
                            f(kTs[u % 2], ps[:, 0, :], ACT.Copy).then_inc(e_ksb, 1)
                            if g in (2, 4, 6):
                                copy_scores(4 * i + g // 2 - 1)
                        if g == 6 and i > 0:
                            act.wait_ge(e_xs, i)
                            if i > 2:
                                act.wait_ge(e_pv, i - 2)
                            f(pp[(i - 1) % 2], xs[(i - 1) % 2], ACT.Exp).then_inc(e_p, 1)
                        if g == 7 and i < DEC_BATCH:
                            copy_scores(4 * i + 3)

                    steps = iter(range(CACHE_STEPS))

                    for t in tiles:
                        n = rows[t]
                        act.wait_ge(b_T, t + 1)
                        src = ps[:, 4, 0:4 * n].rearrange("p (a n) -> p a n", a=4)
                        f(qkT[:, 0:2, 0:n], src[:, 0:2], ACT.Copy).then_inc(b_Tsb, 1)
                        f(qkT[:, 2:4, 0:n], src[:, 2:4], ACT.Copy, scale=SCALE).then_inc(b_Tsb, 1)
                        for _ in range(3):
                            cache_step(next(steps))
                        if t == NP - 1:
                            act.wait_ge(b_state, NP)
                            for par in range(2):
                                store(d["ret_prompt"][L].rearrange("o a (pr r) d e -> r d (o a pr) e", r=2)[par],
                                      ret[par * HD:(par + 1) * HD])
                    act.wait_ge(b_state, NT)
                    for b in range(DEC_BATCH):
                        at = slice(b % 2 * HD, (b % 2 + 1) * HD)
                        store(d["ret_sample"][L, b].rearrange("o h d e -> d (o h) e"), rs[at, b // 2, :, :])

                    for t in tiles:
                        n = rows[t]
                        act.wait_ge(c_T, t + 1)
                        src = ps[:, 4, 0:4 * n].rearrange("p (a n) -> p a n", a=4)
                        f(qkT[:, 0:2, 0:n], src[:, 0:2], ACT.Copy).then_inc(c_Tsb, 1)
                        f(qkT[:, 2:4, 0:n], src[:, 2:4], ACT.Copy, scale=SCALE).then_inc(c_Tsb, 1)
                        if t > 0:
                            act.wait_ge(c_up, t)
                        else:
                            act.wait_ge(c_free, 1)
                        f(vx[0:n, :, 0:HD], heads(Z(t, "c_v", n)), ACT.Copy).then_inc(c_vx, 1)
                        cache_step(next(steps))
                        act.wait_ge(c_t, t + 1)
                        for h in range(HEADS):
                            c = t * HEADS + h
                            f(wexp[0:n, h, 0:n], wexp[0:n, h, 0:n], ACT.Exp, bias=gi[0:n, c:c + 1]).then_inc(c_w, 1)
                        cache_step(next(steps))
                        act.wait_ge(c_mt, t + 1)
                        f(we[0:n], wx[0:n], ACT.Exp).then_inc(c_exps, 1)
                        act.wait_ge(c_gin, t + 1)
                        f(ge[0:n], gx[0:n], ACT.Exp).then_inc(c_gs, 1)
                        for _ in range(2):
                            cache_step(next(steps))
                        if t == NP - 1:
                            act.wait_ge(c_cd, NP)
                            for par in range(2):
                                at = slice(par * HD, (par + 1) * HD)
                                store(d["mlstm_c_prompt"][L].rearrange("o a (pr r) d e -> r d (o a pr) e", r=2)[par],
                                      mem[at, :, 0:HD])
                                store(d["mlstm_n_prompt"][L].rearrange("o a (pr r) d -> r d (o a pr)", r=2)[par],
                                      mem[at, :, HD:HD + 1].rearrange("p a b -> p (a b)"), allow_slow_non_contiguous=True)
                            store(d["mlstm_m_prompt"][L].rearrange("o a h -> (o a) h"), mp_p[0:1, :])
                    act.wait_ge(c_cd, NT)
                    for b in range(DEC_BATCH):
                        at = slice(b % 2 * HD, (b % 2 + 1) * HD)
                        store(d["mlstm_c_sample"][L, b].rearrange("o h d e -> d (o h) e"), cs[at, b // 2, :, 0:HD])
                        store(d["mlstm_n_sample"][L, b].rearrange("o h d -> d (o h)"),
                              cs[at, b // 2, :, HD:HD + 1].rearrange("p h o -> p (h o)"), allow_slow_non_contiguous=True)
                    store(d["mlstm_m_sample"][L].rearrange("o b h -> (o b) h"), mp_s[0:NS:DEC_SEQ, :])
                    act.wait_ge(stored, own(stored, 0))
                    act.sem_inc(stored_in, 1)

                    for t in range(NP):
                        act.wait_ge(d_T, t + 1)
                        src = ps[:, 4 + 2 * (t % 2), :].rearrange("p (a n) -> p a n", a=4)
                        f(qTa[:, :, t * P:(t + 1) * P], src[:, 0:2], ACT.Copy, scale=SCALE).then_inc(d_Tsb, 1)
                        f(kTa[:, :, t * P:(t + 1) * P], src[:, 2:4], ACT.Copy).then_inc(d_Tsb, 1)
                    cache_step(next(steps))
                    for m in range(NP * HEADS + 1):
                        if m < NP * HEADS:
                            w = (m // HEADS + 1) * P
                            act.wait_ge(d_lgx, m + 1)
                            f(lg[m % 2][:, 0:w], lg[m % 2][:, 0:w], ACT.Exp, bias=nmax[:, m:m + 1],
                              accum_out=rsum[:, m:m + 1]).then_inc(d_exp, 1)
                        if m > 0:
                            w = (m - 1) // HEADS + 1
                            act.wait_ge(d_pT, m)
                            f(pT[(m - 1) % 2][:, 0:w, :], ps[:, 5, 0:w * P].rearrange("p (a n) -> p a n", n=P),
                              ACT.Copy).then_inc(d_pTsb, 1)
                        if m < NP * HEADS:
                            for _ in range(2):
                                cache_step(next(steps))
                    for u in steps:
                        cache_step(u)

                    for _ in MERGED:
                        act.wait_ge(rms_s, due(rms_s))
                        rsqrt(s_rstd, s_sum, T("rms_eps"), 1.0 / HD, rms_r)

                    def layer_norm():
                        for t in tiles:
                            n = rows[t]
                            act.wait_ge(o_var, due(o_var))
                            rsqrt(lnr[0:n, 0:1], lnmv[0:n, 1:2], T("ln_eps", n), 1.0, o_rstd)
                    layer_norm()
                    for i in range(2 * NT):
                        t, hf = i // 2, i % 2
                        act.wait_ge(xT_ps, 2 * NT + i + 1)
                        f(xTv[:, 4 * hf:4 * hf + 4, t * P:t * P + rows[t]], ps[:, 4 + i % 4, 0:4 * rows[t]].rearrange("p (k n) -> p k n", k=4),
                          ACT.Copy).then_inc(xT_sb, 1)
                    act.wait_ge(r_lg, 1)
                    f(r_ge, r_gd, ACT.Exp).then_inc(r_exp, 1)
                    act.wait_ge(r_e2, 1)
                    f(r_ex, r_vd, ACT.Exp).then_inc(r_e2x, 1)
                    act.wait_ge(planned, 1)
                    last_pair = act.value_load(plan[0:1, N_BLOCKS:N_BLOCKS + 1], min_val=EXPERTS // 2 - 1, max_val=N_BLOCKS // 2 - 1)
                    act.wait_ge(x_sent, layer * (16 * NT * TOP_K) + 16 * NT * TOP_K)
                    xg_in, y_out = (xg_in0, xg_in1), (y_out0, y_out1)

                    def load_block(k, s):
                        act.dma_start(xg[s], xd[bass.ds(k * BLOCK, BLOCK), :]).then_inc(xg_in[s], 16)

                    def turn_block(k2, s):
                        for hf in range(2):
                            act.wait_ge(xgT_ps, k2 + (hf + 1))
                            f(xgT[s][:, 4 * hf:4 * hf + 4, :], ps[:, hf, :].rearrange("p (k n) -> p k n", k=4), ACT.Copy).then_inc(xgT_sb, 1)

                    def act_block(i, k, s, more, turn):
                        if more:
                            load_block(k + 2, s)
                        act.wait_ge(h_ps, k + 1)
                        f(sil[s], ps[:, 2 + s, 0:2 * BLOCK], ACT.Silu).then_inc(sil_sb, 1)
                        if turn:
                            turn_block(k * 2 + 2, 1 - s)
                        act.wait_ge(y_ps, k + 1)
                        act.wait_ge(y_out[s], i * 16 + 16)
                        f(yo[s][:, SLAB:], ps[:, 5 + 2 * s, :], ACT.Copy).then_inc(y_sb, 1)
                        act.wait_ge(y_sb, k * 2 + 5)
                        act.dma_start(yd[bass.ds(k * BLOCK, BLOCK), :], yo[s]).then_inc(y_out[s], 16)

                    act.sem_inc(y_out0, 16)
                    act.sem_inc(y_out1, 16)
                    for s in range(2):
                        act.dma_start(xg[s], xd[s * BLOCK:(s + 1) * BLOCK, :]).then_inc(xg_in[s], 16)
                    turn_block(0, 0)
                    with act.Fori(0, last_pair) as i:
                        act_block(i, i * 2, 0, True, True)
                        act_block(i, i * 2 + 1, 1, True, True)
                    lp = last_pair
                    act_block(lp, lp * 2, 0, False, True)
                    act_block(lp, lp * 2 + 1, 1, False, False)
                    for s in range(2):
                        act.wait_ge(y_out[s], last_pair * 16 + 32)
                    act.sem_inc(y_stored, 1)
                    for t in tiles:
                        f(x[0:rows[t], t, :], x[0:rows[t], t, :], ACT.Copy, scale=ALPHA).then_inc(y_init, 1)
                    layer_norm()
                    act.wait_ge(stored, own(stored, 0))

                @block.vector
                def _(dve):
                    due = Due()
                    own = Due()
                    V = nc.vector

                    def link(ins, sem=None):
                        sem = sem or chain_v
                        ins.then_inc(sem, 1)
                        dve.wait_ge(sem, own(sem))

                    def tt(out, a, b, op):
                        return V.tensor_tensor(out, a, b, op)

                    V.tensor_copy(idx_u[:, :], idx_f[:, :]).then_inc(idx_set, 1)
                    link(V.tensor_scalar(idx_f[:, :], idx_f[:, :], float(N_POOL * RPP), None, ALU.add))
                    dve.wait_ge(bias_in, 16)
                    for g in range(N_SLABS):
                        w = min(SLAB, D_IN - g * SLAB)
                        for t in tiles:
                            i, n = g * NT + t, rows[t]
                            dve.wait_ge(z_ps, i + 1)
                            tt(zt[0:n, t, g * SLAB:g * SLAB + w], ps[0:n, i % 4, 0:w], vbuf[0:n, g * SLAB:g * SLAB + w],
                               ALU.add).then_inc(z_sb, 1)
                    dve.wait_ge(z_sb, NT * N_SLABS)
                    dve.wait_ge(gelu_done, 1)
                    va, sq = v4(Zall("a_v")), v4(tmp_a)
                    link(V.tensor_reduce(th(s_sum), va, AX.X, ALU.add))
                    link(V.tensor_scalar(s_sum, s_sum, 1.0 / HD, None, ALU.mult))
                    link(tt(va, va, over_e(th(s_sum)), ALU.subtract))
                    link(tt(sq, va, va, ALU.mult))
                    V.tensor_reduce(th(s_sum), sq, AX.X, ALU.add).then_inc(norm_sum, 1)
                    V.tensor_copy(th(ff)[:, :, 0:HEADS], Zall("c_f", HEADS))
                    link(V.tensor_copy(th(ff)[:, :, HEADS:], Zall("d_f", HEADS)))
                    link(V.tensor_scalar(fa, ff, -1.0, None, ALU.mult))
                    tt(fa, ff, fa, ALU.min).then_inc(f_in, 1)
                    c0 = COLS["b_q"]
                    qk = zt[:, :, c0:c0 + 2 * GW].rearrange("p t (h r e) -> p t h r e", h=2 * HEADS, r=2)
                    x1, x2 = qk[:, :, :, 0, :], qk[:, :, :, 1, :]
                    co, si = [T(name).rearrange("p (t e) -> p t e", t=NT).unsqueeze(2).to_broadcast([P, NT, 2 * HEADS, HD // 2])
                              for name in ("cos", "sin")]
                    rb, rc = [tmp.rearrange("p t (h e) -> p t h e", h=2 * HEADS) for tmp in (tmp_b, tmp_c)]
                    tt(rb, x1, si, ALU.mult)
                    link(tt(rc, x2, si, ALU.mult))
                    tt(x1, x1, co, ALU.mult)
                    link(tt(x2, x2, co, ALU.mult))
                    tt(x1, x1, rc, ALU.subtract)
                    link(tt(x2, x2, rb, ALU.add))
                    dve.wait_ge(norm_rs, 1)
                    tt(va, va, over_e(th(s_rstd)), ALU.mult).then_inc(va_ready, 1)
                    dve.wait_ge(va_ready, 1)
                    V.memset(ret[:, :, :], 0.0)
                    V.memset(mem[:, :, :], 0.0)
                    V.memset(mp_p, 0.0).then_inc(rope_done, 1)
                    dve.wait_ge(rope_done, 1)
                    dve.wait_ge(f_exp, 1)
                    link(V.tensor_scalar(ff, ff, 0.0, None, ALU.min))
                    tt(lf, ff, fe, ALU.subtract).then_inc(f_gates, 1)
                    dve.wait_ge(f_gates, 1)
                    dve.wait_ge(gate_in, 16 * (3 * DEC_BATCH + 2))
                    up_b = T("lower_s", NS).rearrange("p (b s) -> p b s", s=DEC_SEQ).unsqueeze(1)
                    link(tt(ws_exp[0:NS].rearrange("p h (b s) -> p h b s", s=DEC_SEQ),
                            ws8[:, :, :].unsqueeze(2).to_broadcast([NS, HEADS, DEC_BATCH, DEC_SEQ]),
                            up_b.to_broadcast([NS, HEADS, DEC_BATCH, DEC_SEQ]), ALU.mult), ws_s8)
                    dve.wait_ge(ws_ps, 1)
                    tt(wsT[:, :, :], ps[:, 4, :].rearrange("p (h t) -> p h t", h=HEADS), rep(T("upper"), HEADS), ALU.mult).then_inc(ws_sb, 1)
                    dve.wait_ge(ws_ps, 2)
                    V.tensor_copy(wsTs[:, :, :], ps[0:NS, 5, 0:GW].rearrange("p (h t) -> p h t", h=HEADS)).then_inc(ws_sb, 1)
                    dve.wait_ge(a_ps, 1)
                    ya = v4(Zall("a_u"))
                    for t in tiles:
                        n = rows[t]
                        link(tt(mix[0:n, :, 0:HD], heads(ps[0:n, t if t < NP else 6, 0:GW]), b3((bs if t < NP else bss)[0:n, :], HD), ALU.add))
                        link(tt(ya[0:n, t], ya[0:n, t], mix[0:n, :, 0:HD], ALU.mult))
                    dve.wait_ge(gate_ps, 1)
                    V.tensor_copy(cum[:, 0:NP * HEADS], ps[:, 7, 0:NP * HEADS])
                    link(V.tensor_copy(cum[0:NS, NP * HEADS:], ps[0:NS, 7, NP * HEADS:NT * HEADS]), gate_sb)
                    ci = Zall("c_i", HEADS)
                    tt(th(gi)[:, 0:NP], ci[:, 0:NP], th(cum)[:, 0:NP], ALU.subtract)
                    link(tt(gi[0:NS, NP * HEADS:], ci[0:NS, NP], cum[0:NS, NP * HEADS:], ALU.subtract))

                    def sample_queries(name):
                        link(V.tensor_copy(qd2[0:NS].rearrange("p h (r e) -> p h r e", r=2),
                                           heads(Z(NP, name, NS)).unsqueeze(2).to_broadcast([NS, HEADS, 2, HD])), qm_q)
                        dve.wait_ge(qm_ps, due(qm_ps))
                        for bp in range(BP):
                            m = tt(qm[:, bp], ps[:, 4, 0:GW].rearrange("p (h n) -> p h n", h=HEADS),
                                   rep(T("seq_of")[:, bp * NS:(bp + 1) * NS], HEADS), ALU.mult)
                        m.then_inc(qm_sb, 1)

                    def sample_keys(w):
                        for h in range(HEADS):
                            if h > 0:
                                dve.wait_ge(km_used, due(km_used))
                            tt(km[0:NS], rep(kd[0:NS, h * HD:(h + 1) * HD], DEC_BATCH), b3(T("in_seq", NS), HD), ALU.mult).then_inc(km_sb, 1)
                        due(km_used)
                        dve.wait_ge(km_used, own(km_used, HEADS))

                    dve.wait_ge(d_cum, 1)
                    V.tensor_scalar(ncum[:, 0:NP * HEADS], ps[:, 5, 0:NP * HEADS], -1.0, None, ALU.mult)
                    link(V.tensor_scalar(ncum[0:NS, NP * HEADS:], ps[0:NS, 5, NP * HEADS:NT * HEADS], -1.0, None, ALU.mult))
                    V.memset(qz, 0.0)
                    V.memset(xs[0], NEG)
                    link(V.memset(xs[1], NEG))
                    dve.wait_ge(e_Tsb, 1)
                    for par in range(2):
                        at = slice(par * HD, (par + 1) * HD)
                        for pair in range(PAIRS):
                            c = (2 * pair + par) * DEC_SEQ
                            V.tensor_scalar(qz[at, pair, :, c:c + DEC_SEQ], ps[at, 0, pair * NS:(pair + 1) * NS].rearrange("p (b t) -> p b t", t=DEC_SEQ),
                                            SCALE, None, ALU.mult).then_inc(e_Tsb, 1)
                    msk = T("neg_ts", NS).rearrange("p (b t) -> p b t", t=DEC_SEQ)
                    for h in range(HEADS):
                        m = tt(newb[0:NS, :, h, :], msk, ncum[0:NS, NP * HEADS + h:NP * HEADS + h + 1].unsqueeze(2).to_broadcast([NS, DEC_BATCH, DEC_SEQ]), ALU.add)
                    link(m)
                    dve.wait_ge(l_in, layer * (16 * DEC_BATCH) + 16 * DEC_BATCH)
                    link(V.tensor_reduce(sufp.rearrange("p (b h) -> p b h", h=HEADS), lfg.rearrange("p b k h -> p b h k"), AX.X, ALU.add), e_tot)
                    dve.wait_ge(e_cumps, 1)
                    link(V.tensor_copy(sfx[:, :, KPP - 1, :], ps[:, 3, 0:DEC_BATCH * HEADS].rearrange("p (b h) -> p b h", h=HEADS)))
                    for k in range(KPP - 2, -1, -1):
                        link(tt(sfx[:, :, k, :], sfx[:, :, k + 1, :], lfg[:, :, k + 1, :], ALU.add))

                    def finish_sequence(i):
                        dve.wait_ge(e_pv, i + 1)
                        link(V.reciprocal(prec[0:HQ, 0:1], ps[0:HQ, 3, GW:GW + 1]))
                        V.scalar_tensor_tensor(ym[0:HQ, i], ps[0:HQ, 3, 0:GW], prec[0:HQ, 0:1], T("own_head", HQ), ALU.mult, ALU.mult).then_inc(e_ym, 1)

                    def cache_step(u):
                        i, g = u // 8 - 1, u % 8
                        if i < 0:
                            return
                        X = xs[i % 2]
                        if g == 0:
                            dve.wait_ge(e_s, 4 * i + 4)
                            dve.wait_ge(e_psum, i + 1)
                            if i >= 2:
                                dve.wait_ge(e_p, i - 1)
                            S = ps[:, 2, :].rearrange("p (k h t) -> p (k h) t", h=HEADS, t=DEC_SEQ)
                            tt(X[:, 0:KPP, :].rearrange("p k (h t) -> p (k h) t", t=DEC_SEQ), S, b3(sfx[:, i].rearrange("p k h -> p (k h)"), DEC_SEQ), ALU.add)
                            c = NEW + i % 2 * HQ
                            link(tt(X[0:NS, KPP, :], ps[0:NS, 3, c:c + HQ], newb[0:NS, i].rearrange("p h t -> p (h t)"), ALU.add))
                            V.tensor_reduce(pmax, X.rearrange("p k c -> p c k"), AX.X, ALU.max).then_inc(e_pm, 1)
                            if i > 0:
                                finish_sequence(i - 1)
                        if g == 3:
                            dve.wait_ge(e_mt, i + 1)
                            link(V.tensor_reduce(pcol[0:HQ, 0:1], ps[0:HQ, 3, MT:MT + P], AX.X, ALU.max))
                            V.tensor_scalar(pdiag[0:HQ], T("ident", HQ)[:, 0:HQ], pcol[0:HQ, 0:1], None, ALU.mult).then_inc(e_dg, 1)
                        if g == 5:
                            dve.wait_ge(e_bc, i + 1)
                            link(V.tensor_copy(pmax, ps[:, 3, BC:BC + HQ]))
                            tt(X, X, rep(pmax, NK), ALU.subtract).then_inc(e_xs, 1)
                        if g == 7:
                            dve.wait_ge(e_p, i + 1)
                            V.tensor_reduce(ptot, pp[i % 2].rearrange("p k c -> p c k"), AX.X, ALU.add).then_inc(e_lf, 1)

                    steps = iter(range(CACHE_STEPS))

                    for t in tiles:
                        n, samp = rows[t], t == NP
                        sfx_ = "_s" if samp else ""
                        kdec = b3(T("k_dec" + sfx_, n), HD)
                        link(tt(heads(kd[0:n]), heads(Z(t, "b_k", n)), kdec, ALU.mult), b_kd)
                        cache_step(next(steps))
                        if samp:
                            sample_queries("b_q")
                        dve.wait_ge(b_sc, t + 1)
                        tt(sw[0:n, :, 0:n].rearrange("p (a b) n -> p a b n", a=2), ps[0:n, 6:8, 0:2 * n].rearrange("p a (b n) -> p a b n", b=2),
                           T("dec" + sfx_, n).rearrange("p (a b n) -> p a b n", a=2, b=2), ALU.mult).then_inc(b_sw, 1)
                        cache_step(next(steps))
                        dve.wait_ge(b_out, t + 1)
                        yb = heads(Z(t, "b_q", n))
                        if not samp:
                            link(tt(by_par(mix[0:n, :, 0:HD]), ps[0:n, 6:8, 0:2 * HD].rearrange("p a (b e) -> p a b e", b=2),
                                    T("q_dec", n).rearrange("p (a b) -> p a b", a=2).unsqueeze(3).to_broadcast([n, 2, 2, HD]), ALU.mult))
                        else:
                            link(tt(mix[0:n, :, 0:HD], heads(ps[0:n, 6, 0:GW]), b3(T("q_dec_s", n), HD), ALU.mult))
                        link(tt(yb, heads(ps[0:n, 4, 0:GW]), mix[0:n, :, 0:HD], ALU.add))
                        if not samp:
                            link(tt(ret[:, :, :], ret[:, :, :], b3(T("c_dec"), HD), ALU.mult))
                            dve.wait_ge(b_up, t + 1)
                            for par in range(2):
                                at = slice(par * HD, (par + 1) * HD)
                                m = tt(ret[at], ret[at], ps[at, 5, 0:4 * HD].rearrange("p (a b) -> p a b", a=2)[:, :, par * HD:(par + 1) * HD], ALU.add)
                            link(m, b_state)
                        else:
                            sample_keys("b")
                            link(tt(rs, rs, T("c_dec_s").unsqueeze(1).unsqueeze(3).to_broadcast([P, BP, HEADS, HD]), ALU.mult))
                            link(tt(rs.rearrange("p (x a) h e -> p x (a h e)", x=2), rs.rearrange("p (x a) h e -> p x (a h e)", x=2), ps[:, 4:6, :], ALU.add), b_state)
                        cache_step(next(steps))

                    V.memset(vx[:, :, HD:HD + 1], 1.0).then_inc(c_free, 1)
                    dve.wait_ge(c_free, 1)
                    for t in tiles:
                        n, samp = rows[t], t == NP
                        sfx_ = "_s" if samp else ""
                        mp = mp_s if samp else mp_p
                        g_t, b_t = [a[0:n, t * HEADS:(t + 1) * HEADS] for a in (gi, cum)]
                        link(V.scalar_tensor_tensor(gp[0:n], mp[0:n], T("start" + sfx_, n), g_t, ALU.add, ALU.max))
                        tt(diag[0:n, :, 0:n], rep(T("ident", n)[:, 0:n], HEADS), b3(gp[0:n], n), ALU.mult).then_inc(c_dg, 1)
                        cache_step(next(steps))
                        if samp:
                            sample_queries("c_q")
                        dve.wait_ge(c_row, t + 1)
                        mr = mrow_flat[0:n, 0:HEADS * n]
                        link(V.tensor_tensor_scan(mr, T("reset" + sfx_, n), ps[0:n, 5, 0:HEADS * n], 0.0, ALU.add, ALU.max))
                        mr = mr.rearrange("p (h n) -> p h n", h=HEADS)
                        tt(wexp[0:n, :, 0:n], rep(T("neg_ts" if samp else "neg_t", n), HEADS), mr, ALU.subtract).then_inc(c_t, 1)
                        link(tt(diag[0:n, :, 0:n], rep(T("ident", n)[:, 0:n], HEADS), mr, ALU.mult))
                        link(V.tensor_reduce(mcol[0:n], diag[0:n, :, 0:n], AX.X, ALU.add))
                        tt(wx[0:n, 0:HEADS], mp[0:n], mcol[0:n], ALU.subtract)
                        V.tensor_copy(mtb[0:n, HEADS:], b_t)
                        link(tt(mtb[0:n, 0:HEADS], b_t, mcol[0:n], ALU.add))
                        link(V.tensor_scalar(wx[0:n, HEADS:], mtb[0:n, 0:HEADS], -1.0, None, ALU.mult), c_mt)
                        cache_step(next(steps))
                        dve.wait_ge(c_last, t + 1)
                        link(V.tensor_copy(lastv[0:n], ps[0:n, 5, 0:2 * HEADS]))
                        link(tt(lastv[0:n, HEADS:], lastv[0:n, HEADS:], lastv[0:n, 0:HEADS], ALU.subtract))
                        tt(gx[0:n, 0:HEADS], g_t, lastv[0:n, HEADS:], ALU.add)
                        link(tt(gx[0:n, HEADS:], mp[0:n], lastv[0:n, HEADS:], ALU.add), c_gin)
                        V.tensor_copy(mp[0:n], lastv[0:n, 0:HEADS])
                        dve.wait_ge(c_gs, t + 1)
                        link(V.scalar_tensor_tensor(heads(kd[0:n]), heads(Z(t, "c_k", n)), SCALE, b3(ge[0:n, 0:HEADS], HD), ALU.mult, ALU.mult), c_kd)
                        dve.wait_ge(c_sc, t + 1)
                        dve.wait_ge(c_w, HEADS * (t + 1))
                        tt(sw[0:n, :, 0:n].rearrange("p (a b) n -> p a b n", a=2), ps[0:n, 6:8, 0:2 * n].rearrange("p a (b n) -> p a b n", b=2),
                           by_par(wexp[0:n, :, 0:n]), ALU.mult).then_inc(c_sw, 1)
                        cache_step(next(steps))
                        dve.wait_ge(c_out, t + 1)
                        dve.wait_ge(c_exps, t + 1)
                        wst = b3(we[0:n, 0:HEADS], HD + 1)
                        if not samp:
                            link(tt(by_par(mix[0:n]), ps[0:n, 6:8, 0:2 * (HD + 1)].rearrange("p a (b e) -> p a b e", b=2), by_par(wst), ALU.mult))
                        else:
                            link(tt(mix[0:n], heads(ps[0:n, 6, 0:HEADS * (HD + 1)], HD + 1), wst, ALU.mult))
                        link(tt(mix[0:n], heads(ps[0:n, 4, 0:HEADS * (HD + 1)], HD + 1), mix[0:n], ALU.add))
                        dcol = mix[0:n, :, HD:HD + 1].rearrange("p h o -> p (h o)")
                        link(V.scalar_tensor_tensor(den[0:n], dcol, -1.0, we[0:n, HEADS:], ALU.mult, ALU.max))
                        link(tt(den[0:n], den[0:n], dcol, ALU.max))
                        link(V.reciprocal(rden[0:n], den[0:n]))
                        link(tt(heads(Z(t, "c_q", n)), mix[0:n, :, 0:HD], b3(rden[0:n], HD), ALU.mult))
                        if not samp:
                            for par in range(2):
                                at = slice(par * HD, (par + 1) * HD)
                                m = V.tensor_copy(gcol[at], ge[at, HEADS:].rearrange("p (a b) -> p b a", b=2)[:, par, :])
                            link(m)
                            link(tt(mem[:, :, :], mem[:, :, :], b3(gcol, HD + 1), ALU.mult))
                            dve.wait_ge(c_up, t + 1)
                            for par in range(2):
                                at = slice(par * HD, (par + 1) * HD)
                                m = tt(mem[at], mem[at], ps[at, 5, 0:4 * (HD + 1)].rearrange("p (a b) -> p a b", a=2)[:, :, par * (HD + 1):(par + 1) * (HD + 1)], ALU.add)
                            link(m, c_cd)
                        else:
                            sample_keys("c")
                            csf = cs.rearrange("p a h e -> p (a h) e")
                            dve.wait_ge(c_up, t + 1)
                            link(tt(csf, csf, b3(ps[:, 7, CU:CU + BP * HEADS], HD + 1), ALU.mult))
                            for bp, bank in enumerate((4, 5, 6, 7)):
                                m = tt(cs[:, bp].rearrange("p h e -> p (h e)"), cs[:, bp].rearrange("p h e -> p (h e)"),
                                       ps[:, bank, 0:HEADS * (HD + 1)], ALU.add)
                            link(m, c_cd)
                        cache_step(next(steps))

                    dve.wait_ge(stored_in, 1)
                    for h in range(HEADS):
                        if h >= 2:
                            dve.wait_ge(d_row, h - 1)
                        tt(dg[h % 2], rep(T("ident"), NP), b3(th(ncum)[:, 0:NP, h:h + 1].rearrange("p t o -> p (t o)"), P), ALU.mult).then_inc(d_dg, 1)
                        if h >= 1:
                            dve.wait_ge(d_row, h)
                            V.tensor_copy(ncr[:, h - 1, :], ps[:, 5 + 2 * ((h - 1) % 2), :]).then_inc(d_ncr, 1)
                    dve.wait_ge(d_row, HEADS)
                    V.tensor_copy(ncr[:, HEADS - 1, :], ps[:, 5 + 2 * ((HEADS - 1) % 2), :]).then_inc(d_ncr, 1)
                    dve.wait_ge(d_ncr, HEADS)
                    cache_step(next(steps))

                    def d_finish(c):
                        dve.wait_ge(d_o, HEADS * (c + 1))
                        dve.wait_ge(d_exp, HEADS * (c + 1))
                        at = slice(c * HEADS, (c + 1) * HEADS)
                        link(V.reciprocal(drec[:, at], rsum[:, at]))
                        tt(heads(Z(c, "d_q")), heads(ps[:, 7, 0:GW]), b3(drec[:, at], HD), ALU.mult).then_inc(d_y, 1)

                    for m in range(NP * HEADS):
                        c, h = m // HEADS, m % HEADS
                        w = (c + 1) * P
                        if m >= 2:
                            dve.wait_ge(d_pT, m - 1)
                        dve.wait_ge(d_lg, m + 1)
                        link(tt(lg[m % 2][:, 0:w], ps[:, 4 + 2 * (m % 2), 0:w], ncr[:, h, 0:w], ALU.add))
                        V.tensor_reduce(nmax[:, m:m + 1], lg[m % 2][:, 0:w], AX.X, ALU.max, negate=True).then_inc(d_lgx, 1)
                        if h == 1 and c > 0:
                            d_finish(c - 1)
                        for _ in range(2):
                            cache_step(next(steps))
                    d_finish(NP - 1)
                    for u in steps:
                        cache_step(u)
                    finish_sequence(DEC_BATCH - 1)

                    dve.wait_ge(e_fin, 1)
                    link(V.tensor_copy(Z(NP, "d_q", NS), ps[0:NS, 0, 0:GW]))

                    dve.wait_ge(sigm_done, 1)
                    link(tt(Zall("c_q"), Zall("c_q"), Zall("c_o"), ALU.mult))
                    for name in MERGED:
                        y = v4(Zall(name))
                        link(tt(v4(tmp_a), y, y, ALU.mult))
                        V.tensor_reduce(th(s_sum), v4(tmp_a), AX.X, ALU.add).then_inc(rms_s, 1)
                        dve.wait_ge(rms_r, due(rms_r))
                        link(tt(y, y, over_e(th(s_rstd)), ALU.mult))
                        if name == "b_q":
                            dve.wait_ge(silu_done, 1)
                            link(tt(Zall("b_q"), Zall("b_q"), Zall("b_g"), ALU.mult))
                    V.memset(pcol, 0.0).then_inc(merged, 1)
                    for i in range(2 * NT):
                        t, hf = i // 2, i % 2
                        n = rows[t]
                        dve.wait_ge(m_ps, i + 1)
                        tt(xTv[:, 4 * hf:4 * hf + 4, t * P:t * P + n], ps[:, 4 + i % 4, 0:4 * n].rearrange("p (k n) -> p k n", k=4),
                           b3(gmix[:, 4 * hf:4 * hf + 4], n), ALU.mult).then_inc(m_sb, 1)

                    def layer_norm(t, gcol_, src):
                        n = rows[t]
                        X = src[0:n, t, :]
                        for hf in range(2):
                            m = V.bn_stats(lnst[0:n, 6 * hf:6 * hf + 6], X[:, hf * 512:hf * 512 + 512])
                        link(m)
                        link(V.bn_aggr(lnmv[0:n, :], lnst[0:n, :]), o_var)
                        dve.wait_ge(o_rstd, due(o_rstd))
                        link(V.tensor_scalar(X, X, lnmv[0:n, 0:1], lnr[0:n, 0:1], ALU.subtract, ALU.mult))
                        g = gcol_ * D_MODEL
                        link(tt(X, X, vbuf[0:n, g:g + D_MODEL], ALU.mult))
                        link(tt(x[0:n, t, :], X, vbuf[0:n, g + D_MODEL:g + 2 * D_MODEL], ALU.add), ln_n)

                    dve.wait_ge(ln_par, 64)
                    for t in tiles:
                        n = rows[t]
                        dve.wait_ge(o_ps, t + 1)
                        bank = 2 * (t % 2)
                        link(V.scalar_tensor_tensor(x[0:n, t, :].rearrange("p (a b) -> p a b", a=2), x[0:n, t, :].rearrange("p (a b) -> p a b", a=2), ALPHA,
                                                    ps[0:n, bank:bank + 2, :], ALU.mult, ALU.add), y_free)
                        layer_norm(t, 0, x)

                    dve.wait_ge(r_w, 16 * 7)
                    V.memset(rt[:, :, :], 0.0)
                    dve.wait_ge(r_ps, 1)
                    link(V.memset(moe_small, 0.0))
                    NR = GROUPS + EXPERTS
                    tt(rt[:, 0:NP, :], ps[:, 0, 0:NP * NR].rearrange("p (t c) -> p t c", t=NP), rep(br, NP), ALU.add)
                    link(tt(rt[0:NS, NP, :], ps[0:NS, 0, NP * NR:NT * NR], br[0:NS], ALU.add))

                    def first_max(v, vmax, hot):
                        link(V.tensor_reduce(vmax, v, AX.X, ALU.max))
                        link(tt(hot, v, over(vmax), ALU.is_equal))
                        link(tt(hot, hot, rank, ALU.mult))
                        link(V.tensor_reduce(r_m, hot, AX.X, ALU.max))
                        link(tt(hot, hot, over(r_m), ALU.is_equal))

                    def over(v):
                        return b3(v, 4)

                    rank = rep(T("rank"), NT)
                    g_l = rt[:, :, 0:GROUPS]
                    first_max(g_l, r_gm, r_goh)
                    link(tt(r_gd, g_l, over(r_gm), ALU.subtract), r_lg)
                    e_l = rt[:, :, GROUPS:].rearrange("p t (g e) -> p t g e", g=GROUPS)
                    link(tt(r_t16, e_l, r_goh.unsqueeze(3).to_broadcast([P, NT, GROUPS, 4]), ALU.mult))
                    link(V.tensor_reduce(r_el, r_t16.rearrange("p t g e -> p t e g"), AX.X, ALU.add))
                    first_max(r_el, r_v1, r_oh1)
                    link(V.scalar_tensor_tensor(r_e2l, r_oh1, NEG, r_el, ALU.mult, ALU.add))
                    first_max(r_e2l, r_v2, r_oh2)
                    link(tt(r_vd, r_v2, r_v1, ALU.subtract), r_e2)
                    dve.wait_ge(r_exp, 1)
                    link(V.tensor_reduce(r_gw, r_ge, AX.X, ALU.add))
                    link(V.reciprocal(r_gw, r_gw))
                    dve.wait_ge(r_e2x, 1)
                    link(V.tensor_scalar(r_w1, r_ex, 1.0, None, ALU.add))
                    link(V.reciprocal(r_w1, r_w1))
                    link(tt(r_w1, r_w1, r_gw, ALU.mult))
                    link(tt(r_w2, r_w1, r_ex, ALU.mult))
                    for hot, oh in zip(r_hot, (r_oh1, r_oh2)):
                        m = tt(hot.rearrange("p t (g e) -> p t g e", g=GROUPS), r_goh.unsqueeze(3).to_broadcast([P, NT, GROUPS, 4]),
                               oh.unsqueeze(2).to_broadcast([P, NT, GROUPS, 4]), ALU.mult)
                    link(m)
                    link(tt(r_pick, r_hot[0], r_hot[1], ALU.add), r_picked)
                    dve.wait_ge(r_pos_ps, 1)
                    V.memset(r_pos[:, NP:NT, :], 0.0)
                    V.tensor_copy(r_pos[:, 0:NP, :], ps[:, 1, 0:NP * EXPERTS].rearrange("p (t e) -> p t e", t=NP))
                    link(V.tensor_copy(r_tot, ps[:, 1, NT * EXPERTS:(NT + 1) * EXPERTS]))
                    V.tensor_copy(r_pos[0:NS, NP, :], ps[0:NS, 1, NP * EXPERTS:NT * EXPERTS])
                    link(V.tensor_scalar(r_nb, r_tot, float(BLOCK), None, ALU.is_gt))
                    for c in range(2, MORE_PER_EXPERT + 1):
                        link(V.scalar_tensor_tensor(r_nb, r_tot, float(c * BLOCK), r_nb, ALU.is_gt, ALU.add))
                    link(V.tensor_tensor_scan(r_cum, T("ones")[:, 0:EXPERTS], r_nb, 0.0, ALU.mult, ALU.add))
                    V.tensor_copy(r_plan[:, 0:EXPERTS], T("experts"))
                    link(tt(r_owner3, rep(r_cum, MORE), b3(T("count"), EXPERTS), ALU.is_le))
                    link(V.tensor_reduce(r_plan[:, EXPERTS:N_BLOCKS], r_owner3, AX.X, ALU.add))
                    V.tensor_scalar(r_plan[:, EXPERTS:N_BLOCKS], r_plan[:, EXPERTS:N_BLOCKS], float(EXPERTS - 1), None, ALU.min)
                    link(tt(r_even, r_cum[:, EXPERTS - 1:EXPERTS].to_broadcast([P, MORE // 2]), T("count")[:, 0:MORE:2], ALU.is_gt))
                    link(V.tensor_reduce(r_plan[:, N_BLOCKS:], r_even, AX.X, ALU.add))
                    link(V.tensor_scalar(r_plan[:, N_BLOCKS:], r_plan[:, N_BLOCKS:], float(EXPERTS // 2 - 1), None, ALU.add))
                    V.tensor_copy(plan[:, :], r_plan[0:1, :])
                    link(tt(r_more, r_cum, r_nb, ALU.subtract))
                    link(V.scalar_tensor_tensor(r_more, r_more, float(BLOCK), T("more_row"), ALU.mult, ALU.add))
                    link(V.scalar_tensor_tensor(r_row, r_pos, float(BLOCK), rep(r_more, NT), ALU.is_ge, ALU.mult))
                    link(tt(r_row, r_row, r_pos, ALU.add))
                    link(tt(r_row, r_row, rep(T("first_row"), NT), ALU.add))
                    for c in range(TOP_K):
                        link(tt(r_hot[c], r_hot[c], r_row, ALU.mult))
                        link(V.tensor_reduce(r_rowf[:, :, c:c + 1], r_hot[c], AX.X, ALU.add))
                    V.tensor_copy(rows_u[:, :, :], r_rowf).then_inc(planned, 1)
                    dve.wait_ge(planned, 1)
                    last_pair = dve.value_load(plan[0:1, N_BLOCKS:N_BLOCKS + 1], min_val=EXPERTS // 2 - 1, max_val=N_BLOCKS // 2 - 1)

                    def dve_block(k, i, s):
                        dve.wait_ge(sil_sb, k + 1)
                        tt(hT[s].rearrange("p a n -> p (a n)"), sil[s], ps[:, 2 + s, 2 * BLOCK:], ALU.mult).then_inc(hT_sb, 1)
                        dve.wait_ge(y_ps, k + 1)
                        dve.wait_ge((y_out0, y_out1)[s], i * 16 + 16)
                        V.tensor_copy(yo[s][:, 0:SLAB], ps[:, 4 + 2 * s, :]).then_inc(y_sb, 1)

                    dve.sem_inc(y_sb, 3)
                    with dve.Fori(0, last_pair + 1) as i:
                        dve_block(i * 2, i, 0)
                        dve_block(i * 2 + 1, i, 1)
                    for t in tiles:
                        n = rows[t]
                        dve.wait_ge(y_init, t + 1)
                        dve.wait_ge(y_back[t], layer * (16 * TOP_K) + 16 * TOP_K)
                        for c, w in enumerate((r_w1, r_w2)):
                            link(V.scalar_tensor_tensor(x[0:n, t, :], yg[0:n, t, c, :], w[0:n, t:t + 1], x[0:n, t, :], ALU.mult, ALU.add))
                        layer_norm(t, 2, x)

                @block.tensor
                def _(pe):
                    due = Due()
                    mm = nc.tensor.matmul
                    tr = nc.tensor.transpose
                    idn = T("ident")

                    def turn_x(base):
                        for i in range(2 * NT):
                            t, hf = i // 2, i % 2
                            n = rows[t]
                            if base + i >= 4:
                                pe.wait_ge(xT_sb, max(base + i - 3, base))
                            for k in range(4):
                                c = (4 * hf + k) * P
                                m = tr(ps[:, 4 + i % 4, k * n:(k + 1) * n], x[0:n, t, c:c + P], idn[0:n, 0:n])
                            m.then_inc(xT_ps, 1)

                    turn_x(0)
                    pe.wait_ge(xT_sb, 2 * NT)
                    w_slab = (w_slab0, w_slab1, w_slab2)
                    for g in range(N_SLABS):
                        w = min(SLAB, D_IN - g * SLAB)
                        pe.wait_ge(w_slab[g % 3], 16 * (g // 3 + 1))
                        for t in tiles:
                            i, n = g * NT + t, rows[t]
                            if i >= 4:
                                pe.wait_ge(z_sb, i - 3)
                            for k in range(KD):
                                m = mm(ps[0:n, i % 4, 0:w], xTv[:, k, t * P:t * P + n], slab[g % 3][:, k, 0:w], start=(k == 0), stop=(k == KD - 1))
                            m.then_inc(z_ps, 1)
                    pe.wait_ge(ws_n, 16)
                    for h in range(HEADS):
                        m = tr(ps[:, 4, h * P:(h + 1) * P], ws_nat[:, h, :], idn)
                    m.then_inc(ws_ps, 1)
                    pe.wait_ge(ws_s8, 1)
                    for h in range(HEADS):
                        m = tr(ps[0:NS, 5, h * NS:(h + 1) * NS], ws_exp[0:NS, h, :], idn[0:NS, 0:NS])
                    m.then_inc(ws_ps, 1)
                    pe.wait_ge(f_gates, 1)
                    for t in tiles:
                        n = rows[t]
                        m = mm(ps[0:n, 7, t * HEADS:(t + 1) * HEADS], T("upper" if t < NP else "upper_s", n), th(lf)[0:n, t, 0:HEADS], start=True, stop=True)
                    m.then_inc(gate_ps, 1)
                    pe.wait_ge(va_ready, 1)
                    pe.wait_ge(ws_sb, 2)
                    pe.wait_ge(z_sb, NT * N_SLABS)
                    for t in tiles:
                        n = rows[t]
                        for h in range(HEADS):
                            v = COLS["a_v"] + h * HD
                            m = mm(ps[0:n, t if t < NP else 6, h * HD:(h + 1) * HD], (wsT if t < NP else wsTs)[0:n, h, 0:n], zt[0:n, t, v:v + HD], start=True, stop=True)
                    m.then_inc(a_ps, 1)

                    def turn_qk(t, q, k, bank, sem):
                        n = rows[t]
                        for a, name in enumerate((q, q, k, k)):
                            c = COLS[name] + a % 2 * P
                            m = tr(ps[:, bank, a * n:(a + 1) * n], zt[0:n, t, c:c + P], idn[0:n, 0:n])
                        m.then_inc(sem, 1)

                    def scores(t, sem):
                        n = rows[t]
                        for pair in range(PAIRS):
                            for par in range(2):
                                at = slice(par * HD, (par + 1) * HD)
                                m = mm(ps[0:n, 6 + par, pair * n:(pair + 1) * n], qkT[at, 2 + pair, 0:n], qkT[at, pair, 0:n], start=True, stop=True)
                        m.then_inc(sem, 1)

                    def sample_queries():
                        pe.wait_ge(qm_q, due(qm_q))
                        for h in range(HEADS):
                            m = tr(ps[:, 4, h * NS:(h + 1) * NS], qd2[0:NS, h, :], idn[0:NS, 0:NS])
                        m.then_inc(qm_ps, 1)

                    def mixed(t, state, sstate, w, val, sem):
                        n = rows[t]
                        if t == NP:
                            pe.wait_ge(qm_sb, due(qm_sb))
                            pe.wait_ge(s_in, 16 * 3 * DEC_BATCH)
                        for h in range(HEADS):
                            m = mm(ps[0:n, 4, h * w:(h + 1) * w], sw[0:n, h % 2 * 2 + h // 2, 0:n], val(h), start=True, stop=True)
                        if t < NP:
                            for pair in range(PAIRS):
                                for par in range(2):
                                    at = slice(par * HD, (par + 1) * HD)
                                    m = mm(ps[0:n, 6 + par, pair * w:(pair + 1) * w], qkT[at, pair, 0:n], state[at, pair, :], start=True, stop=True)
                        else:
                            for h in range(HEADS):
                                for bp in range(BP):
                                    m = mm(ps[0:n, 6, h * w:(h + 1) * w], qm[:, bp, h, :], sstate[:, bp, h, :], start=(bp == 0), stop=(bp == BP - 1))
                        m.then_inc(sem, 1)

                    def sample_update(w, val, place):
                        for h in range(HEADS):
                            pe.wait_ge(km_sb, due(km_sb))
                            for bp in range(BP):
                                m = mm(place(bp, h), km[0:NS, 2 * bp:2 * bp + 2, :].rearrange("p a b -> p (a b)"), val(h), start=True, stop=True)
                            m.then_inc(km_used, 1)

                    pe.wait_ge(rope_done, 1)
                    pe.wait_ge(gate_sb, 1)
                    for t in tiles:
                        n = rows[t]
                        lfd = lambda c: th(lf)[0:n, c, HEADS:]
                        for c in range(t if t < NP else 0):
                            mm(ps[0:n, 5, t * HEADS:(t + 1) * HEADS], T("ones"), lfd(c), start=(c == 0), stop=False)
                        m = mm(ps[0:n, 5, t * HEADS:(t + 1) * HEADS], T("upper" if t < NP else "upper_s", n), lfd(t), start=(t in (0, NP)), stop=True)
                    m.then_inc(d_cum, 1)
                    turn_qk(NP, "d_q", "d_k", 0, e_T)
                    pe.wait_ge(e_tot, 1)
                    mm(ps[:, 3, 0:DEC_BATCH * HEADS], T("after"), sufp, start=True, stop=True).then_inc(e_cumps, 1)
                    pe.wait_ge(e_Tsb, 1 + 2 * PAIRS)
                    kv = kbuf[:, :].rearrange("p (k c) -> p k c", k=KPP)
                    vv = vbuf[:, :].rearrange("p (k c) -> p k c", k=KPP)

                    def cache_scores(u):
                        r, pair = u // 2, u % 2
                        pe.wait_ge(e_ksb, u + 1)
                        if pair == 0 and r >= 1:
                            pe.wait_ge(e_rsb, r)
                        mm(ps[0:HQ, 1, :], qz[:, pair, r // 4, :], kTs[u % 2], start=(pair == 0), stop=(pair == 1)).then_inc(e_row, 1)

                    def turn_scores(r):
                        pe.wait_ge(e_rsb, r + 1)
                        if r % 4 == 0 and r > 0:
                            pe.wait_ge(e_pm, r // 4)
                        for a in range(4):
                            k = r % 4 * 4 + a
                            m = tr(ps[:, 2, k * HQ:(k + 1) * HQ], srow[r % 2][0:HQ, a * P:(a + 1) * P], idn[0:HQ, 0:HQ])
                        m.then_inc(e_s, 1)

                    def cache_values(j):
                        pe.wait_ge(v_in, layer * (16 * DEC_BATCH) + 16 * (j + 1))
                        pe.wait_ge(e_p, j + 1)
                        for k in range(KPP):
                            mm(ps[0:HQ, 3, 0:GW], pp[j % 2][:, k, :], vv[:, k, :], start=(k == 0), stop=False)
                        c = COLS["d_v"]
                        mm(ps[0:HQ, 3, 0:GW], pp[j % 2][0:NS, KPP, :], zt[0:NS, NP, c:c + GW], start=False, stop=True)
                        pe.wait_ge(e_lf, j + 1)
                        mm(ps[0:HQ, 3, GW:GW + 1], ptot, T("ones")[:, 0:1], start=True, stop=True).then_inc(e_pv, 1)

                    def cache_step(u):
                        i, g = u // 8, u % 8
                        j = i - 1
                        if i < DEC_BATCH:
                            if g == 0:
                                pe.wait_ge(k_in, layer * (16 * DEC_BATCH) + 16 * (i + 1))
                            if u >= 1:
                                pe.wait_ge(e_ksb, u)
                            for a in range(4):
                                m = tr(ps[:, 0, a * P:(a + 1) * P], kv[:, g // 2 * 4 + a, g % 2 * P:(g % 2 + 1) * P], idn)
                            m.then_inc(e_kps, 1)
                            if g > 0:
                                cache_scores(u - 1)
                            if g in (3, 5, 7):
                                turn_scores(4 * i + (g - 3) // 2)
                        if j >= 0 and g == 2:
                            pe.wait_ge(e_pm, j + 1)
                            if j >= 1:
                                pe.wait_ge(e_ym, j)
                            tr(ps[0:HQ, 3, MT:MT + P], pmax, idn).then_inc(e_mt, 1)
                        if j >= 0 and g == 4:
                            pe.wait_ge(e_dg, j + 1)
                            mm(ps[:, 3, BC:BC + HQ], T("ones", HQ), pdiag[0:HQ], start=True, stop=True).then_inc(e_bc, 1)
                        if g == 7:
                            if i < DEC_BATCH:
                                cache_scores(u)
                                if i > 0:
                                    pe.wait_ge(e_xs, i)
                                c = NEW + i % 2 * HQ
                                for pair in range(PAIRS):
                                    m = mm(ps[0:NS, 3, c:c + HQ], kTn[:, pair, :], qz[:, pair, i, :], start=(pair == 0), stop=(pair == 1))
                                m.then_inc(e_psum, 1)
                            if j >= 0:
                                cache_values(j)
                            if i < DEC_BATCH:
                                turn_scores(4 * i + 3)

                    steps = iter(range(CACHE_STEPS))

                    for t in tiles:
                        n = rows[t]
                        if t > 0:
                            pe.wait_ge(b_state, t)
                        turn_qk(t, "b_q", "b_k", 4, b_T)
                        cache_step(next(steps))
                        pe.wait_ge(b_Tsb, 2 * t + 2)
                        scores(t, b_sc)
                        if t == NP:
                            sample_queries()
                        val = lambda h: zt[0:n, t, COLS["b_v"] + h * HD:COLS["b_v"] + (h + 1) * HD]
                        cache_step(next(steps))
                        pe.wait_ge(b_sw, t + 1)
                        mixed(t, ret, rs, HD, val, b_out)
                        pe.wait_ge(b_kd, t + 1)
                        if t < NP:
                            for pair in range(PAIRS):
                                c = COLS["b_v"] + pair * P
                                m = mm(ps[:, 5, pair * P:(pair + 1) * P], kd[:, pair * P:(pair + 1) * P], zt[:, t, c:c + P], start=True, stop=True)
                            m.then_inc(b_up, 1)
                        else:
                            sample_update(HD, val, lambda bp, h: ps[:, 4 + bp // 2, (bp % 2 * HEADS + h) * HD:(bp % 2 * HEADS + h + 1) * HD])
                        cache_step(next(steps))
                    pe.wait_ge(b_state, NT)
                    for t in tiles:
                        n = rows[t]
                        W = HD + 1
                        if t > 0:
                            pe.wait_ge(c_cd, t)
                        turn_qk(t, "c_q", "c_k", 4, c_T)
                        pe.wait_ge(c_dg, t + 1)
                        m = mm(ps[0:n, 5, 0:HEADS * n], T("ones", n)[:, 0:n], diag[0:n, :, 0:n], start=True, stop=True)
                        m.then_inc(c_row, 1)
                        cache_step(next(steps))
                        pe.wait_ge(c_Tsb, 2 * t + 2)
                        scores(t, c_sc)
                        if t == NP:
                            sample_queries()
                        cache_step(next(steps))
                        pe.wait_ge(c_mt, t + 1)
                        mm(ps[0:n, 5, 0:2 * HEADS], T("last" if t < NP else "last_s", n), mtb[0:n, :], start=True, stop=True).then_inc(c_last, 1)
                        cache_step(next(steps))
                        val = lambda h: vx[0:n, h, :]
                        pe.wait_ge(c_sw, t + 1)
                        pe.wait_ge(c_vx, t + 1)
                        mixed(t, mem, cs, W, val, c_out)
                        pe.wait_ge(c_kd, t + 1)
                        if t < NP:
                            for pair in range(PAIRS):
                                m = mm(ps[:, 5, pair * 2 * W:(pair + 1) * 2 * W], kd[:, pair * P:(pair + 1) * P],
                                       vx[:, 2 * pair:2 * pair + 2, :].rearrange("p a b -> p (a b)"), start=True, stop=True)
                            m.then_inc(c_up, 1)
                        else:
                            sample_update(W, val, lambda bp, h: ps[:, 4 + bp, h * W:(h + 1) * W])
                            for bp in range(BP):
                                m = mm(ps[:, 7, CU + bp * HEADS:CU + (bp + 1) * HEADS], T("last_of", NS)[:, bp * P:(bp + 1) * P], ge[0:NS, HEADS:], start=True, stop=True)
                            m.then_inc(c_up, 1)
                        cache_step(next(steps))
                    pe.wait_ge(c_cd, NT)
                    for t in range(NP):
                        if t >= 2:
                            pe.wait_ge(d_Tsb, 2 * t - 2)
                        turn_qk(t, "d_q", "d_k", 4 + 2 * (t % 2), d_T)
                    for h in range(HEADS):
                        pe.wait_ge(d_dg, h + 1)
                        if h >= 2:
                            pe.wait_ge(d_ncr, h - 1)
                        mm(ps[:, 5 + 2 * (h % 2), :], T("ones"), dg[h % 2].rearrange("p a b -> p (a b)"), start=True, stop=True).then_inc(d_row, 1)
                    pe.wait_ge(d_Tsb, 2 * NP)

                    def logits(m_):
                        c, h = m_ // HEADS, m_ % HEADS
                        w = (c + 1) * P
                        at = slice(h % 2 * HD, (h % 2 + 1) * HD)
                        if m_ >= 2:
                            pe.wait_ge(d_lgx, m_ - 1)
                        mm(ps[:, 4 + 2 * (m_ % 2), 0:w], qTa[at, h // 2, c * P:(c + 1) * P], kTa[at, h // 2, 0:w], start=True, stop=False)
                        mm(ps[:, 4 + 2 * (m_ % 2), c * P:w], idn, T("neg_q"), start=False, stop=True).then_inc(d_lg, 1)

                    def values(m_):
                        c, h = m_ // HEADS, m_ % HEADS
                        pe.wait_ge(d_pTsb, m_ + 1)
                        if c >= 1 and h == 0:
                            pe.wait_ge(d_y, c)
                        v = COLS["d_v"] + h * HD
                        for s in range(c + 1):
                            m = mm(ps[:, 7, h * HD:(h + 1) * HD], pT[m_ % 2][:, s, :], zt[:, s, v:v + HD], start=(s == 0), stop=(s == c))
                        m.then_inc(d_o, 1)

                    pe.wait_ge(d_ncr, HEADS)
                    cache_step(next(steps))
                    for m_ in range(NP * HEADS + 2):
                        if m_ < NP * HEADS:
                            logits(m_)
                        if m_ >= 2:
                            values(m_ - 2)
                        if 1 <= m_ <= NP * HEADS:
                            pe.wait_ge(d_exp, m_)
                            for s in range((m_ - 1) // HEADS + 1):
                                m = tr(ps[:, 5, s * P:(s + 1) * P], lg[(m_ - 1) % 2][:, s * P:(s + 1) * P], idn)
                            m.then_inc(d_pT, 1)
                        if m_ < NP * HEADS:
                            for _ in range(2):
                                cache_step(next(steps))
                    for u in steps:
                        cache_step(u)
                    pe.wait_ge(e_ym, DEC_BATCH)
                    for i in range(DEC_BATCH):
                        c = NS - DEC_SEQ - DEC_SEQ * i
                        m = mm(ps[0:NS, 0, 0:GW], T("to_row", HQ)[:, c:c + NS], ym[0:HQ, i], start=(i == 0), stop=(i == DEC_BATCH - 1))
                    m.then_inc(e_fin, 1)
                    pe.wait_ge(merged, 1)
                    for i in range(2 * NT):
                        t, hf = i // 2, i % 2
                        n = rows[t]
                        if i >= 4:
                            pe.wait_ge(m_sb, i - 3)
                        for k in range(4):
                            kk = 4 * hf + k
                            c = COLS[MERGED[kk // 2]] + kk % 2 * P
                            m = tr(ps[:, 4 + i % 4, k * n:(k + 1) * n], zt[0:n, t, c:c + P], idn[0:n, 0:n])
                        m.then_inc(m_ps, 1)
                    pe.wait_ge(m_sb, 2 * NT)
                    pe.wait_ge(wout_in, 32)
                    for t in tiles:
                        n = rows[t]
                        bank = 2 * (t % 2)
                        if t >= 2:
                            pe.wait_ge(y_free, t - 1)
                        for hf in range(2):
                            for k in range(KD):
                                m = mm(ps[0:n, bank + hf, :], xTv[:, k, t * P:t * P + n], slab[hf][:, k, :], start=(k == 0), stop=(k == KD - 1))
                        m.then_inc(o_ps, 1)
                    pe.wait_ge(ln_n, NT)
                    turn_x(2 * NT)
                    pe.wait_ge(xT_sb, 4 * NT)
                    pe.wait_ge(r_w, 16 * 7)
                    NR = GROUPS + EXPERTS
                    for t in tiles:
                        n = rows[t]
                        for k in range(KD):
                            m = mm(ps[0:n, 0, t * NR:(t + 1) * NR], xTv[:, k, t * P:t * P + n], wr[:, k, :], start=(k == 0), stop=(k == KD - 1))
                    m.then_inc(r_ps, 1)

                    pe.wait_ge(r_picked, 1)
                    for t in tiles:
                        n = rows[t]
                        out = ps[0:n, 1, t * EXPERTS:(t + 1) * EXPERTS]
                        for c in range(t):
                            mm(out, T("ones")[:, 0:n], r_pick[:, c, :], start=(c == 0), stop=False)
                        mm(out, T("before", n)[:, 0:n], r_pick[0:n, t, :], start=(t == 0), stop=True)
                    for t in tiles:
                        m = mm(ps[:, 1, NT * EXPERTS:(NT + 1) * EXPERTS], T("ones", rows[t]), r_pick[0:rows[t], t, :], start=(t == 0), stop=(t == NP))
                    m.then_inc(r_pos_ps, 1)
                    pe.wait_ge(planned, 1)
                    last_pair = pe.value_load(plan[0:1, N_BLOCKS:N_BLOCKS + 1], min_val=EXPERTS // 2 - 1, max_val=N_BLOCKS // 2 - 1)

                    def pe_turn(i, s):
                        pe.wait_ge((xg_in0, xg_in1)[s], i * 16 + 16)
                        for hf in range(2):
                            for k in range(4):
                                m = tr(ps[:, hf, k * P:(k + 1) * P], xg[s][:, 4 * hf + k::KD], idn)
                            m.then_inc(xgT_ps, 1)

                    def pe_h(i, k, s):
                        pe.wait_ge((w13_in0, w13_in1)[s], i * 32 + 32)
                        pe.wait_ge(xgT_sb, k * 2 + 2)
                        for w in range(2):
                            for c in range(2):
                                at = (2 * w + c) * BLOCK
                                for q in range(KD):
                                    m = mm(ps[:, 2 + s, at:at + BLOCK], w13[s][:, w, q, c::2], xgT[s][:, q, :], start=(q == 0), stop=(q == KD - 1))
                        m.then_inc(h_ps, 1)

                    def pe_y(i, k, s):
                        pe.wait_ge((w2_in0, w2_in1)[s], i * 16 + 16)
                        pe.wait_ge(hT_sb, k + 1)
                        pe.wait_ge(y_sb, k * 2 + 1)
                        for hf in range(2):
                            for c in range(2):
                                m = mm(ps[:, 4 + 2 * s + hf, :], hT[s][:, c, :], w2[s][:, c, hf * SLAB:(hf + 1) * SLAB], start=(c == 0), stop=(c == 1))
                        m.then_inc(y_ps, 1)

                    pe.wait_ge(y_free, NT)
                    pe_turn(0, 0)
                    with pe.Fori(0, last_pair) as i:
                        pe_h(i, i * 2, 0)
                        pe_turn(i, 1)
                        pe_y(i, i * 2, 0)
                        pe_h(i, i * 2 + 1, 1)
                        pe_turn(i + 1, 0)
                        pe_y(i, i * 2 + 1, 1)
                    lp = last_pair
                    pe_h(lp, lp * 2, 0)
                    pe_turn(lp, 1)
                    pe_y(lp, lp * 2, 0)
                    pe_h(lp, lp * 2 + 1, 1)
                    pe_y(lp, lp * 2 + 1, 1)

            nc.all_engine_barrier()
            nc.sync.sem_clear(range(signals[0].num, signals[-1].num + 1))
            nc.all_engine_barrier()

        with nc.Block() as block:
            @block.sync
            def _(sp):
                sp.dma_start(d["y_prompt"].rearrange("o (t p) n -> p (o t) n", p=P), x[:, 0:NP, :]).then_inc(s_x0, 16)
                sp.dma_start(d["y_sample"].rearrange("b s n -> (b s) n"), x[0:NS, NP, :]).then_inc(s_x0, 16)
                sp.wait_ge(s_x0, 64)

_INS = ["x_prompt", "x_sample", "cache_k", "cache_v", "cache_logf", "page_table", "state_ret", "state_mlstm_c",
        "state_mlstm_n", "state_mlstm_m", "w_in", "b_in", "w_s", "b_s", "g_mix", "w_out", "ln1_g", "ln1_b",
        "w_rg", "b_rg", "w_re", "b_re", "w1", "w3", "w2", "ln2_g", "ln2_b"]
_KV = (HEADS, HD)
_OUTS = [("y_prompt", (1, SEQ, D_MODEL)), ("y_sample", (DEC_BATCH, DEC_SEQ, D_MODEL)),
         ("k_prompt", (DEPTH, 1, SEQ) + _KV), ("v_prompt", (DEPTH, 1, SEQ) + _KV), ("logf_prompt", (DEPTH, 1, SEQ, HEADS)),
         ("ret_prompt", (DEPTH, 1, HEADS, HD, HD)), ("mlstm_c_prompt", (DEPTH, 1, HEADS, HD, HD)),
         ("mlstm_n_prompt", (DEPTH, 1, HEADS, HD)), ("mlstm_m_prompt", (DEPTH, 1, HEADS)),
         ("k_sample", (DEPTH, DEC_BATCH, DEC_SEQ) + _KV), ("v_sample", (DEPTH, DEC_BATCH, DEC_SEQ) + _KV),
         ("logf_sample", (DEPTH, DEC_BATCH, DEC_SEQ, HEADS)),
         ("ret_sample", (DEPTH, DEC_BATCH, HEADS, HD, HD)), ("mlstm_c_sample", (DEPTH, DEC_BATCH, HEADS, HD, HD)),
         ("mlstm_n_sample", (DEPTH, DEC_BATCH, HEADS, HD)), ("mlstm_m_sample", (DEPTH, DEC_BATCH, HEADS)),
         ("chunk_v_sample", (DEPTH, DEC_BATCH, DEC_SEQ) + _KV)]

def kernel(**inputs):
    import concourse.bacc as _bacc
    from concourse.bass_utils import run_bass_kernel_spmd as _run

    nc = _bacc.Bacc("TRN2", target_bir_lowering=False, num_devices=1)
    arrays, d = {}, {}
    for name in _INS + ["tables"]:
        a = np.ascontiguousarray(TABLES if name == "tables" else inputs[name])
        if name in ("w1", "w3", "w2"):
            a = a.reshape((DEPTH * EXPERTS,) + a.shape[2:])
        arrays["in_" + name] = a
        d[name] = nc.dram_tensor("in_" + name, a.shape, mybir.dt.from_np(a.dtype), kind="ExternalInput").ap()
    for name, shape in _OUTS:
        d[name] = nc.dram_tensor("out_" + name, shape, F32, kind="ExternalOutput").ap()
    decoder(nc, d)
    r = _run(nc, [arrays], core_ids=[0])
    return tuple(r.results[0]["out_" + name] for name, _ in _OUTS)
```

```python
import numpy as np
from contextlib import ExitStack

import concourse.bass as bass
from concourse import mybir
from concourse.alu_op_type import AluOpType as ALU

F32 = mybir.dt.float32
U32 = mybir.dt.uint32
I32 = mybir.dt.int32
ACT = mybir.ActivationFunctionType
AX = mybir.AxisListType

P = 128
D_MODEL = 1024
SEQ = 512
DEPTH = 2
DEC_BATCH = 8
DEC_SEQ = 8
PAST_LEN = 2048
PAGE_SIZE = 128
N_PAGES = PAST_LEN // PAGE_SIZE
N_POOL = (5 * DEC_BATCH * N_PAGES) // 4
HEADS = 4
HD = 64
GW = HEADS * HD
PAIRS = HEADS // 2
EXPERTS = 16
GROUPS = 4
D_EXPERT = D_MODEL // 4
ALPHA = (2 * DEPTH) ** 0.25
LN_EPS = 1e-5
RMS_EPS = 1e-6
SCALE = HD ** -0.5
KD = D_MODEL // P
NT = SEQ // P + 1
NP = NT - 1
NS = DEC_BATCH * DEC_SEQ
TOK = SEQ + NS
TOP_K = 2
BLOCK = P
MORE = TOP_K * TOK // (BLOCK + 1)
MORE_PER_EXPERT = -(-TOK // BLOCK) - 1
N_BLOCKS = EXPERTS + MORE
assert MORE % 2 == 0
KPP = PAST_LEN // P
RPP = PAGE_SIZE // KPP
BP = DEC_BATCH // 2
NEG = -1e30
RESET = -3e38

COLS, _at = {}, 0
for _name, _w in (("a_u", GW), ("a_v", GW), ("b_q", GW), ("b_k", GW), ("b_v", GW), ("b_g", GW),
                  ("c_q", GW), ("c_k", GW), ("c_v", GW), ("c_o", GW), ("c_i", HEADS), ("c_f", HEADS),
                  ("d_q", GW), ("d_k", GW), ("d_v", GW), ("d_f", HEADS)):
    COLS[_name] = _at
    _at += _w
D_IN = _at
SLAB = 512
N_SLABS = -(-D_IN // SLAB)
SLAB_ORDER = (0, 1, 5, 6, 2, 3, 4)
assert sorted(SLAB_ORDER) == list(range(N_SLABS))
MERGED = ("a_u", "b_q", "c_q", "d_q")

def make_tables():
    f = np.float32
    parts = []
    i = np.arange(P)
    s, t = i[:, None], i[None, :]
    log_g = np.log1p(-np.exp2(-5.0 - np.arange(HEADS)))
    j = np.arange(NS)
    block, step = j // DEC_SEQ, j % DEC_SEQ
    same = block[:, None] == block[None, :]
    up_s = same & (j[:, None] <= j[None, :])

    def put(name, a):
        a = np.asarray(a, np.float64)
        a = a.reshape(a.shape[0], -1)
        full = np.zeros((P, a.shape[1]), f)
        full[:a.shape[0]] = a.astype(f)
        parts.append((name, full))

    put("ident", np.eye(P))
    put("sub_row", (i % RPP)[:, None])
    put("ones", np.ones((P, P)))
    put("upper", s <= t)
    put("after", s > t)
    put("neg_t", np.where(s <= t, 0.0, NEG))
    put("neg_q", np.where(t <= s, 0.0, NEG))
    put("last", np.repeat((i == P - 1)[:, None], P, 1))
    dec = np.where(s <= t, np.exp(log_g[:, None, None] * np.maximum(t - s, 0)), 0.0)
    by_parity = [2 * pair + par for par in range(2) for pair in range(PAIRS)]
    put("dec", dec[by_parity].transpose(1, 0, 2))
    reset = np.zeros((P, HEADS, P))
    reset[:, :, 0] = RESET
    put("reset", reset)
    put("upper_s", up_s)
    put("lower_s", up_s.T)
    put("neg_ts", np.where(up_s, 0.0, NEG))
    put("last_s", (j[:, None] == 8 * block[None, :] + DEC_SEQ - 1))
    dec_s = np.where(up_s, np.exp(log_g[:, None, None] * np.maximum(j[None, :] - j[:, None], 0)), 0.0)
    put("dec_s", dec_s[by_parity].transpose(1, 0, 2))
    reset = np.zeros((NS, HEADS, NS))
    reset[:, :, ::DEC_SEQ] = RESET
    put("reset_s", reset)
    half = np.repeat(np.arange(2), HD)
    put("last_of", (j[:, None, None] == DEC_SEQ * (2 * np.arange(BP)[:, None] + half) + DEC_SEQ - 1))
    put("seq_of", (2 * np.arange(BP)[:, None] + half[:, None, None] == block))
    put("in_seq", block[:, None] == np.arange(DEC_BATCH))
    n_half = HD // 2
    inv = f(10000.0) ** (-np.arange(n_half, dtype=f) / f(n_half))
    pos = np.zeros((P, NT), f)
    pos[:, :NP] = i[:, None] + P * np.arange(NP)
    pos[:NS, NP] = PAST_LEN + step
    ang = (pos[:, :, None] * inv.astype(f)).astype(f).astype(np.float64)
    put("cos", np.cos(ang))
    put("sin", np.sin(ang))
    put("q_dec", np.exp(log_g[by_parity] * (i[:, None] + 1.0)))
    put("q_dec_s", np.exp(log_g * (step[:, None] + 1.0)))
    put("k_dec", np.exp(log_g * (P - 1.0 - i[:, None])) * SCALE)
    put("k_dec_s", np.exp(log_g * (DEC_SEQ - 1.0 - step[:, None])) * SCALE)
    put("c_dec", np.exp(log_g.reshape(PAIRS, 2).T * P)[half])
    put("c_dec_s", np.tile(np.exp(log_g * DEC_SEQ), (P, 1)))
    put("start", np.where(i[:, None] == 0, 0.0, NEG))
    put("start_s", np.where(step[:, None] == 0, 0.0, NEG))

    hq = np.arange(HEADS * DEC_SEQ)
    put("own_head", (hq[:, None] // DEC_SEQ) == (np.arange(GW)[None, :] // HD))
    put("to_row", np.arange(2 * NS - DEC_SEQ)[None, :] == NS - DEC_SEQ + hq[:, None] % DEC_SEQ)
    put("ln_eps", np.full((P, 1), LN_EPS))
    put("rms_eps", np.full((P, 1), RMS_EPS))
    put("rank", np.tile(np.arange(GROUPS, 0, -1), (P, 1)))
    put("before", s < t)
    e = np.arange(EXPERTS)
    put("first_row", np.tile(e * BLOCK, (P, 1)))
    put("more_row", np.tile(EXPERTS * BLOCK - BLOCK - e * BLOCK, (P, 1)))
    put("count", np.tile(np.arange(MORE), (P, 1)))
    put("experts", np.tile(e, (P, 1)))
    at, cols = 0, {}
    for name, a in parts:
        cols[name] = (at, a.shape[1])
        at += a.shape[1]
    return cols, np.concatenate([a for _, a in parts], 1)

TABLE_COLS, TABLES = make_tables()
FIRST_TABLES = P + 1

class Due:

    def __init__(self):
        self.n = {}

    def __call__(self, sem, k=1):
        self.n[sem.name] = self.n.get(sem.name, 0) + k
        return self.n[sem.name]

def b3(ap, n):
    return ap.unsqueeze(2).to_broadcast([ap.shape[0], ap.shape[1], n])

def rep(ap, n):
    return ap.unsqueeze(1).to_broadcast([ap.shape[0], n, ap.shape[1]])

def decoder(nc, d):
    ctx = ExitStack()
    with ctx:
        def sb(name, shape, dt=F32):
            return ctx.enter_context(nc.sbuf_tensor(name, shape, dt))

        signals = []

        def sig(name):
            s = ctx.enter_context(nc.semaphore(name))
            signals.append(s)
            return s

        tab = sb("tab", [P, TABLES.shape[1]])

        def T(name, n=P):
            at, w = TABLE_COLS[name]
            return tab[0:n, at:at + w]

        x = sb("x", [P, NT, D_MODEL])
        xT = sb("xT", [P, KD * TOK])
        z = sb("z", [P, NT * D_IN])
        ring = sb("ring", [P, 3, KD * SLAB])
        kbuf = sb("kbuf", [P, KPP * GW])
        vbuf = sb("vbuf", [P, KPP * GW])
        wsT = sb("wsT", [P, HEADS, P])
        wsTs = sb("wsTs", [NS, HEADS, NS])
        ws8 = sb("ws8", [NS, HEADS, DEC_SEQ])
        bs = sb("bs", [P, HEADS])
        bss = sb("bss", [NS, HEADS])
        gmix = sb("gmix", [P, KD])
        ret = sb("ret", [P, PAIRS, HD])
        mem = sb("mem", [P, PAIRS, HD + 1])
        small = sb("small", [P, 600])
        idx_f = sb("idx_f", [P, DEC_BATCH])
        idx_u = sb("idx_u", [P, DEC_BATCH], U32)
        idx_k = sb("idx_k", [P, 2, DEC_BATCH], U32)
        pages = sb("pages", [P, DEC_BATCH], I32)

        rows_u = sb("rows_u", [P, NT, TOP_K], U32)
        plan = sb("plan", [1, N_BLOCKS + 1], I32)
        zero = sb("zero", [P, P])
        xd = nc.dram_tensor("expert_in", (N_BLOCKS * BLOCK, D_MODEL), F32, kind="Internal").ap()
        yd = nc.dram_tensor("expert_out", (N_BLOCKS * BLOCK, D_MODEL), F32, kind="Internal").ap()

        ps = ctx.enter_context(nc.psum_tensor("ps", [P, 8, SLAB], F32))

        zt = z[:, :].rearrange("p (t c) -> p t c", t=NT)
        xTv = xT[:, :].rearrange("p (k n) -> p k n", k=KD)

        def Z(t, name, n=P, w=GW):
            c = COLS[name]
            return zt[0:n, t, c:c + w]

        def Zall(name, w=GW):
            c = COLS[name]
            return zt[:, :, c:c + w]

        cut = [0]

        def stat(w):
            cut[0] += w
            assert cut[0] <= 600, cut[0]
            return small[:, cut[0] - w:cut[0]]

        def carve(tensor, start, *dims):
            n = int(np.prod(dims))
            v = tensor[:, start:start + n]
            if len(dims) == 2:
                v = v.rearrange("p (a b) -> p a b", b=dims[1])
            if len(dims) == 3:
                v = v.rearrange("p (a b c) -> p a b c", b=dims[1], c=dims[2])
            return v

        r2 = ring[:, 2, :]
        qkT = carve(r2, 512, 4, P)
        sw = carve(r2, 1024, HEADS, P)
        wexp = carve(r2, 1536, HEADS, P)
        mrow = carve(r2, 2048, HEADS, P)
        diag = carve(r2, 2560, HEADS, P)
        kd = carve(r2, 3072, GW)
        vx = carve(r2, 3328, HEADS, HD + 1)
        mix = carve(r2, 3588, HEADS, HD + 1)
        mrow_flat = mrow.rearrange("p a b -> p (a b)")
        ws_nat = carve(vbuf, D_IN, HEADS, P)
        ws_exp = carve(kbuf, 3 * NT * GW, HEADS, NS)
        tmp_a, tmp_b, tmp_c = [carve(kbuf, i * NT * GW, NT, GW) for i in range(3)]
        sq_all = carve(xT, 0, NT, GW)
        rs = carve(xT, 0, BP, HEADS, HD)
        cs = carve(xT, 1024, BP, HEADS, HD + 1)
        qm = carve(xT, 2064, BP, HEADS, NS)
        km = carve(xT, 3088, DEC_BATCH, HD)
        qd2 = carve(xT, 3600, HEADS, 2 * HD)
        qTa = carve(xT, 2064, PAIRS, SEQ)
        kTa = carve(xT, 3088, PAIRS, SEQ)
        sq_t = carve(xT, 4112, GW)
        n_sum = carve(xT, 4368, 4 * NT * HEADS)
        pT = [carve(xT, i * SLAB, 4, P) for i in range(2)]
        lg = [carve(r2, i * SLAB, SEQ) for i in range(2)]
        dg = [carve(r2, (2 + i) * SLAB, 4, P) for i in range(2)]
        ncr = carve(r2, 2048, HEADS, SEQ)
        NK = KPP + 1
        HQ = HEADS * DEC_SEQ
        r01 = ring[:, 0:2, :].rearrange("p s c -> p (s c)")
        xs = [carve(r01, i * NK * HQ, NK, HQ) for i in range(2)]
        pp = [carve(r01, (2 + i) * NK * HQ, NK, HQ) for i in range(2)]
        kTs = [carve(r01, 2176 + i * SLAB, SLAB) for i in range(2)]
        srow = [carve(r01, 3200 + i * SLAB, SLAB) for i in range(2)]
        qz = carve(r01, 4224, PAIRS, DEC_BATCH, HQ)
        newb = carve(r01, 4736, DEC_BATCH, HEADS, DEC_SEQ)
        kTn = carve(r01, 4992, PAIRS, NS)
        sfx = carve(r01, 5120, DEC_BATCH, KPP, HEADS)
        lfg = carve(r01, 5632, DEC_BATCH, KPP, HEADS)
        ym = carve(r01, 6144, DEC_BATCH, GW)

        xg = [carve(z, i * 1024, D_MODEL) for i in range(2)]
        xgT = [carve(z, 2048 + i * 1024, KD, BLOCK) for i in range(2)]
        hT = [carve(z, 4096 + i * 256, 2, BLOCK) for i in range(2)]
        sil = [carve(z, 4608 + i * 256, 2 * BLOCK) for i in range(2)]
        yo = [carve(z, 5120 + i * 1024, D_MODEL) for i in range(2)]
        wr = carve(z, 7168, KD, GROUPS + EXPERTS)
        br = carve(z, 7328, GROUPS + EXPERTS)
        rt = carve(z, 7348, NT, GROUPS + EXPERTS)
        yg = carve(z, 0, NT, TOP_K, D_MODEL)
        moe_small = carve(z, 10240, 2000)

        r_at = [0]

        def rview(*dims):
            n = int(np.prod(dims))
            r_at[0] += n
            assert r_at[0] <= 2000
            return carve(moe_small, r_at[0] - n, *dims)

        r_gm, r_gw, r_v1, r_v2, r_vd, r_ex, r_w1, r_w2, r_m = [rview(NT) for _ in range(9)]
        r_goh, r_gd, r_ge, r_el, r_oh1, r_oh2, r_e2l = [rview(NT, 4) for _ in range(7)]
        r_t16 = rview(NT, GROUPS, 4)
        r_hot = [rview(NT, EXPERTS) for _ in range(TOP_K)]
        r_pick = rview(NT, EXPERTS)
        r_pos, r_row = rview(NT, EXPERTS), rview(NT, EXPERTS)
        r_sums = rview(NT, EXPERTS)
        r_nb, r_cum, r_more = [rview(EXPERTS) for _ in range(3)]
        n_stats, n_mv, n_rs = rview(NT, 12), rview(NT, 2), rview(NT, 2)
        r_owner3 = rview(MORE, EXPERTS)
        r_plan = rview(N_BLOCKS + 1)
        r_even = rview(MORE // 2)
        r_rowf = rview(NT, TOP_K)

        w13 = [ring[:, s, :].rearrange("p (w k f) -> p w k f", w=2, k=KD) for s in range(2)]
        w2 = [ring[:, 2, s * 2048:(s + 1) * 2048].rearrange("p (f n) -> p f n", f=2) for s in range(2)]
        slab = [ring[:, s, :].rearrange("p (k n) -> p k n", k=KD) for s in range(3)]

        CACHE_STEPS = 8 * (DEC_BATCH + 1)
        B_STEPS, C_STEPS, D_STEPS = (1, 1, 1), (1, 1, 2, 1), (1, 1)
        MT, BC, NEW = 260, 388, 420
        CU = HEADS * (HD + 1)
        rows = [P] * NP + [NS]
        tiles = range(NT)

        s_tab = ctx.enter_context(nc.semaphore("tables_loaded"))
        s_rest = ctx.enter_context(nc.semaphore("more_tables_loaded"))
        s_slab = ctx.enter_context(nc.semaphore("first_slab_in"))
        s_x0 = ctx.enter_context(nc.semaphore("tokens_loaded"))
        s_fill = ctx.enter_context(nc.semaphore("expert_in_filled"))
        with nc.Block() as block:
            @block.sync
            def _(sp):
                sp.dma_start(tab[:, 0:FIRST_TABLES], d["tables"][:, 0:FIRST_TABLES]).then_inc(s_tab, 16)
                for i in range(N_PAGES):
                    sp.dma_start(pages[i * RPP:(i + 1) * RPP, :],
                                 d["page_table"][:, i:i + 1].rearrange("b o -> o b").to_broadcast([RPP, DEC_BATCH]),
                                 allow_slow_non_contiguous=True).then_inc(s_tab, 16)
                sp.dma_start(x[:, 0:NP, :], d["x_prompt"].rearrange("o (t p) n -> p (o t) n", p=P)).then_inc(s_x0, 16)
                sp.dma_start(x[0:NS, NP, :], d["x_sample"].rearrange("b s n -> (b s) n")).then_inc(s_x0, 16)
                sp.dma_start(slab[0][:, :, :], d["w_in"][0].rearrange("(k p) c -> p k c", p=P)[:, :, 0:SLAB]).then_inc(s_slab, 16)
                sp.dma_start(tab[:, FIRST_TABLES:], d["tables"][:, FIRST_TABLES:]).then_inc(s_rest, 16)
                sp.wait_ge(s_x0, 32)

            @block.vector
            def _(dve):
                dve.memset(zero[:, :], 0.0)
                dve.memset(x[NS:P, NP, :], 0.0)
                dve.memset(zt[NS:P, NP, :], 0.0)
                dve.wait_ge(s_tab, 16 * (1 + N_PAGES))
                dve.tensor_scalar(idx_f[:, :], pages[:, :], float(RPP), T("sub_row"), ALU.mult, ALU.add)

        xT_ps = sig("xT_ps")
        xT_sb = sig("xT_sb")
        w_slab0 = sig("w_slab0")
        w_slab1 = sig("w_slab1")
        w_slab2 = sig("w_slab2")
        z_ps = sig("z_ps")
        z_sb = sig("z_sb")
        bias_in = sig("bias_in")
        gate_in = sig("gate_in")
        gelu_done = sig("gelu_done")
        silu_done = sig("silu_done")
        sigm_done = sig("sigm_done")
        norm_sum = sig("norm_sum")
        norm_rs = sig("norm_rs")
        va_ready = sig("va_ready")
        ws_ps = sig("ws_ps")
        ws_n = sig("ws_n")
        ws_s8 = sig("ws_s8")
        ws_sb = sig("ws_sb")
        a_ps = sig("a_ps")
        rope_done = sig("rope_done")
        chain_v = sig("chain_v")
        chain_a = sig("chain_a")
        b_T = sig("b_T")
        b_Tsb = sig("b_Tsb")
        b_sc = sig("b_sc")
        b_sw = sig("b_sw")
        b_out = sig("b_out")
        b_kd = sig("b_kd")
        b_up = sig("b_up")
        b_state = sig("b_state")
        s_in = sig("s_in")
        qm_q = sig("qm_q")
        qm_ps = sig("qm_ps")
        qm_sb = sig("qm_sb")
        km_sb = sig("km_sb")
        km_used = sig("km_used")
        idx_set = sig("idx_set")
        f_in = sig("f_in")
        f_exp = sig("f_exp")
        f_gates = sig("f_gates")
        gate_ps = sig("gate_ps")
        gate_sb = sig("gate_sb")
        c_T = sig("c_T")
        c_Tsb = sig("c_Tsb")
        c_dg = sig("c_dg")
        c_row = sig("c_row")
        c_t = sig("c_t")
        c_w = sig("c_w")
        c_exps = sig("c_exps")
        c_mt = sig("c_mt")
        c_last = sig("c_last")
        c_gin = sig("c_gin")
        c_gs = sig("c_gs")
        c_sc = sig("c_sc")
        c_sw = sig("c_sw")
        c_vx = sig("c_vx")
        c_out = sig("c_out")
        c_kd = sig("c_kd")
        c_up = sig("c_up")
        c_cd = sig("c_cd")
        c_free = sig("c_free")
        d_T = sig("d_T")
        d_Tsb = sig("d_Tsb")
        d_cum = sig("d_cum")
        d_dg = sig("d_dg")
        d_row = sig("d_row")
        d_ncr = sig("d_ncr")
        d_lg = sig("d_lg")
        d_lgx = sig("d_lgx")
        d_exp = sig("d_exp")
        d_pT = sig("d_pT")
        d_pTsb = sig("d_pTsb")
        d_o = sig("d_o")
        d_y = sig("d_y")
        e_T = sig("e_T")
        e_Tsb = sig("e_Tsb")
        e_kps = sig("e_kps")
        e_row = sig("e_row")
        e_rsb = sig("e_rsb")
        e_ksb = sig("e_ksb")
        e_s = sig("e_s")
        e_pm = sig("e_pm")
        e_mt = sig("e_mt")
        e_dg = sig("e_dg")
        e_bc = sig("e_bc")
        e_xs = sig("e_xs")
        e_p = sig("e_p")
        e_psum = sig("e_psum")
        e_pv = sig("e_pv")
        e_fin = sig("e_fin")
        e_lf = sig("e_lf")
        e_cumps = sig("e_cumps")
        e_cumsb = sig("e_cumsb")
        e_ym = sig("e_ym")
        e_tot = sig("e_tot")
        rms_s = sig("rms_s")
        rms_r = sig("rms_r")
        merged = sig("merged")
        m_ps = sig("m_ps")
        m_sb = sig("m_sb")
        wout_in = sig("wout_in")
        o_ps = sig("o_ps")
        o_var = sig("o_var")
        o_rstd = sig("o_rstd")
        ln_n = sig("ln_n")
        n_var = sig("n_var")
        n_normed = sig("n_normed")
        n_scaled = sig("n_scaled")
        n_done = sig("n_done")
        ln_par = sig("ln_par")
        h_ps = sig("h_ps")
        sil_sb = sig("sil_sb")
        y_ps = sig("y_ps")
        w13_in0 = sig("w13_in0")
        w13_in1 = sig("w13_in1")
        w2_in0 = sig("w2_in0")
        w2_in1 = sig("w2_in1")
        r_ps = sig("r_ps")
        r_w = sig("r_w")
        r_exp = sig("r_exp")
        r_lg = sig("r_lg")
        r_e2 = sig("r_e2")
        r_e2x = sig("r_e2x")
        stored = sig("stored")
        rs_out = sig("rs_out")
        cs_out = sig("cs_out")
        y_init = sig("y_init")
        x_taken = sig("x_taken")
        y_free = sig("y_free")
        r_picked = sig("r_picked")
        r_pos_ps = sig("r_pos_ps")
        planned = sig("planned")
        xg_in0 = sig("xg_in0")
        xg_in1 = sig("xg_in1")
        xgT_ps = sig("xgT_ps")
        xgT_sb = sig("xgT_sb")
        hT_sb = sig("hT_sb")
        y_out0 = sig("y_out0")
        y_out1 = sig("y_out1")
        y_sb = sig("y_sb")
        y_stored = sig("y_stored")
        k_in = [ctx.enter_context(nc.semaphore(f"k_gathered{i}")) for i in range(2)]
        v_in = ctx.enter_context(nc.semaphore("v_gathered"))
        l_in = ctx.enter_context(nc.semaphore("logf_gathered"))
        x_sent = ctx.enter_context(nc.semaphore("tokens_sent"))
        y_back = [ctx.enter_context(nc.semaphore(f"outputs_back{t}")) for t in range(NT)]

        s_sum = stat(NT * HEADS)
        s_rstd = stat(NT * HEADS)
        ff = stat(NT * 2 * HEADS)
        fa = stat(NT * 2 * HEADS)
        fe = stat(NT * 2 * HEADS)
        lf = stat(NT * 2 * HEADS)
        cum = stat(NT * HEADS)
        gi = stat(NT * HEADS)
        ncum = stat(NT * HEADS)
        mp_p = stat(HEADS)
        mp_s = stat(HEADS)
        gp = stat(HEADS)
        mcol = stat(HEADS)
        mtb = stat(2 * HEADS)
        wx = stat(2 * HEADS)
        we = stat(2 * HEADS)
        gx = stat(2 * HEADS)
        ge = stat(2 * HEADS)
        gcol = stat(PAIRS)
        den = stat(HEADS)
        rden = stat(HEADS)
        nmax = stat(NP * HEADS)
        rsum = stat(NP * HEADS)
        drec = stat(NP * HEADS)
        pmax = stat(32)
        pcol = stat(2)
        pdiag = stat(32)
        ptot = stat(32)
        prec = stat(32)
        sufp = stat(DEC_BATCH * HEADS)
        lastv = stat(2 * HEADS)
        lnst = stat(12)
        lnmv = stat(2)
        lnr = stat(2)
        par_pair = "p (a b) -> p b a"

        def v4(ap):
            return ap.rearrange("p t (h e) -> p t h e", h=HEADS)

        def th(ap, a=NT):
            return ap.rearrange("p (t h) -> p t h", t=a)

        def over_e(ap4, n=HD):
            return ap4.unsqueeze(3).to_broadcast([*ap4.shape, n])

        def heads(ap, w=HD):
            return ap.rearrange("p (h e) -> p h e", e=w)

        def by_par(ap):
            return ap.rearrange("p (b a) e -> p a b e", a=2)

        with nc.Fori(0, DEPTH) as layer:
            L = bass.ds(layer, 1)
            with nc.Block() as block:
                @block.sync
                def _(sp):
                    sp.dma_start(vbuf[:, 0:D_IN], d["b_in"][L, :].to_broadcast([P, D_IN])).then_inc(bias_in, 16)
                    w_in_l = d["w_in"][L].rearrange("o (k p) c -> p (o k) c", p=P)
                    w_slab = (w_slab0, w_slab1, w_slab2)

                    def load_slab(at):
                        g = SLAB_ORDER[at]
                        w = min(SLAB, D_IN - g * SLAB)
                        sp.dma_start(slab[at % 3][:, :, 0:w], w_in_l[:, :, g * SLAB:g * SLAB + w]).then_inc(w_slab[at % 3], 16)

                    for at in range(1, 3):
                        load_slab(at)
                    with sp.If(layer < 1):
                        for rows_d in (xd, yd):
                            sp.dma_start(rows_d.rearrange("(p a) (c n) -> p (a c) n", p=P, n=P),
                                         zero[:, :].unsqueeze(1).to_broadcast([P, N_BLOCKS * D_MODEL // P, P])).then_inc(s_fill, 16)
                    ws_l = d["w_s"][L].rearrange("o h t s -> t (o h) s")
                    bs_l = d["b_s"][L].rearrange("o h t -> t (o h)")
                    for b in range(DEC_BATCH):
                        at = slice(b * DEC_SEQ, (b + 1) * DEC_SEQ)
                        sp.dma_start(ws8[at], ws_l[0:DEC_SEQ, :, 0:DEC_SEQ]).then_inc(gate_in, 16)
                        sp.dma_start(bss[at, :], bs_l[0:DEC_SEQ, :], allow_slow_non_contiguous=True).then_inc(gate_in, 16)
                        sp.dma_start(mp_s[at, :], d["state_mlstm_m"][L, b, :].to_broadcast([DEC_SEQ, HEADS])).then_inc(gate_in, 16)
                    sp.dma_start(bs[:, :], bs_l, allow_slow_non_contiguous=True).then_inc(gate_in, 16)
                    sp.dma_start(gmix[:, :], d["g_mix"][L].rearrange("o (k p) -> p (o k)", p=P),
                                 allow_slow_non_contiguous=True).then_inc(gate_in, 16)
                    sp.dma_start(ws_nat, ws_l).then_inc(ws_n, 16)
                    for at in range(3, N_SLABS):
                        sp.wait_ge(z_ps, NT * (at - 2))
                        load_slab(at)
                    sp.wait_ge(z_ps, NT * N_SLABS)
                    for b in range(DEC_BATCH):
                        at = slice(b % 2 * HD, (b % 2 + 1) * HD)
                        for st, to in (("state_ret", rs[at, b // 2, :, :]), ("state_mlstm_c", cs[at, b // 2, :, 0:HD])):
                            sp.dma_start(to, d[st][L, b].rearrange("o h d e -> d (o h) e")).then_inc(s_in, 16)
                        sp.dma_start(cs[at, b // 2, :, HD:HD + 1].rearrange("p h o -> p (h o)"), d["state_mlstm_n"][L, b].rearrange("o h d -> d (o h)"),
                                     allow_slow_non_contiguous=True).then_inc(s_in, 16)
                    sp.wait_ge(b_state, NT)
                    for b in range(DEC_BATCH):
                        at = slice(b % 2 * HD, (b % 2 + 1) * HD)
                        sp.dma_start(d["ret_sample"][L, b].rearrange("o h d e -> d (o h) e"), rs[at, b // 2, :, :]).then_inc(rs_out, 16)
                    sp.wait_ge(c_cd, NT)
                    for b in range(DEC_BATCH):
                        at = slice(b % 2 * HD, (b % 2 + 1) * HD)
                        sp.dma_start(d["mlstm_c_sample"][L, b].rearrange("o h d e -> d (o h) e"), cs[at, b // 2, :, 0:HD]).then_inc(cs_out, 16)
                        sp.dma_start(d["mlstm_n_sample"][L, b].rearrange("o h d -> d (o h)"),
                              cs[at, b // 2, :, HD:HD + 1].rearrange("p h o -> p (h o)"), allow_slow_non_contiguous=True).then_inc(cs_out, 16)
                    sp.wait_ge(e_fin, 1)
                    w_out_l = d["w_out"][L].rearrange("o (k p) c -> p (o k) c", p=P)
                    for s in range(2):
                        sp.dma_start(slab[s][:, :, :], w_out_l[:, :, s * SLAB:(s + 1) * SLAB]).then_inc(wout_in, 16)
                    for i, name in enumerate(("ln1_g", "ln1_b", "ln2_g", "ln2_b")):
                        sp.dma_start(vbuf[:, i * D_MODEL:(i + 1) * D_MODEL],
                                     d[name][L, :].to_broadcast([P, D_MODEL])).then_inc(ln_par, 16)
                    sp.wait_ge(m_ps, 2 * NT)
                    sp.dma_start(wr[:, :, 0:GROUPS], d["w_rg"][L].rearrange("o (k p) g -> p (o k) g", p=P)).then_inc(r_w, 16)
                    for g in range(GROUPS):
                        c = GROUPS * (g + 1)
                        sp.dma_start(wr[:, :, c:c + 4], d["w_re"][L, g].rearrange("o (k p) e -> p (o k) e", p=P)).then_inc(r_w, 16)
                    sp.dma_start(br[:, 0:GROUPS], d["b_rg"][L, :].to_broadcast([P, GROUPS])).then_inc(r_w, 16)
                    sp.dma_start(br[:, GROUPS:], d["b_re"][L].rearrange("o g e -> o (g e)").to_broadcast([P, EXPERTS])).then_inc(r_w, 16)
                    sp.wait_ge(o_ps, NT)
                    w13_in, w2_in = (w13_in0, w13_in1), (w2_in0, w2_in1)

                    def load_w13(e, s):
                        sp.dma_start(w13[s][:, 0], d["w1"][e].rearrange("o (p k) f -> p (o k) f", p=P)).then_inc(w13_in[s], 16)
                        sp.dma_start(w13[s][:, 1], d["w3"][e].rearrange("o (p k) f -> p (o k) f", p=P)).then_inc(w13_in[s], 16)

                    def load_w2(e, s):
                        sp.dma_start(w2[s], d["w2"][e].rearrange("o (p f) n -> p (o f) n", p=P)).then_inc(w2_in[s], 16)

                    def expert_of(k):
                        return bass.ds(layer * EXPERTS + sp.value_load(plan[0:1, bass.ds(k, 1)], min_val=0, max_val=EXPERTS - 1), 1)

                    for s in range(2):
                        load_w13(bass.ds(layer * EXPERTS + s, 1), s)
                    for s in range(2):
                        load_w2(bass.ds(layer * EXPERTS + s, 1), s)
                    sp.wait_ge(planned, 2)
                    last_pair = sp.value_load(plan[0:1, N_BLOCKS:N_BLOCKS + 1], min_val=EXPERTS // 2 - 1, max_val=N_BLOCKS // 2 - 1)
                    with sp.Fori(1, last_pair + 1) as i:
                        es = [expert_of(i * 2 + s) for s in range(2)]
                        for s in range(2):
                            sp.wait_ge(h_ps, i * 2 + (s - 1))
                            load_w13(es[s], s)
                        for s in range(2):
                            sp.wait_ge(y_ps, i * 2 + (s - 1))
                            load_w2(es[s], s)
                    assert DEPTH == 2
                    with sp.If(layer < DEPTH - 1):
                        sp.wait_ge(h_ps, last_pair * 2 + 1)
                        sp.dma_start(slab[0][:, :, :], d["w_in"][DEPTH - 1:DEPTH].rearrange("o (k p) c -> p (o k) c", p=P)[:, :, 0:SLAB]).then_inc(s_slab, 16)

                @block.gpsimd
                def _(pool):
                    ck = d["cache_k"].rearrange("l n (a b) h e -> (l n a) (b h e)", b=KPP // 2)
                    cv = d["cache_v"].rearrange("l n (a b) h e -> (l n a) (b h e)", b=KPP)
                    cl = d["cache_logf"].rearrange("l n (a b) h -> (l n a) (b h)", b=KPP)

                    def gather(to, table, b, sem):
                        pool.indirect_dma_start(to, None, table, bass.IndirectOffsetOnAxis(idx_u[:, b:b + 1], 0)).then_inc(sem, 16)

                    pool.wait_ge(idx_set, 2)

                    def gather_keys(b, half):
                        w = KPP * GW // 2
                        pool.indirect_dma_start(kbuf[:, half * w:(half + 1) * w], None, ck,
                                                bass.IndirectOffsetOnAxis(idx_k[:, half, b:b + 1], 0)).then_inc(k_in[half], 16)

                    pool.wait_ge(z_ps, NT * 5)
                    for b in range(DEC_BATCH):
                        gather(lfg[:, b, :, :].rearrange("p a b -> p (a b)"), cl, b, l_in)
                    pool.wait_ge(gate_sb, 1)
                    for half in range(2):
                        gather_keys(0, half)
                    pool.wait_ge(z_sb, NT * N_SLABS)
                    pool.wait_ge(ws_ps, 2)
                    gather(vbuf[:, :], cv, 0, v_in)
                    for b in range(DEC_BATCH):
                        if b < DEC_BATCH - 1:
                            for half in range(2):
                                pool.wait_ge(e_kps, 8 * b + 4 * (half + 1))
                                gather_keys(b + 1, half)
                        if b > 0:
                            pool.wait_ge(e_pv, b)
                            gather(vbuf[:, :], cv, b, v_in)

                    pool.wait_ge(s_fill, 32)
                    pool.wait_ge(planned, 1)
                    for t in tiles:
                        n = rows[t]
                        for c in range(TOP_K):
                            pool.indirect_dma_start(xd, bass.IndirectOffsetOnAxis(rows_u[0:n, t, c:c + 1], 0), x[0:n, t, :], None).then_inc(x_sent, 16)
                    pool.wait_ge(x_taken, 1)
                    for t in tiles:
                        pool.tensor_scalar(x[0:rows[t], t, :], x[0:rows[t], t, :], ALPHA, None, ALU.mult).then_inc(y_init, 1)
                    pool.wait_ge(y_stored, 1)
                    for t in tiles:
                        n = rows[t]
                        for c in range(TOP_K):
                            pool.indirect_dma_start(yg[0:n, t, c, :], None, yd, bass.IndirectOffsetOnAxis(rows_u[0:n, t, c:c + 1], 0)).then_inc(y_back[t], 16)
                    for t in tiles:
                        n = rows[t]
                        pool.wait_ge(n_normed, t + 1)
                        pool.tensor_tensor(x[0:n, t, :], x[0:n, t, :], vbuf[0:n, 2 * D_MODEL:3 * D_MODEL], ALU.mult).then_inc(n_scaled, 1)
                        pool.wait_ge(n_scaled, t + 1)
                        pool.tensor_tensor(x[0:n, t, :], x[0:n, t, :], vbuf[0:n, 3 * D_MODEL:4 * D_MODEL], ALU.add).then_inc(n_done, 1)

                @block.scalar
                def _(act):
                    due = Due()
                    own = Due()

                    def link(ins):
                        ins.then_inc(chain_a, 1)
                        act.wait_ge(chain_a, own(chain_a))

                    def f(out, in_, fn, **kw):
                        return nc.scalar.activation(out, in_, fn, **kw)

                    def root(out, in_, eps, scale, sem):
                        f(out, in_, ACT.Sqrt, scale=scale, bias=eps).then_inc(sem, 1)

                    def store(out, in_, **kw):
                        act.dma_start(out, in_, **kw).then_inc(stored, 16)
                        own(stored, 16)

                    for i in range(2 * NT):
                        t, hf = i // 2, i % 2
                        act.wait_ge(xT_ps, i + 1)
                        f(xTv[:, 4 * hf:4 * hf + 4, t * P:t * P + rows[t]], ps[:, 4 + i % 3, 0:4 * rows[t]].rearrange("p (k n) -> p k n", k=4),
                          ACT.Copy).then_inc(xT_sb, 1)
                    act.wait_ge(z_sb, NT * 1)
                    f(zt[:, :, 0:2 * GW], zt[:, :, 0:2 * GW], ACT.Gelu_apprx_tanh).then_inc(gelu_done, 1)
                    act.wait_ge(norm_sum, 1)
                    root(s_rstd, s_sum, T("ln_eps"), 1.0 / HD, norm_rs)
                    act.wait_ge(va_ready, 1)
                    store(d["chunk_v_sample"][L].rearrange("o b t h e -> (o b t) (h e)"), Z(NP, "a_v", NS))
                    act.wait_ge(f_in, 1)
                    link(f(fe, fa, ACT.Exp))
                    f(fe, fe, ACT.Ln, bias=1.0).then_inc(f_exp, 1)
                    act.wait_ge(f_gates, 1)
                    store(d["logf_prompt"][L].rearrange("o a (t p) h -> p (o a t) h", p=P), th(lf)[:, 0:NP, HEADS:])
                    store(d["logf_sample"][L].rearrange("o b t h -> (o b t) h"), th(lf)[0:NS, NP, HEADS:])
                    kp, vp = d["k_prompt"], d["v_prompt"]
                    for name, out in (("d_k", kp), ("d_v", vp)):
                        c = COLS[name]
                        store(out[L].rearrange("o a (t p) h e -> p (o a t) (h e)", p=P), zt[:, 0:NP, c:c + GW])
                    for name, out in (("d_k", d["k_sample"]), ("d_v", d["v_sample"])):
                        store(out[L].rearrange("o b t h e -> (o b t) (h e)"), Z(NP, name, NS))
                    act.wait_ge(z_sb, NT * (1 + SLAB_ORDER.index(COLS["b_g"] // SLAB)))
                    f(Zall("b_g"), Zall("b_g"), ACT.Silu).then_inc(silu_done, 1)

                    act.wait_ge(e_T, 1)
                    f(kTn, ps[:, 4, 2 * NS:4 * NS].rearrange("p (a n) -> p a n", a=2), ACT.Copy).then_inc(e_Tsb, 1)

                    def copy_scores(r):
                        act.wait_ge(e_row, 2 * r + 2)
                        if r >= 2:
                            act.wait_ge(e_s, r - 1)
                        f(srow[r % 2][0:HQ], ps[0:HQ, 1, :], ACT.Copy).then_inc(e_rsb, 1)

                    def cache_step(u):
                        i, g = u // 8, u % 8
                        if i < DEC_BATCH:
                            act.wait_ge(e_kps, u + 1)
                            if u >= 2:
                                act.wait_ge(e_row, u - 1)
                            f(kTs[u % 2], ps[:, 0, :], ACT.Copy).then_inc(e_ksb, 1)
                            if g in (2, 4, 6):
                                copy_scores(4 * i + g // 2 - 1)
                        if g == 6 and i > 0:
                            act.wait_ge(e_xs, i)
                            if i > 2:
                                act.wait_ge(e_pv, i - 2)
                            f(pp[(i - 1) % 2], xs[(i - 1) % 2], ACT.Exp).then_inc(e_p, 1)
                        if g == 7 and i < DEC_BATCH:
                            copy_scores(4 * i + 3)

                    steps = iter(range(CACHE_STEPS))

                    def cache_steps(n):
                        for _ in range(n):
                            cache_step(next(steps))

                    for t in tiles:
                        n = rows[t]
                        act.wait_ge(b_T, t + 1)
                        src = ps[:, 4, 0:4 * n].rearrange("p (a n) -> p a n", a=4)
                        f(qkT[:, 0:2, 0:n], src[:, 0:2], ACT.Copy).then_inc(b_Tsb, 1)
                        f(qkT[:, 2:4, 0:n], src[:, 2:4], ACT.Copy, scale=SCALE).then_inc(b_Tsb, 1)
                        cache_steps(sum(B_STEPS) + (HEADS if t == NP else 0))
                        if t == 1:
                            f(Zall("c_o"), Zall("c_o"), ACT.Sigmoid).then_inc(sigm_done, 1)
                        if t == NP - 1:
                            act.wait_ge(b_state, NP)
                            for par in range(2):
                                store(d["ret_prompt"][L].rearrange("o a (pr r) d e -> r d (o a pr) e", r=2)[par],
                                      ret[par * HD:(par + 1) * HD])
                    for t in tiles:
                        n = rows[t]
                        act.wait_ge(c_T, t + 1)
                        src = ps[:, 4, 0:4 * n].rearrange("p (a n) -> p a n", a=4)
                        f(qkT[:, 0:2, 0:n], src[:, 0:2], ACT.Copy).then_inc(c_Tsb, 1)
                        f(qkT[:, 2:4, 0:n], src[:, 2:4], ACT.Copy, scale=SCALE).then_inc(c_Tsb, 1)
                        if t > 0:
                            act.wait_ge(c_up, t)
                        else:
                            act.wait_ge(c_free, 1)
                        f(vx[0:n, :, 0:HD], heads(Z(t, "c_v", n)), ACT.Copy).then_inc(c_vx, 1)
                        cache_steps(C_STEPS[0])
                        act.wait_ge(c_t, t + 1)
                        for h in range(HEADS):
                            c = t * HEADS + h
                            f(wexp[0:n, h, 0:n], wexp[0:n, h, 0:n], ACT.Exp, bias=gi[0:n, c:c + 1]).then_inc(c_w, 1)
                        cache_steps(C_STEPS[1])
                        act.wait_ge(c_mt, t + 1)
                        f(we[0:n], wx[0:n], ACT.Exp).then_inc(c_exps, 1)
                        act.wait_ge(c_gin, t + 1)
                        f(ge[0:n], gx[0:n], ACT.Exp).then_inc(c_gs, 1)
                        cache_steps(C_STEPS[2] + (C_STEPS[3] if t < NP else 1 + HEADS))
                        if t == NP - 1:
                            act.wait_ge(c_cd, NP)
                            for par in range(2):
                                at = slice(par * HD, (par + 1) * HD)
                                store(d["mlstm_c_prompt"][L].rearrange("o a (pr r) d e -> r d (o a pr) e", r=2)[par],
                                      mem[at, :, 0:HD])
                                store(d["mlstm_n_prompt"][L].rearrange("o a (pr r) d -> r d (o a pr)", r=2)[par],
                                      mem[at, :, HD:HD + 1].rearrange("p a b -> p (a b)"), allow_slow_non_contiguous=True)
                            store(d["mlstm_m_prompt"][L].rearrange("o a h -> (o a) h"), mp_p[0:1, :])
                    act.wait_ge(c_cd, NT)
                    store(d["mlstm_m_sample"][L].rearrange("o b h -> (o b) h"), mp_s[0:NS:DEC_SEQ, :])
                    cache_steps(1)

                    for t in range(NP):
                        act.wait_ge(d_T, t + 1)
                        src = ps[:, 4 + 2 * (t % 2), :].rearrange("p (a n) -> p a n", a=4)
                        f(qTa[:, :, t * P:(t + 1) * P], src[:, 0:2], ACT.Copy, scale=SCALE).then_inc(d_Tsb, 1)
                        f(kTa[:, :, t * P:(t + 1) * P], src[:, 2:4], ACT.Copy).then_inc(d_Tsb, 1)
                        if t % 2:
                            cache_steps(1)
                    cache_steps(1)
                    act.wait_ge(rs_out, 16 * DEC_BATCH)
                    for m in range(NP * HEADS + 1):
                        if m < NP * HEADS:
                            w = (m // HEADS + 1) * P
                            act.wait_ge(d_lgx, m + 1)
                            f(lg[m % 2][:, 0:w], lg[m % 2][:, 0:w], ACT.Exp, bias=nmax[:, m:m + 1],
                              accum_out=rsum[:, m:m + 1]).then_inc(d_exp, 1)
                        if m > 0:
                            w = (m - 1) // HEADS + 1
                            act.wait_ge(d_pT, m)
                            f(pT[(m - 1) % 2][:, 0:w, :], ps[:, 5, 0:w * P].rearrange("p (a n) -> p a n", n=P),
                              ACT.Copy).then_inc(d_pTsb, 1)
                        if m < NP * HEADS:
                            cache_steps(D_STEPS[m % 2])
                    for u in steps:
                        cache_step(u)

                    act.wait_ge(cs_out, 2 * 16 * DEC_BATCH)
                    for at in (slice(0, 3 * NT * HEADS), slice(3 * NT * HEADS, 4 * NT * HEADS)):
                        act.wait_ge(rms_s, due(rms_s))
                        root(n_sum[:, at], n_sum[:, at], T("rms_eps"), 1.0 / HD, rms_r)

                    def layer_norm(t):
                        n = rows[t]
                        act.wait_ge(o_var, due(o_var))
                        root(lnr[0:n, 0:1], lnmv[0:n, 1:2], T("ln_eps", n), 1.0, o_rstd)

                    for i in range(2 * NT):
                        t, hf = i // 2, i % 2
                        if hf == 0:
                            layer_norm(t)
                        act.wait_ge(xT_ps, 2 * NT + i + 1)
                        f(xTv[:, 4 * hf:4 * hf + 4, t * P:t * P + rows[t]], ps[:, 4 + i % 3, 0:4 * rows[t]].rearrange("p (k n) -> p k n", k=4),
                          ACT.Copy).then_inc(xT_sb, 1)
                    act.wait_ge(r_lg, 1)
                    f(r_ge, r_gd, ACT.Exp).then_inc(r_exp, 1)
                    act.wait_ge(r_e2, 1)
                    f(r_ex, r_vd, ACT.Exp).then_inc(r_e2x, 1)
                    act.wait_ge(planned, 2)
                    last_pair = act.value_load(plan[0:1, N_BLOCKS:N_BLOCKS + 1], min_val=EXPERTS // 2 - 1, max_val=N_BLOCKS // 2 - 1)
                    act.wait_ge(x_sent, layer * (16 * NT * TOP_K) + 16 * NT * TOP_K)
                    act.sem_inc(x_taken, 1)
                    xg_in, y_out = (xg_in0, xg_in1), (y_out0, y_out1)

                    def load_block(k, s):
                        act.dma_start(xg[s], xd[bass.ds(k * BLOCK, BLOCK), :]).then_inc(xg_in[s], 16)

                    def turn_block(k2, s):
                        for hf in range(2):
                            act.wait_ge(xgT_ps, k2 + (hf + 1))
                            f(xgT[s][:, 4 * hf:4 * hf + 4, :], ps[:, hf, :].rearrange("p (k n) -> p k n", k=4), ACT.Copy).then_inc(xgT_sb, 1)

                    def act_block(i, k, s, more, turn):
                        if more:
                            load_block(k + 2, s)
                        act.wait_ge(h_ps, k + 1)
                        f(sil[s], ps[:, 2 + s, 0:2 * BLOCK], ACT.Silu).then_inc(sil_sb, 1)
                        if turn:
                            turn_block(k * 2 + 2, 1 - s)
                        act.wait_ge(y_ps, k + 1)
                        act.wait_ge(y_out[s], i * 16 + 16)
                        f(yo[s][:, SLAB:], ps[:, 5 + 2 * s, :], ACT.Copy).then_inc(y_sb, 1)
                        act.wait_ge(y_sb, k * 2 + 5)
                        act.dma_start(yd[bass.ds(k * BLOCK, BLOCK), :], yo[s]).then_inc(y_out[s], 16)

                    act.sem_inc(y_out0, 16)
                    act.sem_inc(y_out1, 16)
                    for s in range(2):
                        act.dma_start(xg[s], xd[s * BLOCK:(s + 1) * BLOCK, :]).then_inc(xg_in[s], 16)
                    turn_block(0, 0)
                    with act.Fori(0, last_pair) as i:
                        act_block(i, i * 2, 0, True, True)
                        act_block(i, i * 2 + 1, 1, True, True)
                    lp = last_pair
                    act_block(lp, lp * 2, 0, False, True)
                    act_block(lp, lp * 2 + 1, 1, False, False)
                    for s in range(2):
                        act.wait_ge(y_out[s], last_pair * 16 + 32)
                    act.sem_inc(y_stored, 1)
                    for t in tiles:
                        n = rows[t]
                        act.wait_ge(n_var, t + 1)
                        rstd = n_rs[0:n, t, 0:1]
                        link(f(rstd, n_mv[0:n, t, 1:2], ACT.Ln, bias=T("ln_eps", n)))
                        link(f(rstd, rstd, ACT.Exp, scale=-0.5))
                        link(f(n_rs[0:n, t, 1:2], n_mv[0:n, t, 0:1], ACT.Copy, scale=rstd))
                        f(x[0:n, t, :], x[0:n, t, :], ACT.Identity, scale=rstd, bias=n_rs[0:n, t, 1:2]).then_inc(n_normed, 1)
                    act.wait_ge(stored, own(stored, 0))

                @block.vector
                def _(dve):
                    due = Due()
                    own = Due()
                    V = nc.vector

                    def link(ins, sem=None):
                        sem = sem or chain_v
                        ins.then_inc(sem, 1)
                        dve.wait_ge(sem, own(sem))

                    def tt(out, a, b, op):
                        return V.tensor_tensor(out, a, b, op)

                    V.tensor_copy(idx_u[:, :], idx_f[:, :])
                    for half in range(2):
                        V.tensor_scalar(idx_k[:, half, :], idx_f[:, :], 2.0, float(half), ALU.mult, ALU.add).then_inc(idx_set, 1)
                    link(V.tensor_scalar(idx_f[:, :], idx_f[:, :], float(N_POOL * RPP), None, ALU.add))
                    dve.wait_ge(bias_in, 16)
                    def key_terms():
                        dve.wait_ge(e_cumps, 1)
                        link(V.tensor_copy(sfx[:, :, KPP - 1, :], ps[:, 5, 0:DEC_BATCH * HEADS].rearrange("p (b h) -> p b h", h=HEADS)), e_cumsb)
                        for k in range(KPP - 2, -1, -1):
                            link(tt(sfx[:, :, k, :], sfx[:, :, k + 1, :], lfg[:, :, k + 1, :], ALU.add))

                    for at, g in enumerate(SLAB_ORDER):
                        w = min(SLAB, D_IN - g * SLAB)
                        for t in tiles:
                            if at == 6 and t == 4:
                                key_terms()
                            i, n = at * NT + t, rows[t]
                            dve.wait_ge(z_ps, i + 1)
                            tt(zt[0:n, t, g * SLAB:g * SLAB + w], ps[0:n, i % 4, 0:w], vbuf[0:n, g * SLAB:g * SLAB + w],
                               ALU.add).then_inc(z_sb, 1)
                        dve.wait_ge(z_sb, NT * (at + 1))
                        if at == 1:
                            dve.wait_ge(s_rest, 16)
                            dve.wait_ge(gelu_done, 1)
                            va, sq = v4(Zall("a_v")), v4(tmp_a)
                            link(V.tensor_reduce(th(s_sum), va, AX.X, ALU.add))
                            link(V.tensor_scalar(s_sum, s_sum, 1.0 / HD, None, ALU.mult))
                            link(tt(va, va, over_e(th(s_sum)), ALU.subtract))
                            link(tt(sq, va, va, ALU.mult))
                            V.tensor_reduce(th(s_sum), sq, AX.X, ALU.add).then_inc(norm_sum, 1)
                            dve.wait_ge(gate_in, 16 * (3 * DEC_BATCH + 2))
                            up_b = T("lower_s", NS).rearrange("p (b s) -> p b s", s=DEC_SEQ).unsqueeze(1)
                            link(tt(ws_exp[0:NS].rearrange("p h (b s) -> p h b s", s=DEC_SEQ),
                                    ws8[:, :, :].unsqueeze(2).to_broadcast([NS, HEADS, DEC_BATCH, DEC_SEQ]),
                                    up_b.to_broadcast([NS, HEADS, DEC_BATCH, DEC_SEQ]), ALU.mult), ws_s8)
                        if at == 2:
                            c0 = COLS["b_q"]
                            qk = zt[:, :, c0:c0 + 2 * GW].rearrange("p t (h r e) -> p t h r e", h=2 * HEADS, r=2)
                            x1, x2 = qk[:, :, :, 0, :], qk[:, :, :, 1, :]
                            co, si = [T(name).rearrange("p (t e) -> p t e", t=NT).unsqueeze(2).to_broadcast([P, NT, 2 * HEADS, HD // 2])
                                      for name in ("cos", "sin")]
                            rb, rc = [tmp.rearrange("p t (h e) -> p t h e", h=2 * HEADS) for tmp in (tmp_b, tmp_c)]
                            tt(rb, x1, si, ALU.mult)
                            link(tt(rc, x2, si, ALU.mult))
                            tt(x1, x1, co, ALU.mult)
                            link(tt(x2, x2, co, ALU.mult))
                            tt(x1, x1, rc, ALU.subtract)
                            link(tt(x2, x2, rb, ALU.add))
                            dve.wait_ge(norm_rs, 1)
                            link(V.reciprocal(s_rstd, s_rstd))
                            tt(va, va, over_e(th(s_rstd)), ALU.mult).then_inc(va_ready, 1)
                            dve.wait_ge(va_ready, 1)
                            V.memset(ret[:, :, :], 0.0)
                            V.memset(mem[:, :, :], 0.0)
                            V.memset(mp_p, 0.0).then_inc(rope_done, 1)
                            dve.wait_ge(rope_done, 1)
                        if at == 3:
                            V.tensor_copy(th(ff)[:, :, 0:HEADS], Zall("c_f", HEADS))
                            link(V.tensor_copy(th(ff)[:, :, HEADS:], Zall("d_f", HEADS)))
                            link(V.tensor_scalar(fa, ff, -1.0, None, ALU.mult))
                            tt(fa, ff, fa, ALU.min).then_inc(f_in, 1)
                            dve.wait_ge(ws_ps, 1)
                            tt(wsT[:, :, :], ps[:, 7, :].rearrange("p (h t) -> p h t", h=HEADS), rep(T("upper"), HEADS), ALU.mult).then_inc(ws_sb, 1)
                            dve.wait_ge(ws_ps, 2)
                            V.tensor_copy(wsTs[:, :, :], ps[0:NS, 6, 0:GW].rearrange("p (h t) -> p h t", h=HEADS)).then_inc(ws_sb, 1)
                            dve.wait_ge(f_exp, 1)
                            link(V.tensor_scalar(ff, ff, 0.0, None, ALU.min))
                            tt(lf, ff, fe, ALU.subtract).then_inc(f_gates, 1)
                            dve.wait_ge(f_gates, 1)
                        if at == 5:
                            dve.wait_ge(a_ps, 1)
                            ya = v4(Zall("a_u"))
                            for t in tiles:
                                n = rows[t]
                                w_v = v4(tmp_a)[0:n, t]
                                link(tt(w_v, heads(ps[0:n, 4 + t // 2, t % 2 * GW:(t % 2 + 1) * GW]), b3((bs if t < NP else bss)[0:n, :], HD), ALU.add))
                                link(tt(ya[0:n, t], ya[0:n, t], w_v, ALU.mult))
                            dve.wait_ge(gate_ps, 1)
                            V.tensor_copy(cum[:, 0:NP * HEADS], ps[:, 7, 0:NP * HEADS])
                            link(V.tensor_copy(cum[0:NS, NP * HEADS:], ps[0:NS, 7, NP * HEADS:NT * HEADS]), gate_sb)
                            ci = Zall("c_i", HEADS)
                            tt(th(gi)[:, 0:NP], ci[:, 0:NP], th(cum)[:, 0:NP], ALU.subtract)
                            link(tt(gi[0:NS, NP * HEADS:], ci[0:NS, NP], cum[0:NS, NP * HEADS:], ALU.subtract))

                            dve.wait_ge(d_cum, 1)
                            V.tensor_scalar(ncum[:, 0:NP * HEADS], ps[:, 7, 2 * P:2 * P + NP * HEADS], -1.0, None, ALU.mult)
                            link(V.tensor_scalar(ncum[0:NS, NP * HEADS:], ps[0:NS, 7, 2 * P + NP * HEADS:2 * P + NT * HEADS], -1.0, None, ALU.mult))
                            link(V.memset(qz, 0.0))
                            dve.wait_ge(e_Tsb, 1)
                            for par in range(2):
                                rows_ = slice(par * HD, (par + 1) * HD)
                                for pair in range(PAIRS):
                                    c = (2 * pair + par) * DEC_SEQ
                                    V.tensor_scalar(qz[rows_, pair, :, c:c + DEC_SEQ], ps[rows_, 4, pair * NS:(pair + 1) * NS].rearrange("p (b t) -> p b t", t=DEC_SEQ),
                                                    SCALE, None, ALU.mult).then_inc(e_Tsb, 1)
                            msk = T("neg_ts", NS).rearrange("p (b t) -> p b t", t=DEC_SEQ)
                            for h in range(HEADS):
                                m = tt(newb[0:NS, :, h, :], msk, ncum[0:NS, NP * HEADS + h:NP * HEADS + h + 1].unsqueeze(2).to_broadcast([NS, DEC_BATCH, DEC_SEQ]), ALU.add)
                            link(m)
                            dve.wait_ge(l_in, layer * (16 * DEC_BATCH) + 16 * DEC_BATCH)
                            link(V.tensor_reduce(sufp.rearrange("p (b h) -> p b h", h=HEADS), lfg.rearrange("p b k h -> p b h k"), AX.X, ALU.add), e_tot)
                    for X in xs:
                        V.memset(X, NEG)

                    def sample_queries(name):
                        link(V.tensor_copy(qd2[0:NS].rearrange("p h (r e) -> p h r e", r=2),
                                           heads(Z(NP, name, NS)).unsqueeze(2).to_broadcast([NS, HEADS, 2, HD])), qm_q)
                        dve.wait_ge(qm_ps, due(qm_ps))
                        for bp in range(BP):
                            m = tt(qm[:, bp], ps[:, 4, 0:GW].rearrange("p (h n) -> p h n", h=HEADS),
                                   rep(T("seq_of")[:, bp * NS:(bp + 1) * NS], HEADS), ALU.mult)
                        m.then_inc(qm_sb, 1)

                    def sample_keys(w):
                        for h in range(HEADS):
                            if h > 0:
                                dve.wait_ge(km_used, due(km_used))
                            tt(km[0:NS], rep(kd[0:NS, h * HD:(h + 1) * HD], DEC_BATCH), b3(T("in_seq", NS), HD), ALU.mult).then_inc(km_sb, 1)
                            cache_steps(1)
                        due(km_used)
                        dve.wait_ge(km_used, own(km_used, HEADS))

                    def finish_sequence(i):
                        dve.wait_ge(e_pv, i + 1)
                        link(V.reciprocal(prec[0:HQ, 0:1], ps[0:HQ, 3, GW:GW + 1]))
                        V.scalar_tensor_tensor(ym[0:HQ, i], ps[0:HQ, 3, 0:GW], prec[0:HQ, 0:1], T("own_head", HQ), ALU.mult, ALU.mult).then_inc(e_ym, 1)

                    def cache_step(u):
                        i, g = u // 8 - 1, u % 8
                        if i < 0:
                            return
                        X = xs[i % 2]
                        if g == 0:
                            dve.wait_ge(e_s, 4 * i + 4)
                            dve.wait_ge(e_psum, i + 1)
                            if i >= 2:
                                dve.wait_ge(e_p, i - 1)
                            S = ps[:, 2, :].rearrange("p (k h t) -> p (k h) t", h=HEADS, t=DEC_SEQ)
                            tt(X[:, 0:KPP, :].rearrange("p k (h t) -> p (k h) t", t=DEC_SEQ), S, b3(sfx[:, i].rearrange("p k h -> p (k h)"), DEC_SEQ), ALU.add)
                            c = NEW + i % 2 * HQ
                            link(tt(X[0:NS, KPP, :], ps[0:NS, 3, c:c + HQ], newb[0:NS, i].rearrange("p h t -> p (h t)"), ALU.add))
                            V.tensor_reduce(pmax, X.rearrange("p k c -> p c k"), AX.X, ALU.max).then_inc(e_pm, 1)
                            if i > 0:
                                finish_sequence(i - 1)
                        if g == 3:
                            dve.wait_ge(e_mt, i + 1)
                            link(V.tensor_reduce(pcol[0:HQ, 0:1], ps[0:HQ, 3, MT:MT + P], AX.X, ALU.max))
                            V.tensor_scalar(pdiag[0:HQ], T("ident", HQ)[:, 0:HQ], pcol[0:HQ, 0:1], None, ALU.mult).then_inc(e_dg, 1)
                        if g == 5:
                            dve.wait_ge(e_bc, i + 1)
                            link(V.tensor_copy(pmax, ps[:, 3, BC:BC + HQ]))
                            tt(X, X, rep(pmax, NK), ALU.subtract).then_inc(e_xs, 1)
                        if g == 7:
                            dve.wait_ge(e_p, i + 1)
                            V.tensor_reduce(ptot, pp[i % 2].rearrange("p k c -> p c k"), AX.X, ALU.add).then_inc(e_lf, 1)

                    steps = iter(range(CACHE_STEPS))

                    def cache_steps(n):
                        for _ in range(n):
                            cache_step(next(steps))

                    for t in tiles:
                        n, samp = rows[t], t == NP
                        sfx_ = "_s" if samp else ""
                        kdec = b3(T("k_dec" + sfx_, n), HD)
                        link(tt(heads(kd[0:n]), heads(Z(t, "b_k", n)), kdec, ALU.mult), b_kd)
                        cache_steps(B_STEPS[0])
                        if samp:
                            sample_queries("b_q")
                        dve.wait_ge(b_sc, t + 1)
                        tt(sw[0:n, :, 0:n].rearrange("p (a b) n -> p a b n", a=2), ps[0:n, 6:8, 0:2 * n].rearrange("p a (b n) -> p a b n", b=2),
                           T("dec" + sfx_, n).rearrange("p (a b n) -> p a b n", a=2, b=2), ALU.mult).then_inc(b_sw, 1)
                        cache_steps(B_STEPS[1])
                        dve.wait_ge(b_out, t + 1)
                        yb = heads(Z(t, "b_q", n))
                        if not samp:
                            link(tt(by_par(mix[0:n, :, 0:HD]), ps[0:n, 6:8, 0:2 * HD].rearrange("p a (b e) -> p a b e", b=2),
                                    T("q_dec", n).rearrange("p (a b) -> p a b", a=2).unsqueeze(3).to_broadcast([n, 2, 2, HD]), ALU.mult))
                        else:
                            link(tt(mix[0:n, :, 0:HD], heads(ps[0:n, 6, 0:GW]), b3(T("q_dec_s", n), HD), ALU.mult))
                        link(tt(yb, heads(ps[0:n, 4, 0:GW]), mix[0:n, :, 0:HD], ALU.add))
                        if not samp:
                            link(tt(ret[:, :, :], ret[:, :, :], b3(T("c_dec"), HD), ALU.mult))
                            dve.wait_ge(b_up, t + 1)
                            for par in range(2):
                                at = slice(par * HD, (par + 1) * HD)
                                m = tt(ret[at], ret[at], ps[at, 5, 0:4 * HD].rearrange("p (a b) -> p a b", a=2)[:, :, par * HD:(par + 1) * HD], ALU.add)
                            link(m, b_state)
                        else:
                            sample_keys("b")
                            link(tt(rs, rs, T("c_dec_s").unsqueeze(1).unsqueeze(3).to_broadcast([P, BP, HEADS, HD]), ALU.mult))
                            link(tt(rs.rearrange("p (x a) h e -> p x (a h e)", x=2), rs.rearrange("p (x a) h e -> p x (a h e)", x=2), ps[:, 4:6, :], ALU.add), b_state)
                        cache_steps(B_STEPS[2])

                    V.memset(vx[:, :, HD:HD + 1], 1.0).then_inc(c_free, 1)
                    dve.wait_ge(c_free, 1)
                    for t in tiles:
                        n, samp = rows[t], t == NP
                        sfx_ = "_s" if samp else ""
                        mp = mp_s if samp else mp_p
                        g_t, b_t = [a[0:n, t * HEADS:(t + 1) * HEADS] for a in (gi, cum)]
                        link(V.scalar_tensor_tensor(gp[0:n], mp[0:n], T("start" + sfx_, n), g_t, ALU.add, ALU.max))
                        tt(diag[0:n, :, 0:n], rep(T("ident", n)[:, 0:n], HEADS), b3(gp[0:n], n), ALU.mult).then_inc(c_dg, 1)
                        cache_steps(C_STEPS[0])
                        if samp:
                            sample_queries("c_q")
                        dve.wait_ge(c_row, t + 1)
                        mr = mrow_flat[0:n, 0:HEADS * n]
                        link(V.tensor_tensor_scan(mr, T("reset" + sfx_, n), ps[0:n, 5, 0:HEADS * n], 0.0, ALU.add, ALU.max))
                        mr = mr.rearrange("p (h n) -> p h n", h=HEADS)
                        tt(wexp[0:n, :, 0:n], rep(T("neg_ts" if samp else "neg_t", n), HEADS), mr, ALU.subtract).then_inc(c_t, 1)
                        link(tt(diag[0:n, :, 0:n], rep(T("ident", n)[:, 0:n], HEADS), mr, ALU.mult))
                        link(V.tensor_reduce(mcol[0:n], diag[0:n, :, 0:n], AX.X, ALU.add))
                        tt(wx[0:n, 0:HEADS], mp[0:n], mcol[0:n], ALU.subtract)
                        V.tensor_copy(mtb[0:n, HEADS:], b_t)
                        link(tt(mtb[0:n, 0:HEADS], b_t, mcol[0:n], ALU.add))
                        link(V.tensor_scalar(wx[0:n, HEADS:], mtb[0:n, 0:HEADS], -1.0, None, ALU.mult), c_mt)
                        cache_steps(C_STEPS[1])
                        dve.wait_ge(c_last, t + 1)
                        link(V.tensor_copy(lastv[0:n], ps[0:n, 5, 0:2 * HEADS]))
                        link(tt(lastv[0:n, HEADS:], lastv[0:n, HEADS:], lastv[0:n, 0:HEADS], ALU.subtract))
                        tt(gx[0:n, 0:HEADS], g_t, lastv[0:n, HEADS:], ALU.add)
                        link(tt(gx[0:n, HEADS:], mp[0:n], lastv[0:n, HEADS:], ALU.add), c_gin)
                        V.tensor_copy(mp[0:n], lastv[0:n, 0:HEADS])
                        dve.wait_ge(c_gs, t + 1)
                        link(V.scalar_tensor_tensor(heads(kd[0:n]), heads(Z(t, "c_k", n)), SCALE, b3(ge[0:n, 0:HEADS], HD), ALU.mult, ALU.mult), c_kd)
                        dve.wait_ge(c_sc, t + 1)
                        dve.wait_ge(c_w, HEADS * (t + 1))
                        tt(sw[0:n, :, 0:n].rearrange("p (a b) n -> p a b n", a=2), ps[0:n, 6:8, 0:2 * n].rearrange("p a (b n) -> p a b n", b=2),
                           by_par(wexp[0:n, :, 0:n]), ALU.mult).then_inc(c_sw, 1)
                        cache_steps(C_STEPS[2])
                        dve.wait_ge(c_out, t + 1)
                        dve.wait_ge(c_exps, t + 1)
                        wst = b3(we[0:n, 0:HEADS], HD + 1)
                        if not samp:
                            link(tt(by_par(mix[0:n]), ps[0:n, 6:8, 0:2 * (HD + 1)].rearrange("p a (b e) -> p a b e", b=2), by_par(wst), ALU.mult))
                        else:
                            link(tt(mix[0:n], heads(ps[0:n, 6, 0:HEADS * (HD + 1)], HD + 1), wst, ALU.mult))
                        link(tt(mix[0:n], heads(ps[0:n, 4, 0:HEADS * (HD + 1)], HD + 1), mix[0:n], ALU.add))
                        dcol = mix[0:n, :, HD:HD + 1].rearrange("p h o -> p (h o)")
                        link(V.scalar_tensor_tensor(den[0:n], dcol, -1.0, we[0:n, HEADS:], ALU.mult, ALU.max))
                        link(tt(den[0:n], den[0:n], dcol, ALU.max))
                        link(V.reciprocal(rden[0:n], den[0:n]))
                        link(tt(heads(Z(t, "c_q", n)), mix[0:n, :, 0:HD], b3(rden[0:n], HD), ALU.mult))
                        if not samp:
                            for par in range(2):
                                at = slice(par * HD, (par + 1) * HD)
                                m = V.tensor_copy(gcol[at], ge[at, HEADS:].rearrange("p (a b) -> p b a", b=2)[:, par, :])
                            link(m)
                            link(tt(mem[:, :, :], mem[:, :, :], b3(gcol, HD + 1), ALU.mult))
                            dve.wait_ge(c_up, t + 1)
                            for par in range(2):
                                at = slice(par * HD, (par + 1) * HD)
                                m = tt(mem[at], mem[at], ps[at, 5, 0:4 * (HD + 1)].rearrange("p (a b) -> p a b", a=2)[:, :, par * (HD + 1):(par + 1) * (HD + 1)], ALU.add)
                            link(m, c_cd)
                        else:
                            sample_keys("c")
                            csf = cs.rearrange("p a h e -> p (a h) e")
                            dve.wait_ge(c_up, t + 1)
                            link(tt(csf, csf, b3(ps[:, 7, CU:CU + BP * HEADS], HD + 1), ALU.mult))
                            for bp, bank in enumerate((4, 5, 6, 7)):
                                m = tt(cs[:, bp].rearrange("p h e -> p (h e)"), cs[:, bp].rearrange("p h e -> p (h e)"),
                                       ps[:, bank, 0:HEADS * (HD + 1)], ALU.add)
                            link(m, c_cd)
                        cache_steps(C_STEPS[3] if t < NP else 1)
                    cache_steps(1)

                    cache_steps(2)
                    for h in range(HEADS):
                        if h >= 2:
                            dve.wait_ge(d_row, h - 1)
                        tt(dg[h % 2], rep(T("ident"), NP), b3(th(ncum)[:, 0:NP, h:h + 1].rearrange("p t o -> p (t o)"), P), ALU.mult).then_inc(d_dg, 1)
                        if h >= 1:
                            dve.wait_ge(d_row, h)
                            V.tensor_copy(ncr[:, h - 1, :], ps[:, 5 + 2 * ((h - 1) % 2), :]).then_inc(d_ncr, 1)
                    dve.wait_ge(d_row, HEADS)
                    V.tensor_copy(ncr[:, HEADS - 1, :], ps[:, 5 + 2 * ((HEADS - 1) % 2), :]).then_inc(d_ncr, 1)
                    dve.wait_ge(d_ncr, HEADS)
                    cache_steps(1)

                    def d_finish(c):
                        dve.wait_ge(d_o, HEADS * (c + 1))
                        dve.wait_ge(d_exp, HEADS * (c + 1))
                        at = slice(c * HEADS, (c + 1) * HEADS)
                        link(V.reciprocal(drec[:, at], rsum[:, at]))
                        tt(heads(Z(c, "d_q")), heads(ps[:, 7, 0:GW]), b3(drec[:, at], HD), ALU.mult).then_inc(d_y, 1)

                    for m in range(NP * HEADS):
                        c, h = m // HEADS, m % HEADS
                        w = (c + 1) * P
                        if m >= 2:
                            dve.wait_ge(d_pT, m - 1)
                        dve.wait_ge(d_lg, m + 1)
                        link(tt(lg[m % 2][:, 0:w], ps[:, 4 + 2 * (m % 2), 0:w], ncr[:, h, 0:w], ALU.add))
                        V.tensor_reduce(nmax[:, m:m + 1], lg[m % 2][:, 0:w], AX.X, ALU.max, negate=True).then_inc(d_lgx, 1)
                        if h == 1 and c > 0:
                            d_finish(c - 1)
                        if m < 3 * NT:
                            a, t = m // NT, m % NT
                            y = heads(Z(t, MERGED[a]))
                            if MERGED[a] == "c_q":
                                dve.wait_ge(sigm_done, 1)
                                link(tt(y, y, heads(Z(t, "c_o")), ALU.mult))
                            link(tt(heads(sq_t), y, y, ALU.mult))
                            at = a * NT * HEADS + t * HEADS
                            link(V.tensor_reduce(n_sum[:, at:at + HEADS], heads(sq_t), AX.X, ALU.add))
                            if m == 3 * NT - 1:
                                V.memset(pcol[:, 1:2], 0.0).then_inc(rms_s, 1)
                        cache_steps(D_STEPS[m % 2])
                    d_finish(NP - 1)
                    for u in steps:
                        cache_step(u)
                    finish_sequence(DEC_BATCH - 1)

                    def head_norm(a):
                        y = v4(Zall(MERGED[a]))
                        link(tt(y, y, over_e(th(n_sum[:, a * NT * HEADS:(a + 1) * NT * HEADS])), ALU.mult))

                    dve.wait_ge(rms_r, 1)
                    link(V.reciprocal(n_sum[:, 0:3 * NT * HEADS], n_sum[:, 0:3 * NT * HEADS]))
                    for a in range(2):
                        head_norm(a)
                    dve.wait_ge(silu_done, 1)
                    link(tt(Zall("b_q"), Zall("b_q"), Zall("b_g"), ALU.mult), merged)
                    head_norm(2)
                    dve.wait_ge(e_fin, 1)
                    link(V.tensor_copy(Z(NP, "d_q", NS), ps[0:NS, 0, 0:GW]))
                    y = v4(Zall("d_q"))
                    link(tt(v4(sq_all), y, y, ALU.mult))
                    V.tensor_reduce(th(n_sum[:, 3 * NT * HEADS:]), v4(sq_all), AX.X, ALU.add).then_inc(rms_s, 1)
                    dve.wait_ge(rms_r, 2)
                    link(V.reciprocal(n_sum[:, 3 * NT * HEADS:], n_sum[:, 3 * NT * HEADS:]))
                    head_norm(3)
                    V.memset(pcol, 0.0).then_inc(merged, 1)
                    for i in range(2 * NT):
                        t, hf = i % NT, i // NT
                        n = rows[t]
                        dve.wait_ge(m_ps, i + 1)
                        tt(xTv[:, 4 * hf:4 * hf + 4, t * P:t * P + n], ps[:, 4 + i % 4, 0:4 * n].rearrange("p (k n) -> p k n", k=4),
                           b3(gmix[:, 4 * hf:4 * hf + 4], n), ALU.mult).then_inc(m_sb, 1)

                    def layer_norm(t, gcol_, src):
                        n = rows[t]
                        X = src[0:n, t, :]
                        for hf in range(2):
                            m = V.bn_stats(lnst[0:n, 6 * hf:6 * hf + 6], X[:, hf * 512:hf * 512 + 512])
                        link(m)
                        link(V.bn_aggr(lnmv[0:n, :], lnst[0:n, :]), o_var)
                        dve.wait_ge(o_rstd, due(o_rstd))
                        link(V.reciprocal(lnr[0:n, 0:1], lnr[0:n, 0:1]))
                        link(V.tensor_scalar(X, X, lnmv[0:n, 0:1], lnr[0:n, 0:1], ALU.subtract, ALU.mult))
                        g = gcol_ * D_MODEL
                        link(tt(X, X, vbuf[0:n, g:g + D_MODEL], ALU.mult))
                        link(tt(x[0:n, t, :], X, vbuf[0:n, g + D_MODEL:g + 2 * D_MODEL], ALU.add), ln_n)

                    dve.wait_ge(ln_par, 64)
                    for t in tiles:
                        n = rows[t]
                        dve.wait_ge(o_ps, t + 1)
                        bank = 2 * (t % 2)
                        link(V.scalar_tensor_tensor(x[0:n, t, :].rearrange("p (a b) -> p a b", a=2), x[0:n, t, :].rearrange("p (a b) -> p a b", a=2), ALPHA,
                                                    ps[0:n, bank:bank + 2, :], ALU.mult, ALU.add), y_free)
                        layer_norm(t, 0, x)

                    dve.wait_ge(r_w, 16 * 7)
                    V.memset(rt[:, :, :], 0.0)
                    link(V.memset(moe_small, 0.0))
                    dve.wait_ge(r_ps, NT)
                    NR = GROUPS + EXPERTS
                    tt(rt[:, 0:NP, :], ps[:, 7, 0:NP * NR].rearrange("p (t c) -> p t c", t=NP), rep(br, NP), ALU.add)
                    link(tt(rt[0:NS, NP, :], ps[0:NS, 7, NP * NR:NT * NR], br[0:NS], ALU.add))

                    def first_max(v, vmax, hot):
                        link(V.tensor_reduce(vmax, v, AX.X, ALU.max))
                        link(tt(hot, v, over(vmax), ALU.is_equal))
                        link(tt(hot, hot, rank, ALU.mult))
                        link(V.tensor_reduce(r_m, hot, AX.X, ALU.max))
                        link(tt(hot, hot, over(r_m), ALU.is_equal))

                    def over(v):
                        return b3(v, 4)

                    rank = rep(T("rank"), NT)
                    g_l = rt[:, :, 0:GROUPS]
                    first_max(g_l, r_gm, r_goh)
                    link(tt(r_gd, g_l, over(r_gm), ALU.subtract), r_lg)
                    e_l = rt[:, :, GROUPS:].rearrange("p t (g e) -> p t g e", g=GROUPS)
                    link(tt(r_t16, e_l, r_goh.unsqueeze(3).to_broadcast([P, NT, GROUPS, 4]), ALU.mult))
                    link(V.tensor_reduce(r_el, r_t16.rearrange("p t g e -> p t e g"), AX.X, ALU.add))
                    first_max(r_el, r_v1, r_oh1)
                    link(V.scalar_tensor_tensor(r_e2l, r_oh1, NEG, r_el, ALU.mult, ALU.add))
                    first_max(r_e2l, r_v2, r_oh2)
                    link(tt(r_vd, r_v2, r_v1, ALU.subtract), r_e2)
                    dve.wait_ge(r_exp, 1)
                    link(V.tensor_reduce(r_gw, r_ge, AX.X, ALU.add))
                    link(V.reciprocal(r_gw, r_gw))
                    dve.wait_ge(r_e2x, 1)
                    link(V.tensor_scalar(r_w1, r_ex, 1.0, None, ALU.add))
                    link(V.reciprocal(r_w1, r_w1))
                    link(tt(r_w1, r_w1, r_gw, ALU.mult))
                    link(tt(r_w2, r_w1, r_ex, ALU.mult))
                    for hot, oh in zip(r_hot, (r_oh1, r_oh2)):
                        m = tt(hot.rearrange("p t (g e) -> p t g e", g=GROUPS), r_goh.unsqueeze(3).to_broadcast([P, NT, GROUPS, 4]),
                               oh.unsqueeze(2).to_broadcast([P, NT, GROUPS, 4]), ALU.mult)
                    link(m)
                    link(tt(r_pick, r_hot[0], r_hot[1], ALU.add), r_picked)
                    dve.wait_ge(r_pos_ps, 1)
                    V.memset(r_pos[:, NP:NT, :], 0.0)
                    V.tensor_copy(r_pos[:, 0:NP, :], ps[:, 1, 0:NP * EXPERTS].rearrange("p (t e) -> p t e", t=NP))
                    link(V.tensor_copy(r_sums, ps[:, 1, 2 * P:2 * P + NT * EXPERTS].rearrange("p (t e) -> p t e", t=NT)))
                    link(V.tensor_copy(r_pos[0:NS, NP, :], ps[0:NS, 1, NP * EXPERTS:NT * EXPERTS]))
                    for t in range(1, NT):
                        tt(r_pos[:, t, :], r_pos[:, t, :], r_sums[:, t - 1, :], ALU.add)
                        link(tt(r_sums[:, t, :], r_sums[:, t, :], r_sums[:, t - 1, :], ALU.add))
                    r_tot = r_sums[:, NP, :]
                    link(V.tensor_scalar(r_nb, r_tot, float(BLOCK), None, ALU.is_gt))
                    for c in range(2, MORE_PER_EXPERT + 1):
                        link(V.scalar_tensor_tensor(r_nb, r_tot, float(c * BLOCK), r_nb, ALU.is_gt, ALU.add))
                    link(V.tensor_tensor_scan(r_cum, T("ones")[:, 0:EXPERTS], r_nb, 0.0, ALU.mult, ALU.add))
                    link(tt(r_more, r_cum, r_nb, ALU.subtract))
                    link(V.scalar_tensor_tensor(r_more, r_more, float(BLOCK), T("more_row"), ALU.mult, ALU.add))
                    link(V.scalar_tensor_tensor(r_row, r_pos, float(BLOCK), rep(r_more, NT), ALU.is_ge, ALU.mult))
                    link(tt(r_row, r_row, r_pos, ALU.add))
                    link(tt(r_row, r_row, rep(T("first_row"), NT), ALU.add))
                    for c in range(TOP_K):
                        link(tt(r_hot[c], r_hot[c], r_row, ALU.mult))
                        link(V.tensor_reduce(r_rowf[:, :, c:c + 1], r_hot[c], AX.X, ALU.add))
                    V.tensor_copy(rows_u[:, :, :], r_rowf).then_inc(planned, 1)
                    V.tensor_copy(r_plan[:, 0:EXPERTS], T("experts"))
                    link(tt(r_owner3, rep(r_cum, MORE), b3(T("count"), EXPERTS), ALU.is_le))
                    link(V.tensor_reduce(r_plan[:, EXPERTS:N_BLOCKS], r_owner3, AX.X, ALU.add))
                    V.tensor_scalar(r_plan[:, EXPERTS:N_BLOCKS], r_plan[:, EXPERTS:N_BLOCKS], float(EXPERTS - 1), None, ALU.min)
                    link(tt(r_even, r_cum[:, EXPERTS - 1:EXPERTS].to_broadcast([P, MORE // 2]), T("count")[:, 0:MORE:2], ALU.is_gt))
                    link(V.tensor_reduce(r_plan[:, N_BLOCKS:], r_even, AX.X, ALU.add))
                    link(V.tensor_scalar(r_plan[:, N_BLOCKS:], r_plan[:, N_BLOCKS:], float(EXPERTS // 2 - 1), None, ALU.add))
                    V.tensor_copy(plan[:, :], r_plan[0:1, :]).then_inc(planned, 1)
                    dve.wait_ge(planned, 2)
                    last_pair = dve.value_load(plan[0:1, N_BLOCKS:N_BLOCKS + 1], min_val=EXPERTS // 2 - 1, max_val=N_BLOCKS // 2 - 1)

                    def dve_block(k, i, s):
                        dve.wait_ge(sil_sb, k + 1)
                        tt(hT[s].rearrange("p a n -> p (a n)"), sil[s], ps[:, 2 + s, 2 * BLOCK:], ALU.mult).then_inc(hT_sb, 1)
                        dve.wait_ge(y_ps, k + 1)
                        dve.wait_ge((y_out0, y_out1)[s], i * 16 + 16)
                        V.tensor_copy(yo[s][:, 0:SLAB], ps[:, 4 + 2 * s, :]).then_inc(y_sb, 1)

                    dve.sem_inc(y_sb, 3)
                    with dve.Fori(0, last_pair + 1) as i:
                        dve_block(i * 2, i, 0)
                        dve_block(i * 2 + 1, i, 1)
                    for t in tiles:
                        n = rows[t]
                        dve.wait_ge(y_init, t + 1)
                        dve.wait_ge(y_back[t], layer * (16 * TOP_K) + 16 * TOP_K)
                        for c, w in enumerate((r_w1, r_w2)):
                            link(V.scalar_tensor_tensor(x[0:n, t, :], yg[0:n, t, c, :], w[0:n, t:t + 1], x[0:n, t, :], ALU.mult, ALU.add))
                        for hf in range(2):
                            m = V.bn_stats(n_stats[0:n, t, 6 * hf:6 * hf + 6], x[0:n, t, hf * 512:hf * 512 + 512])
                        link(m)
                        link(V.bn_aggr(n_mv[0:n, t, :], n_stats[0:n, t, :]))
                        V.tensor_scalar(n_mv[0:n, t, 0:1], n_mv[0:n, t, 0:1], -1.0, None, ALU.mult).then_inc(n_var, 1)

                @block.tensor
                def _(pe):
                    due = Due()
                    mm = nc.tensor.matmul
                    tr = nc.tensor.transpose
                    idn = T("ident")

                    def turn_x(t, base):
                        n = rows[t]
                        for hf in range(2):
                            i = 2 * t + hf
                            if i >= 3:
                                pe.wait_ge(xT_sb, base + i - 2)
                            for k in range(4):
                                c = (4 * hf + k) * P
                                m = tr(ps[:, 4 + i % 3, k * n:(k + 1) * n], x[0:n, t, c:c + P], idn[0:n, 0:n])
                            m.then_inc(xT_ps, 1)

                    for t in tiles:
                        turn_x(t, 0)
                    pe.wait_ge(xT_sb, 2 * NT)
                    w_slab = (w_slab0, w_slab1, w_slab2)
                    def turn_qk(t, q, k, bank, sem):
                        n = rows[t]
                        for a, name in enumerate((q, q, k, k)):
                            c = COLS[name] + a % 2 * P
                            m = tr(ps[:, bank, a * n:(a + 1) * n], zt[0:n, t, c:c + P], idn[0:n, 0:n])
                        m.then_inc(sem, 1)

                    def forget_sums():
                        pe.wait_ge(gate_sb, 1)
                        for t in tiles:
                            n = rows[t]
                            lfd = lambda c: th(lf)[0:n, c, HEADS:]
                            for c in range(t if t < NP else 0):
                                mm(ps[0:n, 7, 2 * P + t * HEADS:2 * P + (t + 1) * HEADS], T("ones"), lfd(c), start=(c == 0), stop=False)
                            m = mm(ps[0:n, 7, 2 * P + t * HEADS:2 * P + (t + 1) * HEADS], T("upper" if t < NP else "upper_s", n), lfd(t), start=(t in (0, NP)), stop=True)
                        m.then_inc(d_cum, 1)
                        turn_qk(NP, "d_q", "d_k", 4, e_T)

                    def later_gates():
                        pe.wait_ge(e_tot, 1)
                        mm(ps[:, 5, 0:DEC_BATCH * HEADS], T("after"), sufp, start=True, stop=True).then_inc(e_cumps, 1)

                    for at, g in enumerate(SLAB_ORDER):
                        if at == 3:
                            pe.wait_ge(ws_n, 16)
                            for h in range(HEADS):
                                m = tr(ps[:, 7, h * P:(h + 1) * P], ws_nat[:, h, :], idn)
                            m.then_inc(ws_ps, 1)
                            pe.wait_ge(ws_s8, 1)
                            for h in range(HEADS):
                                m = tr(ps[0:NS, 6, h * NS:(h + 1) * NS], ws_exp[0:NS, h, :], idn[0:NS, 0:NS])
                            m.then_inc(ws_ps, 1)
                        if at == 5:
                            pe.wait_ge(ws_sb, 2)
                            pe.wait_ge(f_gates, 1)
                            for t in tiles:
                                n = rows[t]
                                m = mm(ps[0:n, 7, t * HEADS:(t + 1) * HEADS], T("upper" if t < NP else "upper_s", n), th(lf)[0:n, t, 0:HEADS], start=True, stop=True)
                            m.then_inc(gate_ps, 1)
                            pe.wait_ge(va_ready, 1)
                            for t in tiles:
                                n = rows[t]
                                for h in range(HEADS):
                                    v = COLS["a_v"] + h * HD
                                    c = t % 2 * GW + h * HD
                                    m = mm(ps[0:n, 4 + t // 2, c:c + HD], (wsT if t < NP else wsTs)[0:n, h, 0:n], zt[0:n, t, v:v + HD], start=True, stop=True)
                            m.then_inc(a_ps, 1)
                        w = min(SLAB, D_IN - g * SLAB)
                        if at == 0:
                            pe.wait_ge(s_slab, layer * 16 + 16)
                        else:
                            pe.wait_ge(w_slab[at % 3], 16 * (at // 3 + (1 if at % 3 else 0)))
                        for t in tiles:
                            i, n = at * NT + t, rows[t]
                            if at == 6 and t == 1:
                                forget_sums()
                            if at == 6 and t == 3:
                                later_gates()
                            if i >= 4:
                                pe.wait_ge(z_sb, i - 3)
                            for k in range(KD):
                                m = mm(ps[0:n, i % 4, 0:w], xTv[:, k, t * P:t * P + n], slab[at % 3][:, k, 0:w], start=(k == 0), stop=(k == KD - 1))
                            m.then_inc(z_ps, 1)
                    pe.wait_ge(z_sb, NT * N_SLABS)

                    def scores(t, sem):
                        n = rows[t]
                        for pair in range(PAIRS):
                            for par in range(2):
                                at = slice(par * HD, (par + 1) * HD)
                                m = mm(ps[0:n, 6 + par, pair * n:(pair + 1) * n], qkT[at, 2 + pair, 0:n], qkT[at, pair, 0:n], start=True, stop=True)
                        m.then_inc(sem, 1)

                    def sample_queries():
                        pe.wait_ge(qm_q, due(qm_q))
                        for h in range(HEADS):
                            m = tr(ps[:, 4, h * NS:(h + 1) * NS], qd2[0:NS, h, :], idn[0:NS, 0:NS])
                        m.then_inc(qm_ps, 1)

                    def mixed(t, state, sstate, w, val, sem):
                        n = rows[t]
                        if t == NP:
                            pe.wait_ge(qm_sb, due(qm_sb))
                            pe.wait_ge(s_in, 16 * 3 * DEC_BATCH)
                        for h in range(HEADS):
                            m = mm(ps[0:n, 4, h * w:(h + 1) * w], sw[0:n, h % 2 * 2 + h // 2, 0:n], val(h), start=True, stop=True)
                        if t < NP:
                            for pair in range(PAIRS):
                                for par in range(2):
                                    at = slice(par * HD, (par + 1) * HD)
                                    m = mm(ps[0:n, 6 + par, pair * w:(pair + 1) * w], qkT[at, pair, 0:n], state[at, pair, :], start=True, stop=True)
                        else:
                            for h in range(HEADS):
                                for bp in range(BP):
                                    m = mm(ps[0:n, 6, h * w:(h + 1) * w], qm[:, bp, h, :], sstate[:, bp, h, :], start=(bp == 0), stop=(bp == BP - 1))
                        m.then_inc(sem, 1)

                    def sample_update(w, val, place):
                        for h in range(HEADS):
                            pe.wait_ge(km_sb, due(km_sb))
                            for bp in range(BP):
                                m = mm(place(bp, h), km[0:NS, 2 * bp:2 * bp + 2, :].rearrange("p a b -> p (a b)"), val(h), start=True, stop=True)
                            m.then_inc(km_used, 1)
                            cache_steps(1)

                    pe.wait_ge(rope_done, 1)
                    pe.wait_ge(gate_sb, 1)
                    pe.wait_ge(e_Tsb, 1 + 2 * PAIRS)
                    pe.wait_ge(e_cumsb, 1)
                    kv = kbuf[:, :].rearrange("p (k c) -> p k c", k=KPP)
                    vv = vbuf[:, :].rearrange("p (k c) -> p k c", k=KPP)

                    def cache_scores(u):
                        r, pair = u // 2, u % 2
                        pe.wait_ge(e_ksb, u + 1)
                        if pair == 0 and r >= 1:
                            pe.wait_ge(e_rsb, r)
                        mm(ps[0:HQ, 1, :], qz[:, pair, r // 4, :], kTs[u % 2], start=(pair == 0), stop=(pair == 1)).then_inc(e_row, 1)

                    def turn_scores(r):
                        pe.wait_ge(e_rsb, r + 1)
                        if r % 4 == 0 and r > 0:
                            pe.wait_ge(e_pm, r // 4)
                        for a in range(4):
                            k = r % 4 * 4 + a
                            m = tr(ps[:, 2, k * HQ:(k + 1) * HQ], srow[r % 2][0:HQ, a * P:(a + 1) * P], idn[0:HQ, 0:HQ])
                        m.then_inc(e_s, 1)

                    def cache_values(j):
                        pe.wait_ge(v_in, layer * (16 * DEC_BATCH) + 16 * (j + 1))
                        pe.wait_ge(e_p, j + 1)
                        for k in range(KPP):
                            mm(ps[0:HQ, 3, 0:GW], pp[j % 2][:, k, :], vv[:, k, :], start=(k == 0), stop=False)
                        c = COLS["d_v"]
                        mm(ps[0:HQ, 3, 0:GW], pp[j % 2][0:NS, KPP, :], zt[0:NS, NP, c:c + GW], start=False, stop=True)
                        pe.wait_ge(e_lf, j + 1)
                        mm(ps[0:HQ, 3, GW:GW + 1], ptot, T("ones")[:, 0:1], start=True, stop=True).then_inc(e_pv, 1)

                    def cache_step(u):
                        i, g = u // 8, u % 8
                        j = i - 1
                        if i < DEC_BATCH:
                            if g % 4 == 0:
                                pe.wait_ge(k_in[g // 4], layer * (16 * DEC_BATCH) + 16 * (i + 1))
                            if u >= 1:
                                pe.wait_ge(e_ksb, u)
                            for a in range(4):
                                m = tr(ps[:, 0, a * P:(a + 1) * P], kv[:, g // 2 * 4 + a, g % 2 * P:(g % 2 + 1) * P], idn)
                            m.then_inc(e_kps, 1)
                            if g > 0:
                                cache_scores(u - 1)
                            if g in (3, 5, 7):
                                turn_scores(4 * i + (g - 3) // 2)
                        if j >= 0 and g == 2:
                            pe.wait_ge(e_pm, j + 1)
                            if j >= 1:
                                pe.wait_ge(e_ym, j)
                            tr(ps[0:HQ, 3, MT:MT + P], pmax, idn).then_inc(e_mt, 1)
                        if j >= 0 and g == 4:
                            pe.wait_ge(e_dg, j + 1)
                            mm(ps[:, 3, BC:BC + HQ], T("ones", HQ), pdiag[0:HQ], start=True, stop=True).then_inc(e_bc, 1)
                        if g == 7:
                            if i < DEC_BATCH:
                                cache_scores(u)
                                if i > 0:
                                    pe.wait_ge(e_xs, i)
                                c = NEW + i % 2 * HQ
                                for pair in range(PAIRS):
                                    m = mm(ps[0:NS, 3, c:c + HQ], kTn[:, pair, :], qz[:, pair, i, :], start=(pair == 0), stop=(pair == 1))
                                m.then_inc(e_psum, 1)
                            if j >= 0:
                                cache_values(j)
                            if i < DEC_BATCH:
                                turn_scores(4 * i + 3)

                    steps = iter(range(CACHE_STEPS))

                    def cache_steps(n):
                        for _ in range(n):
                            cache_step(next(steps))

                    for t in tiles:
                        n = rows[t]
                        if t > 0:
                            pe.wait_ge(b_state, t)
                        turn_qk(t, "b_q", "b_k", 4, b_T)
                        cache_steps(B_STEPS[0])
                        pe.wait_ge(b_Tsb, 2 * t + 2)
                        scores(t, b_sc)
                        if t == NP:
                            sample_queries()
                        val = lambda h: zt[0:n, t, COLS["b_v"] + h * HD:COLS["b_v"] + (h + 1) * HD]
                        cache_steps(B_STEPS[1])
                        pe.wait_ge(b_sw, t + 1)
                        mixed(t, ret, rs, HD, val, b_out)
                        pe.wait_ge(b_kd, t + 1)
                        if t < NP:
                            for pair in range(PAIRS):
                                c = COLS["b_v"] + pair * P
                                m = mm(ps[:, 5, pair * P:(pair + 1) * P], kd[:, pair * P:(pair + 1) * P], zt[:, t, c:c + P], start=True, stop=True)
                            m.then_inc(b_up, 1)
                        else:
                            sample_update(HD, val, lambda bp, h: ps[:, 4 + bp // 2, (bp % 2 * HEADS + h) * HD:(bp % 2 * HEADS + h + 1) * HD])
                        cache_steps(B_STEPS[2])
                    pe.wait_ge(b_state, NT)
                    for t in tiles:
                        n = rows[t]
                        W = HD + 1
                        if t > 0:
                            pe.wait_ge(c_cd, t)
                        turn_qk(t, "c_q", "c_k", 4, c_T)
                        pe.wait_ge(c_dg, t + 1)
                        m = mm(ps[0:n, 5, 0:HEADS * n], T("ones", n)[:, 0:n], diag[0:n, :, 0:n], start=True, stop=True)
                        m.then_inc(c_row, 1)
                        cache_steps(C_STEPS[0])
                        pe.wait_ge(c_Tsb, 2 * t + 2)
                        scores(t, c_sc)
                        if t == NP:
                            sample_queries()
                        cache_steps(C_STEPS[1])
                        pe.wait_ge(c_mt, t + 1)
                        mm(ps[0:n, 5, 0:2 * HEADS], T("last" if t < NP else "last_s", n), mtb[0:n, :], start=True, stop=True).then_inc(c_last, 1)
                        cache_steps(C_STEPS[2])
                        val = lambda h: vx[0:n, h, :]
                        pe.wait_ge(c_sw, t + 1)
                        pe.wait_ge(c_vx, t + 1)
                        mixed(t, mem, cs, W, val, c_out)
                        pe.wait_ge(c_kd, t + 1)
                        if t < NP:
                            for pair in range(PAIRS):
                                m = mm(ps[:, 5, pair * 2 * W:(pair + 1) * 2 * W], kd[:, pair * P:(pair + 1) * P],
                                       vx[:, 2 * pair:2 * pair + 2, :].rearrange("p a b -> p (a b)"), start=True, stop=True)
                            m.then_inc(c_up, 1)
                        else:
                            sample_update(W, val, lambda bp, h: ps[:, 4 + bp, h * W:(h + 1) * W])
                            for bp in range(BP):
                                m = mm(ps[:, 7, CU + bp * HEADS:CU + (bp + 1) * HEADS], T("last_of", NS)[:, bp * P:(bp + 1) * P], ge[0:NS, HEADS:], start=True, stop=True)
                            m.then_inc(c_up, 1)
                        cache_steps(C_STEPS[3] if t < NP else 1)
                    cache_steps(1)
                    pe.wait_ge(c_cd, NT)
                    for t in range(NP):
                        if t >= 2:
                            pe.wait_ge(d_Tsb, 2 * t - 2)
                        turn_qk(t, "d_q", "d_k", 4 + 2 * (t % 2), d_T)
                        if t % 2:
                            cache_steps(1)
                    for h in range(HEADS):
                        pe.wait_ge(d_dg, h + 1)
                        if h >= 2:
                            pe.wait_ge(d_ncr, h - 1)
                        mm(ps[:, 5 + 2 * (h % 2), :], T("ones"), dg[h % 2].rearrange("p a b -> p (a b)"), start=True, stop=True).then_inc(d_row, 1)
                    pe.wait_ge(d_Tsb, 2 * NP)

                    def logits(m_):
                        c, h = m_ // HEADS, m_ % HEADS
                        w = (c + 1) * P
                        at = slice(h % 2 * HD, (h % 2 + 1) * HD)
                        if m_ >= 2:
                            pe.wait_ge(d_lgx, m_ - 1)
                        mm(ps[:, 4 + 2 * (m_ % 2), 0:w], qTa[at, h // 2, c * P:(c + 1) * P], kTa[at, h // 2, 0:w], start=True, stop=False)
                        mm(ps[:, 4 + 2 * (m_ % 2), c * P:w], idn, T("neg_q"), start=False, stop=True).then_inc(d_lg, 1)

                    def values(m_):
                        c, h = m_ // HEADS, m_ % HEADS
                        pe.wait_ge(d_pTsb, m_ + 1)
                        if c >= 1 and h == 0:
                            pe.wait_ge(d_y, c)
                        v = COLS["d_v"] + h * HD
                        for s in range(c + 1):
                            m = mm(ps[:, 7, h * HD:(h + 1) * HD], pT[m_ % 2][:, s, :], zt[:, s, v:v + HD], start=(s == 0), stop=(s == c))
                        m.then_inc(d_o, 1)

                    pe.wait_ge(d_ncr, HEADS)
                    cache_steps(1)
                    for m_ in range(NP * HEADS + 2):
                        if m_ < NP * HEADS:
                            logits(m_)
                        if m_ >= 2:
                            values(m_ - 2)
                        if 1 <= m_ <= NP * HEADS:
                            pe.wait_ge(d_exp, m_)
                            for s in range((m_ - 1) // HEADS + 1):
                                m = tr(ps[:, 5, s * P:(s + 1) * P], lg[(m_ - 1) % 2][:, s * P:(s + 1) * P], idn)
                            m.then_inc(d_pT, 1)
                        if m_ < NP * HEADS:
                            cache_steps(D_STEPS[m_ % 2])
                    for u in steps:
                        cache_step(u)
                    pe.wait_ge(e_ym, DEC_BATCH)
                    for i in range(DEC_BATCH):
                        c = NS - DEC_SEQ - DEC_SEQ * i
                        m = mm(ps[0:NS, 0, 0:GW], T("to_row", HQ)[:, c:c + NS], ym[0:HQ, i], start=(i == 0), stop=(i == DEC_BATCH - 1))
                    m.then_inc(e_fin, 1)
                    for i in range(2 * NT):
                        t, hf = i % NT, i // NT
                        n = rows[t]
                        if t == 0:
                            pe.wait_ge(merged, hf + 1)
                        if i >= 4:
                            pe.wait_ge(m_sb, i - 3)
                        for k in range(4):
                            kk = 4 * hf + k
                            c = COLS[MERGED[kk // 2]] + kk % 2 * P
                            m = tr(ps[:, 4 + i % 4, k * n:(k + 1) * n], zt[0:n, t, c:c + P], idn[0:n, 0:n])
                        m.then_inc(m_ps, 1)
                    pe.wait_ge(m_sb, 2 * NT)
                    pe.wait_ge(wout_in, 32)
                    NR = GROUPS + EXPERTS

                    def router(t):
                        n = rows[t]
                        pe.wait_ge(xT_sb, 2 * (NT + t + 1))
                        for k in range(KD):
                            m = mm(ps[0:n, 7, t * NR:(t + 1) * NR], xTv[:, k, t * P:t * P + n], wr[:, k, :], start=(k == 0), stop=(k == KD - 1))
                        m.then_inc(r_ps, 1)

                    for t in tiles:
                        n = rows[t]
                        bank = 2 * (t % 2)
                        if t >= 2:
                            pe.wait_ge(y_free, t - 1)
                        for hf in range(2):
                            for k in range(KD):
                                m = mm(ps[0:n, bank + hf, :], xTv[:, k, t * P:t * P + n], slab[hf][:, k, :], start=(k == 0), stop=(k == KD - 1))
                        m.then_inc(o_ps, 1)
                        if t == 1:
                            pe.wait_ge(r_w, 16 * 7)
                        if t >= 1:
                            pe.wait_ge(ln_n, t)
                            turn_x(t - 1, 2 * NT)
                        if t >= 2:
                            router(t - 2)
                    router(NP - 1)
                    pe.wait_ge(ln_n, NT)
                    turn_x(NP, 2 * NT)
                    router(NP)

                    pe.wait_ge(r_picked, 1)
                    W = NP * EXPERTS
                    mm(ps[:, 1, 0:W], T("before"), r_pick[:, 0:NP, :].rearrange("p t e -> p (t e)"), start=True, stop=True)
                    mm(ps[0:NS, 1, W:W + EXPERTS], T("before", NS)[:, 0:NS], r_pick[0:NS, NP, :], start=True, stop=True)
                    mm(ps[:, 1, 2 * P:2 * P + W], T("ones"), r_pick[:, 0:NP, :].rearrange("p t e -> p (t e)"), start=True, stop=True)
                    mm(ps[:, 1, 2 * P + W:2 * P + W + EXPERTS], T("ones", NS), r_pick[0:NS, NP, :], start=True, stop=True).then_inc(r_pos_ps, 1)
                    pe.wait_ge(planned, 2)
                    last_pair = pe.value_load(plan[0:1, N_BLOCKS:N_BLOCKS + 1], min_val=EXPERTS // 2 - 1, max_val=N_BLOCKS // 2 - 1)

                    def pe_turn(i, s):
                        pe.wait_ge((xg_in0, xg_in1)[s], i * 16 + 16)
                        for hf in range(2):
                            for k in range(4):
                                m = tr(ps[:, hf, k * P:(k + 1) * P], xg[s][:, 4 * hf + k::KD], idn)
                            m.then_inc(xgT_ps, 1)

                    def pe_h(i, k, s):
                        pe.wait_ge((w13_in0, w13_in1)[s], i * 32 + 32)
                        pe.wait_ge(xgT_sb, k * 2 + 2)
                        for w in range(2):
                            for c in range(2):
                                at = (2 * w + c) * BLOCK
                                for q in range(KD):
                                    m = mm(ps[:, 2 + s, at:at + BLOCK], w13[s][:, w, q, c::2], xgT[s][:, q, :], start=(q == 0), stop=(q == KD - 1))
                        m.then_inc(h_ps, 1)

                    def pe_y(i, k, s):
                        pe.wait_ge((w2_in0, w2_in1)[s], i * 16 + 16)
                        pe.wait_ge(hT_sb, k + 1)
                        pe.wait_ge(y_sb, k * 2 + 1)
                        for hf in range(2):
                            for c in range(2):
                                m = mm(ps[:, 4 + 2 * s + hf, :], hT[s][:, c, :], w2[s][:, c, hf * SLAB:(hf + 1) * SLAB], start=(c == 0), stop=(c == 1))
                        m.then_inc(y_ps, 1)

                    pe.wait_ge(y_free, NT)
                    pe_turn(0, 0)
                    with pe.Fori(0, last_pair) as i:
                        pe_h(i, i * 2, 0)
                        pe_turn(i, 1)
                        pe_y(i, i * 2, 0)
                        pe_h(i, i * 2 + 1, 1)
                        pe_turn(i + 1, 0)
                        pe_y(i, i * 2 + 1, 1)
                    lp = last_pair
                    pe_h(lp, lp * 2, 0)
                    pe_turn(lp, 1)
                    pe_y(lp, lp * 2, 0)
                    pe_h(lp, lp * 2 + 1, 1)
                    pe_y(lp, lp * 2 + 1, 1)

            nc.all_engine_barrier()
            nc.sync.sem_clear(range(signals[0].num, signals[-1].num + 1))
            nc.all_engine_barrier()

        with nc.Block() as block:
            @block.sync
            def _(sp):
                sp.dma_start(d["y_prompt"].rearrange("o (t p) n -> p (o t) n", p=P), x[:, 0:NP, :]).then_inc(s_x0, 16)
                sp.dma_start(d["y_sample"].rearrange("b s n -> (b s) n"), x[0:NS, NP, :]).then_inc(s_x0, 16)
                sp.wait_ge(s_x0, 64)

_INS = ["x_prompt", "x_sample", "cache_k", "cache_v", "cache_logf", "page_table", "state_ret", "state_mlstm_c",
        "state_mlstm_n", "state_mlstm_m", "w_in", "b_in", "w_s", "b_s", "g_mix", "w_out", "ln1_g", "ln1_b",
        "w_rg", "b_rg", "w_re", "b_re", "w1", "w3", "w2", "ln2_g", "ln2_b"]
_KV = (HEADS, HD)
_OUTS = [("y_prompt", (1, SEQ, D_MODEL)), ("y_sample", (DEC_BATCH, DEC_SEQ, D_MODEL)),
         ("k_prompt", (DEPTH, 1, SEQ) + _KV), ("v_prompt", (DEPTH, 1, SEQ) + _KV), ("logf_prompt", (DEPTH, 1, SEQ, HEADS)),
         ("ret_prompt", (DEPTH, 1, HEADS, HD, HD)), ("mlstm_c_prompt", (DEPTH, 1, HEADS, HD, HD)),
         ("mlstm_n_prompt", (DEPTH, 1, HEADS, HD)), ("mlstm_m_prompt", (DEPTH, 1, HEADS)),
         ("k_sample", (DEPTH, DEC_BATCH, DEC_SEQ) + _KV), ("v_sample", (DEPTH, DEC_BATCH, DEC_SEQ) + _KV),
         ("logf_sample", (DEPTH, DEC_BATCH, DEC_SEQ, HEADS)),
         ("ret_sample", (DEPTH, DEC_BATCH, HEADS, HD, HD)), ("mlstm_c_sample", (DEPTH, DEC_BATCH, HEADS, HD, HD)),
         ("mlstm_n_sample", (DEPTH, DEC_BATCH, HEADS, HD)), ("mlstm_m_sample", (DEPTH, DEC_BATCH, HEADS)),
         ("chunk_v_sample", (DEPTH, DEC_BATCH, DEC_SEQ) + _KV)]

def kernel(**inputs):
    import concourse.bacc as _bacc
    from concourse.bass_utils import run_bass_kernel_spmd as _run

    nc = _bacc.Bacc("TRN2", target_bir_lowering=False, num_devices=1)
    arrays, d = {}, {}
    for name in _INS + ["tables"]:
        a = np.ascontiguousarray(TABLES if name == "tables" else inputs[name])
        if name in ("w1", "w3", "w2"):
            a = a.reshape((DEPTH * EXPERTS,) + a.shape[2:])
        arrays["in_" + name] = a
        d[name] = nc.dram_tensor("in_" + name, a.shape, mybir.dt.from_np(a.dtype), kind="ExternalInput").ap()
    for name, shape in _OUTS:
        d[name] = nc.dram_tensor("out_" + name, shape, F32, kind="ExternalOutput").ap()
    decoder(nc, d)
    r = _run(nc, [arrays], core_ids=[0])
    return tuple(r.results[0]["out_" + name] for name, _ in _OUTS)
```
